# Optimizing a Trainium2 kernel written in Bass

```python
import math
import jax, jax.numpy as jnp
from jax import lax
import numpy as np
import jax
import jax.numpy as jnp

D_MODEL = 2048
BATCH = 1
SEQ = 256
DEPTH = 1

MEM_LEN = 256
HEAD_DIM = 64
A_WIDTH = 3 * D_MODEL // 8
A_HEADS = A_WIDTH // HEAD_DIM
A_PATTERNS = ((128, 1), (512, 4), (2048, 16))
B_WIDTH = D_MODEL // 4
B_HEADS = B_WIDTH // HEAD_DIM
BLOCK_Q = 128
C_HEADS = 4
C_VW = 3 * D_MODEL // 8
C_DV = C_VW // C_HEADS
C_DK = C_DV // 2
C_KW = C_HEADS * C_DK
C_GATE_RANK = 16
C_GATE_TAU = 16.0
C_CHUNK = 64
MIX_WIDTH = A_WIDTH + B_WIDTH + C_VW
PROJ_SPLITS = (A_WIDTH, A_WIDTH, A_WIDTH, B_WIDTH, B_WIDTH, B_WIDTH, B_HEADS, C_KW, C_KW, C_VW, C_VW, C_GATE_RANK)
PROJ_WIDTH = sum(PROJ_SPLITS)
CROSS_HEADS = 4
CROSS_DH = 128
CROSS_WIDTH = CROSS_HEADS * CROSS_DH
D_FF = ((8 * D_MODEL // 3 + 127) // 128) * 128
CONV_W = 3
REL_BUCKETS = 32
REL_MAX_DIST = 2048
EPS = 1e-6


def rms_norm(x, g):
    xf = x.astype(jnp.float32)
    y = xf * lax.rsqrt(jnp.mean(xf * xf, axis=-1, keepdims=True) + EPS)
    return (y * g.astype(jnp.float32)).astype(x.dtype)

def t5_bucket(dist):
    max_exact = REL_BUCKETS // 2
    d = np.maximum(dist, 1).astype(np.float32)
    large = max_exact + (np.log(d / max_exact) / math.log(REL_MAX_DIST / max_exact)
                         * (REL_BUCKETS - max_exact)).astype(np.int32)
    return np.where(dist < max_exact, dist, np.minimum(large, REL_BUCKETS - 1)).astype(np.int32)

def dilated_pattern(q, k, v, rel_table, window, dilation):
    B, S, H, Dh = q.shape
    span = window // dilation
    L = S // dilation
    nb = -(-L // span)
    Lp = nb * span

    def classes(t):
        t = t.reshape(B, L, dilation, H, Dh).transpose(0, 3, 2, 1, 4)
        return jnp.pad(t, ((0, 0), (0, 0), (0, 0), (0, Lp - L), (0, 0)))

    def band(t):
        t = jnp.pad(classes(t), ((0, 0), (0, 0), (0, 0), (span, 0), (0, 0)))
        t = t.reshape(B, H, dilation, nb + 1, span, Dh)
        return jnp.concatenate([t[:, :, :, :-1], t[:, :, :, 1:]], axis=4)

    qb = classes(q).reshape(B, H, dilation, nb, span, Dh)
    kb, vb = band(k), band(v)
    i = np.arange(span)[:, None]
    j = np.arange(2 * span)[None, :]
    step = i + span - j
    valid = (step >= 0) & (step <= span) & (np.arange(nb)[:, None, None] * span + j - span >= 0)
    bias = rel_table[t5_bucket(np.clip(step, 0, span) * dilation)]
    bias = jnp.transpose(bias, (2, 0, 1)).astype(jnp.float32)
    logits = jnp.einsum('bhrnid,bhrnjd->bhrnij', qb, kb,
                        preferred_element_type=jnp.float32) * HEAD_DIM ** -0.5
    logits = jnp.where(valid, logits + bias[None, :, None, None], -jnp.inf)
    m = jnp.max(logits, axis=-1, keepdims=True)
    p = jnp.exp(logits - m)
    s = jnp.sum(p, axis=-1, keepdims=True)
    o = jnp.einsum('bhrnij,bhrnjd->bhrnid', p.astype(v.dtype), vb,
                   preferred_element_type=jnp.float32) / s
    lse = (m + jnp.log(s))[..., 0]
    o = o.reshape(B, H, dilation, Lp, Dh)[:, :, :, :L].transpose(0, 3, 2, 1, 4).reshape(B, S, H, Dh)
    lse = lse.reshape(B, H, dilation, Lp)[:, :, :, :L].transpose(0, 3, 2, 1).reshape(B, S, H)
    return o, lse

def dilated_mixture_attention(q, k, v, rel_table):
    outs, lses = [], []
    for window, dilation in A_PATTERNS:
        o, lse = dilated_pattern(q, k, v, rel_table, window, dilation)
        outs.append(o)
        lses.append(lse)
    w = jax.nn.softmax(jnp.stack(lses, axis=0), axis=0)
    return jnp.sum(w[..., None] * jnp.stack(outs, axis=0), axis=0)

def forgetting_attention(q, k, v, f_logit):
    B, S, H, Dh = q.shape
    c = jnp.cumsum(jax.nn.log_sigmoid(f_logit.astype(jnp.float32)), axis=1)
    cT = c.transpose(0, 2, 1)
    nq = S // BLOCK_Q
    qb = q.reshape(B, nq, BLOCK_Q, H, Dh).transpose(1, 0, 2, 3, 4)
    cb = cT.reshape(B, H, nq, BLOCK_Q).transpose(2, 0, 1, 3)
    kpos = jnp.arange(S)

    def block(args):
        n, qn, cn = args
        logits = jnp.einsum('bihd,bjhd->bhij', qn, k,
                            preferred_element_type=jnp.float32) * HEAD_DIM ** -0.5
        logits = logits + (cn[..., :, None] - cT[..., None, :])
        qpos = n * BLOCK_Q + jnp.arange(BLOCK_Q)
        logits = jnp.where(kpos[None, :] <= qpos[:, None], logits, -jnp.inf)
        p = jax.nn.softmax(logits, axis=-1)
        return jnp.einsum('bhij,bjhd->bihd', p.astype(v.dtype), v)

    ob = lax.map(block, (jnp.arange(nq), qb, cb))
    return ob.transpose(1, 0, 2, 3, 4).reshape(B, S, H, Dh)

def gla_chunked(q, k, v, log_alpha):
    B, S, H, DK = q.shape
    nc = S // C_CHUNK

    def chunks(t):
        return t.astype(jnp.float32).reshape(B, nc, C_CHUNK, H, t.shape[-1]).transpose(1, 0, 3, 2, 4)

    qc, kc, vc, gc = chunks(q * DK ** -0.5), chunks(k), chunks(v), chunks(log_alpha)
    causal = np.tril(np.ones((C_CHUNK, C_CHUNK), dtype=bool))[:, :, None]

    def step(state, inp):
        qn, kn, vn, gn = inp
        b = jnp.cumsum(gn, axis=2)
        o_inter = jnp.einsum('bhik,bhkv->bhiv', qn * jnp.exp(b), state)
        diff = b[:, :, :, None, :] - b[:, :, None, :, :]
        decay = jnp.exp(jnp.where(causal, diff, -jnp.inf))
        a = jnp.einsum('bhik,bhjk,bhijk->bhij', qn, kn, decay)
        o_intra = jnp.einsum('bhij,bhjv->bhiv', a, vn)
        b_last = b[:, :, -1:, :]
        state = state * jnp.exp(b_last[:, :, 0, :])[..., None] + \
            jnp.einsum('bhjk,bhjv->bhkv', kn * jnp.exp(b_last - b), vn)
        return state, o_inter + o_intra

    state0 = jnp.zeros((B, H, DK, v.shape[-1]), jnp.float32)
    _, o = lax.scan(step, state0, (qc, kc, vc, gc))
    return o.transpose(1, 0, 3, 2, 4).reshape(B, S, H, v.shape[-1])

def hybrid_mixer(h, w_in, f_bias, rel_table, c_gate_w2, c_gate_b, c_norm, w_out):
    B, S, _ = h.shape
    proj = h @ w_in
    qa, ka, va, qb, kb, vb, fl, qc, kc, vc, rc, gl = jnp.split(
        proj, np.cumsum(PROJ_SPLITS)[:-1].tolist(), axis=-1)

    def heads(t, n):
        return t.reshape(B, S, n, -1)

    o_a = dilated_mixture_attention(heads(qa, A_HEADS), heads(ka, A_HEADS), heads(va, A_HEADS), rel_table)
    o_b = forgetting_attention(heads(qb, B_HEADS), heads(kb, B_HEADS), heads(vb, B_HEADS), fl + f_bias)
    log_alpha = jax.nn.log_sigmoid((gl @ c_gate_w2 + c_gate_b).astype(jnp.float32)) / C_GATE_TAU
    o_c = gla_chunked(heads(qc, C_HEADS), heads(kc, C_HEADS), heads(vc, C_HEADS), heads(log_alpha, C_HEADS))
    o_c = rms_norm(o_c.astype(h.dtype), c_norm).reshape(B, S, C_VW) * jax.nn.silu(rc)
    mixed = jnp.concatenate([o_a.reshape(B, S, A_WIDTH).astype(h.dtype),
                             o_b.reshape(B, S, B_WIDTH).astype(h.dtype),
                             o_c.astype(h.dtype)], axis=-1)
    return mixed @ w_out

def memory_cross_attention(h, mem_n, w_q, w_kv, w_o):
    B, S, _ = h.shape
    M = mem_n.shape[1]
    q = (h @ w_q).reshape(B, S, CROSS_HEADS, CROSS_DH)
    k, v = jnp.split(mem_n @ w_kv, 2, axis=-1)
    k = k.reshape(B, M, CROSS_HEADS, CROSS_DH)
    v = v.reshape(B, M, CROSS_HEADS, CROSS_DH)
    logits = jnp.einsum('bshd,bmhd->bhsm', q, k, preferred_element_type=jnp.float32) * CROSS_DH ** -0.5
    p = jax.nn.softmax(logits, axis=-1)
    o = jnp.einsum('bhsm,bmhd->bshd', p.astype(v.dtype), v).reshape(B, S, CROSS_WIDTH)
    return o @ w_o

def conv_ffn(h, w_up, conv_w, conv_b, w_down):
    S = h.shape[1]
    val, gate = jnp.split(h @ w_up, 2, axis=-1)
    gp = jnp.pad(gate, ((0, 0), (CONV_W - 1, 0), (0, 0)))
    g = conv_b
    for i in range(CONV_W):
        g = g + conv_w[i] * gp[:, i:i + S]
    return (jax.nn.silu(g) * val) @ w_down

def first_inputs(seed: int = 0) -> dict:
    key = jax.random.key(seed)
    ks = jax.random.split(key, 21)

    def nrm(k, shape, scale):
        return jax.random.normal(k, shape, jnp.float32) * scale

    def gain(k, shape):
        return 1.0 + 0.05 * jax.random.normal(k, shape, jnp.float32)

    return {
        'x': nrm(ks[0], (BATCH, SEQ, D_MODEL), 1.0),
        'mem': nrm(ks[1], (BATCH, MEM_LEN, D_MODEL), 1.0),
        'rel_table': nrm(ks[2], (REL_BUCKETS, A_HEADS), 0.5),
        'mem_norm': gain(ks[3], (D_MODEL,)),
        'norm_final': gain(ks[4], (D_MODEL,)),
        'norm_mix': gain(ks[5], (DEPTH, D_MODEL)),
        'w_in': nrm(ks[6], (DEPTH, D_MODEL, PROJ_WIDTH), D_MODEL ** -0.5),
        'f_bias': 3.0 + nrm(ks[7], (DEPTH, B_HEADS), 0.1),
        'c_gate_w2': nrm(ks[8], (DEPTH, C_GATE_RANK, C_KW), C_GATE_RANK ** -0.5),
        'c_gate_b': nrm(ks[9], (DEPTH, C_KW), 0.1),
        'c_norm': gain(ks[10], (DEPTH, C_DV)),
        'w_out': nrm(ks[11], (DEPTH, MIX_WIDTH, D_MODEL), MIX_WIDTH ** -0.5),
        'norm_cross': gain(ks[12], (DEPTH, D_MODEL)),
        'w_cq': nrm(ks[13], (DEPTH, D_MODEL, CROSS_WIDTH), D_MODEL ** -0.5),
        'w_ckv': nrm(ks[14], (DEPTH, D_MODEL, 2 * CROSS_WIDTH), D_MODEL ** -0.5),
        'w_co': nrm(ks[15], (DEPTH, CROSS_WIDTH, D_MODEL), CROSS_WIDTH ** -0.5),
        'norm_ffn': gain(ks[16], (DEPTH, D_MODEL)),
        'w_up': nrm(ks[17], (DEPTH, D_MODEL, 2 * D_FF), D_MODEL ** -0.5),
        'conv_w': nrm(ks[18], (DEPTH, CONV_W, D_FF), CONV_W ** -0.5),
        'conv_b': nrm(ks[19], (DEPTH, D_FF), 0.02),
        'w_down': nrm(ks[20], (DEPTH, D_FF, D_MODEL), D_FF ** -0.5),
    }

def first_block(x, mem, rel_table, mem_norm, norm_final, norm_mix, w_in, f_bias, c_gate_w2,
              c_gate_b, c_norm, w_out, norm_cross, w_cq, w_ckv, w_co, norm_ffn, w_up,
              conv_w, conv_b, w_down):
    mem_n = rms_norm(mem, mem_norm)
    for l in range(DEPTH):
        x = x + hybrid_mixer(rms_norm(x, norm_mix[l]), w_in[l], f_bias[l], rel_table,
                             c_gate_w2[l], c_gate_b[l], c_norm[l], w_out[l])
        x = x + memory_cross_attention(rms_norm(x, norm_cross[l]), mem_n, w_cq[l], w_ckv[l], w_co[l])
        x = x + conv_ffn(rms_norm(x, norm_ffn[l]), w_up[l], conv_w[l], conv_b[l], w_down[l])
    return rms_norm(x, norm_final)


NSA_HEADS = 8
NSA_KV_GROUPS = 2
NSA_HPG = NSA_HEADS // NSA_KV_GROUPS
NSA_HEAD_DIM = 128
NSA_WIDTH = NSA_HEADS * NSA_HEAD_DIM
NSA_KV_WIDTH = NSA_KV_GROUPS * NSA_HEAD_DIM
CMP_BLOCK = 32
CMP_STRIDE = 16
CMP_HIDDEN = 256
SEL_BLOCK = 64
SEL_TOP_N = 16
SEL_FORCE = 1000.0
WINDOW = 512
NSA_QBLOCK = 32

GDN_HEADS = 8
GDN_HEAD_DIM = 128
GDN_WIDTH = GDN_HEADS * GDN_HEAD_DIM
CONV_WIDTH = 4
GDN_CHUNK = 64

REL_MAX_DIST_2 = 128

D_FF_2 = 4 * D_MODEL
NORM_EPS = 1e-6

IN_SPLIT_SIZES = (NSA_WIDTH, 6 * NSA_KV_WIDTH, 3 * NSA_HEADS, 3 * GDN_WIDTH, GDN_WIDTH, GDN_HEADS, GDN_HEADS, 2 * D_MODEL)
IN_COLS = NSA_WIDTH + 6 * NSA_KV_WIDTH + 3 * NSA_HEADS + 3 * GDN_WIDTH + GDN_WIDTH + GDN_HEADS + GDN_HEADS + 2 * D_MODEL


def rms_norm_2(x, w):
    xf = x.astype(jnp.float32)
    y = xf * lax.rsqrt(jnp.mean(xf * xf, axis=-1, keepdims=True) + NORM_EPS)
    return (y * w.astype(jnp.float32)).astype(x.dtype)

def masked_softmax(s, valid):
    s = jnp.where(valid, s.astype(jnp.float32), -jnp.inf)
    m = jnp.max(s, axis=-1, keepdims=True)
    m = jnp.where(jnp.isfinite(m), m, 0.0)
    e = jnp.exp(s - m)
    return e / jnp.maximum(jnp.sum(e, axis=-1, keepdims=True), 1e-30)

def t5_bucket_2(dist):
    n = jnp.maximum(dist, 0)
    exact = REL_BUCKETS // 2
    nf = jnp.maximum(n, 1).astype(jnp.float32)
    large = exact + (jnp.log(nf / exact) / math.log(REL_MAX_DIST_2 / exact) * (REL_BUCKETS - exact)).astype(jnp.int32)
    large = jnp.minimum(large, REL_BUCKETS - 1)
    return jnp.where(n < exact, n, large)

def rel_bias_grid(rel_table, dist):
    tq, tk = dist.shape
    b = rel_table[t5_bucket_2(dist)]
    return b.reshape(tq, tk, NSA_KV_GROUPS, NSA_HPG).transpose(2, 3, 0, 1)

def compress_tokens(kv, pe, w1, w2):
    b, s, g, dh = kv.shape
    n_sub = CMP_BLOCK // CMP_STRIDE
    n_cmp = s // CMP_STRIDE - n_sub + 1
    r = kv.reshape(b, s // CMP_STRIDE, CMP_STRIDE, g, dh)
    blocks = jnp.concatenate([r[:, j:j + n_cmp] for j in range(n_sub)], axis=2)
    blocks = blocks + pe[None, None, :, None, :]
    flat = blocks.transpose(0, 1, 3, 2, 4).reshape(b, n_cmp, g, CMP_BLOCK * dh)
    return jax.nn.gelu(flat @ w1) @ w2

def nsa_attention(q, kv, gate_logits, rel_table, pe_k, pe_v, w1_k, w2_k, w1_v, w2_v):
    b, s, _ = q.shape
    g_, j_, dh = NSA_KV_GROUPS, NSA_HPG, NSA_HEAD_DIM
    scale = dh ** -0.5
    q = q.reshape(b, s, g_, j_, dh)
    k_c, v_c, k_s, v_s, k_w, v_w = [t.reshape(b, s, g_, dh) for t in jnp.split(kv, 6, axis=-1)]
    kc = compress_tokens(k_c, pe_k, w1_k, w2_k)
    vc = compress_tokens(v_c, pe_v, w1_v, w2_v)
    n_cmp = kc.shape[1]
    n_sel = s // SEL_BLOCK
    top_n = min(SEL_TOP_N, n_sel)
    ks = k_s.reshape(b, n_sel, SEL_BLOCK, g_, dh).transpose(0, 3, 1, 2, 4)
    vs = v_s.reshape(b, n_sel, SEL_BLOCK, g_, dh).transpose(0, 3, 1, 2, 4)
    pad = ((0, 0), (WINDOW, 0), (0, 0), (0, 0))
    kw = jnp.pad(k_w, pad)
    vw = jnp.pad(v_w, pad)
    gates = jax.nn.sigmoid(gate_logits).reshape(b, s, g_, j_, 3)

    cmp_end = jnp.arange(n_cmp) * CMP_STRIDE + (CMP_BLOCK - 1)
    c_start = np.arange(n_cmp) * CMP_STRIDE
    s_start = np.arange(n_sel) * SEL_BLOCK
    cover = jnp.asarray(((c_start[:, None] <= s_start[None, :] + SEL_BLOCK - 1)
                         & (c_start[:, None] + CMP_BLOCK - 1 >= s_start[None, :])).astype(np.float32))
    sel_ids = jnp.arange(n_sel)
    rel_flat = rel_table.reshape(REL_BUCKETS, g_, j_).transpose(1, 0, 2).reshape(g_ * REL_BUCKETS, j_)
    group_off = jnp.arange(g_)[None, :, None, None, None] * REL_BUCKETS
    gather_blocks = jax.vmap(jax.vmap(lambda blk, ix: blk[ix]))

    def query_block(i):
        q0 = i * NSA_QBLOCK
        t = q0 + jnp.arange(NSA_QBLOCK)
        qb = lax.dynamic_slice_in_dim(q, q0, NSA_QBLOCK, axis=1)
        gb = lax.dynamic_slice_in_dim(gates, q0, NSA_QBLOCK, axis=1)

        dist_c = t[:, None] - cmp_end[None, :]
        s_c = jnp.einsum('btgjd,bngd->bgjtn', qb, kc) * scale + rel_bias_grid(rel_table, dist_c)
        p_c = masked_softmax(s_c, dist_c >= 0)
        o_c = jnp.einsum('bgjtn,bngd->btgjd', p_c.astype(vc.dtype), vc)

        imp = jnp.einsum('bgjtn,nm->btgm', p_c, cover)
        cur = t // SEL_BLOCK
        forced = (sel_ids[None, :] == 0) | (sel_ids[None, :] == cur[:, None]) | (sel_ids[None, :] == cur[:, None] - 1)
        causal_blk = sel_ids[None, :] <= cur[:, None]
        score = jnp.where(causal_blk[:, None, :], imp + jnp.where(forced, SEL_FORCE, 0.0)[:, None, :], -jnp.inf)
        top_val, top_idx = lax.top_k(score, top_n)
        top_idx = top_idx.transpose(0, 2, 1, 3)
        k_sel = gather_blocks(ks, top_idx)
        v_sel = gather_blocks(vs, top_idx)
        key_pos = top_idx[..., None] * SEL_BLOCK + jnp.arange(SEL_BLOCK)
        dist_s = t[None, None, :, None, None] - key_pos
        valid_s = jnp.isfinite(top_val).transpose(0, 2, 1, 3)[..., None] & (dist_s >= 0)
        bias_s = rel_flat[group_off + t5_bucket_2(dist_s)]
        s_s = jnp.einsum('btgjd,bgtnrd->bgjtnr', qb, k_sel) * scale + jnp.moveaxis(bias_s, -1, 2)
        n_keys = top_n * SEL_BLOCK
        p_s = masked_softmax(s_s.reshape(b, g_, j_, NSA_QBLOCK, n_keys),
                             valid_s.reshape(b, g_, 1, NSA_QBLOCK, n_keys))
        o_s = jnp.einsum('bgjtnr,bgtnrd->btgjd', p_s.reshape(s_s.shape).astype(v_sel.dtype), v_sel)

        kwb = lax.dynamic_slice_in_dim(kw, q0, WINDOW + NSA_QBLOCK, axis=1)
        vwb = lax.dynamic_slice_in_dim(vw, q0, WINDOW + NSA_QBLOCK, axis=1)
        kpos = q0 - WINDOW + jnp.arange(WINDOW + NSA_QBLOCK)
        dist_w = t[:, None] - kpos[None, :]
        valid_w = (dist_w >= 0) & (dist_w < WINDOW) & (kpos[None, :] >= 0)
        s_w = jnp.einsum('btgjd,bsgd->bgjts', qb, kwb) * scale + rel_bias_grid(rel_table, dist_w)
        p_w = masked_softmax(s_w, valid_w)
        o_w = jnp.einsum('bgjts,bsgd->btgjd', p_w.astype(vwb.dtype), vwb)

        return gb[..., 0:1] * o_c + gb[..., 1:2] * o_s + gb[..., 2:3] * o_w

    out = lax.map(query_block, jnp.arange(s // NSA_QBLOCK))
    return out.transpose(1, 0, 2, 3, 4, 5).reshape(b, s, NSA_WIDTH)

def causal_depthwise_conv(x, w):
    return lax.conv_general_dilated(x, w[:, None, :], window_strides=(1,), padding=[(CONV_WIDTH - 1, 0)],
                                    dimension_numbers=('NWC', 'WIO', 'NWC'), feature_group_count=x.shape[-1])

def l2_normalize(x):
    return x * lax.rsqrt(jnp.sum(x * x, axis=-1, keepdims=True) + NORM_EPS)

def gated_delta_rule(q, k, v, g, beta):
    b, s, h, dk = q.shape
    dv = v.shape[-1]
    c = GDN_CHUNK
    n = s // c
    q = l2_normalize(q) * dk ** -0.5
    k = l2_normalize(k)

    def chunks(t):
        return jnp.moveaxis(t.reshape(b, n, c, h, *t.shape[3:]), 3, 1)

    q, k, v, g, beta = (chunks(t) for t in (q, k, v, g, beta))
    g = jnp.cumsum(g, axis=-1)
    kb = k * beta[..., None]
    vb = v * beta[..., None]
    tri = jnp.tril(jnp.ones((c, c), dtype=bool))
    strict = jnp.tril(jnp.ones((c, c), dtype=bool), -1)
    diff = g[..., :, None] - g[..., None, :]
    decay = jnp.where(tri, jnp.exp(jnp.where(tri, diff, 0.0)), 0.0)
    lower = jnp.where(strict, jnp.einsum('bhncd,bhnsd->bhncs', kb, k) * decay, 0.0)
    eye = jnp.eye(c, dtype=q.dtype)
    tinv = lax.linalg.triangular_solve(eye + lower, jnp.broadcast_to(eye, lower.shape),
                                       left_side=True, lower=True, unit_diagonal=True)
    u = tinv @ vb
    w = tinv @ (kb * jnp.exp(g)[..., None])
    qk = jnp.einsum('bhncd,bhnsd->bhncs', q, k) * decay

    def step(state, inp):
        qn, kn, un, wn, gn, qkn = inp
        v_new = un - wn @ state
        o = (qn * jnp.exp(gn)[..., None]) @ state + qkn @ v_new
        g_last = gn[..., -1:]
        state = state * jnp.exp(g_last)[..., None] + jnp.einsum('bhck,bhcv->bhkv', kn * jnp.exp(g_last - gn)[..., None], v_new)
        return state, o

    xs = tuple(jnp.moveaxis(t, 2, 0) for t in (q, k, u, w, g, qk))
    state0 = jnp.zeros((b, h, dk, dv), q.dtype)
    _, o = lax.scan(step, state0, xs)
    return o.transpose(1, 0, 3, 2, 4).reshape(b, s, h, dv)

def gated_deltanet(qkv, z, a, bl, conv_w, a_log, dt_bias, norm_w):
    b, s, _ = qkv.shape
    dtype = qkv.dtype
    qkv = jax.nn.silu(causal_depthwise_conv(qkv, conv_w)).astype(jnp.float32)
    q, k, v = jnp.split(qkv, 3, axis=-1)
    shape = (b, s, GDN_HEADS, GDN_HEAD_DIM)
    beta = jax.nn.sigmoid(bl.astype(jnp.float32))
    g = -jnp.exp(a_log.astype(jnp.float32)) * jax.nn.softplus(a.astype(jnp.float32) + dt_bias.astype(jnp.float32))
    o = gated_delta_rule(q.reshape(shape), k.reshape(shape), v.reshape(shape), g, beta)
    o = o * lax.rsqrt(jnp.mean(o * o, axis=-1, keepdims=True) + NORM_EPS) * norm_w.astype(jnp.float32)
    o = o * jax.nn.silu(z.astype(jnp.float32)).reshape(shape)
    return o.reshape(b, s, GDN_WIDTH).astype(dtype)

def hybrid_layer(x, rel_table, ln1_w, w_in, pe_k, pe_v, w1_k, w2_k, w1_v, w2_v, conv_w, a_log, dt_bias,
                 gdn_norm_w, w_pa, w_pb, w_o, ln2_w, w_up, w_down):
    h = rms_norm_2(x, ln1_w)
    proj = h @ w_in
    offs = [int(o) for o in np.cumsum(IN_SPLIT_SIZES)[:-1]]
    nsa_q, nsa_kv, nsa_gate, gdn_qkv, gdn_z, gdn_a, gdn_b, merge = jnp.split(proj, offs, axis=-1)
    o_a = nsa_attention(nsa_q, nsa_kv, nsa_gate, rel_table, pe_k, pe_v, w1_k, w2_k, w1_v, w2_v)
    o_b = gated_deltanet(gdn_qkv, gdn_z, gdn_a, gdn_b, conv_w, a_log, dt_bias, gdn_norm_w)
    g_a, g_b = jnp.split(jax.nn.sigmoid(merge), 2, axis=-1)
    x = x + (g_a * (o_a @ w_pa) + g_b * (o_b @ w_pb)) @ w_o
    h = rms_norm_2(x, ln2_w)
    return x + jnp.square(jax.nn.relu(h @ w_up)) @ w_down

def second_inputs(seed: int = 0) -> dict:
    key = jax.random.key(seed)
    k = jax.random.split(key, 21)
    f32 = jnp.float32
    L = DEPTH

    def normal(kk, shape, scale):
        return jax.random.normal(kk, shape, f32) * scale

    cmp_in = CMP_BLOCK * NSA_HEAD_DIM
    dt = jnp.exp(jax.random.uniform(k[12], (L, GDN_HEADS), f32, math.log(1e-3), math.log(1e-1)))
    return {
        'x': normal(k[0], (BATCH, SEQ, D_MODEL), 1.0),
        'rel_table': normal(k[1], (REL_BUCKETS, NSA_HEADS), 0.5),
        'ln1_w': 1.0 + normal(k[2], (L, D_MODEL), 0.02),
        'w_in': normal(k[3], (L, D_MODEL, IN_COLS), D_MODEL ** -0.5),
        'cmp_pe_k': normal(k[4], (L, CMP_BLOCK, NSA_HEAD_DIM), 0.1),
        'cmp_pe_v': normal(k[5], (L, CMP_BLOCK, NSA_HEAD_DIM), 0.1),
        'cmp_w1_k': normal(k[6], (L, cmp_in, CMP_HIDDEN), cmp_in ** -0.5),
        'cmp_w2_k': normal(k[7], (L, CMP_HIDDEN, NSA_HEAD_DIM), CMP_HIDDEN ** -0.5),
        'cmp_w1_v': normal(k[8], (L, cmp_in, CMP_HIDDEN), cmp_in ** -0.5),
        'cmp_w2_v': normal(k[9], (L, CMP_HIDDEN, NSA_HEAD_DIM), CMP_HIDDEN ** -0.5),
        'conv_w': normal(k[10], (L, CONV_WIDTH, 3 * GDN_WIDTH), CONV_WIDTH ** -0.5),
        'a_log': jnp.log(jax.random.uniform(k[11], (L, GDN_HEADS), f32, 1.0, 16.0)),
        'dt_bias': dt + jnp.log(-jnp.expm1(-dt)),
        'gdn_norm_w': 1.0 + normal(k[13], (L, GDN_HEAD_DIM), 0.02),
        'w_pa': normal(k[14], (L, NSA_WIDTH, D_MODEL), NSA_WIDTH ** -0.5),
        'w_pb': normal(k[15], (L, GDN_WIDTH, D_MODEL), GDN_WIDTH ** -0.5),
        'w_o': normal(k[16], (L, D_MODEL, D_MODEL), D_MODEL ** -0.5),
        'ln2_w': 1.0 + normal(k[17], (L, D_MODEL), 0.02),
        'w_up': normal(k[18], (L, D_MODEL, D_FF_2), D_MODEL ** -0.5),
        'w_down': normal(k[19], (L, D_FF_2, D_MODEL), D_FF_2 ** -0.5),
        'ln_f_w': 1.0 + normal(k[20], (D_MODEL,), 0.02),
    }

def second_block(x, rel_table, ln1_w, w_in, cmp_pe_k, cmp_pe_v, cmp_w1_k, cmp_w2_k, cmp_w1_v, cmp_w2_v, conv_w,
              a_log, dt_bias, gdn_norm_w, w_pa, w_pb, w_o, ln2_w, w_up, w_down, ln_f_w):
    for l in range(DEPTH):
        x = hybrid_layer(x, rel_table, ln1_w[l], w_in[l], cmp_pe_k[l], cmp_pe_v[l], cmp_w1_k[l], cmp_w2_k[l],
                         cmp_w1_v[l], cmp_w2_v[l], conv_w[l], a_log[l], dt_bias[l], gdn_norm_w[l],
                         w_pa[l], w_pb[l], w_o[l], ln2_w[l], w_up[l], w_down[l])
    return rms_norm_2(x, ln_f_w)


def setup_inputs(seed=0):
    out = dict(first_inputs(seed))
    for name, value in second_inputs(seed + 1).items():
        if name != "x":
            out[name + "_2"] = value
    return out


def reference(
    x, mem, rel_table, mem_norm, norm_final, norm_mix, w_in, f_bias, c_gate_w2, c_gate_b,
    c_norm, w_out, norm_cross, w_cq, w_ckv, w_co, norm_ffn, w_up, conv_w, conv_b, w_down,
    rel_table_2, ln1_w_2, w_in_2, cmp_pe_k_2, cmp_pe_v_2, cmp_w1_k_2, cmp_w2_k_2, cmp_w1_v_2,
    cmp_w2_v_2, conv_w_2, a_log_2, dt_bias_2, gdn_norm_w_2, w_pa_2, w_pb_2, w_o_2, ln2_w_2,
    w_up_2, w_down_2, ln_f_w_2,
):
    x = first_block(
        x, mem, rel_table, mem_norm, norm_final, norm_mix, w_in, f_bias, c_gate_w2, c_gate_b,
        c_norm, w_out, norm_cross, w_cq, w_ckv, w_co, norm_ffn, w_up, conv_w, conv_b, w_down,
    )
    return second_block(
        x, rel_table_2, ln1_w_2, w_in_2, cmp_pe_k_2, cmp_pe_v_2, cmp_w1_k_2, cmp_w2_k_2,
        cmp_w1_v_2, cmp_w2_v_2, conv_w_2, a_log_2, dt_bias_2, gdn_norm_w_2, w_pa_2, w_pb_2,
        w_o_2, ln2_w_2, w_up_2, w_down_2, ln_f_w_2,
    )


_drawn_inputs = setup_inputs


def setup_inputs(seed=0):
    import zlib

    import numpy as np

    out = dict(_drawn_inputs(seed))
    spreads = {}
    factors = {'mem_norm': 6.445,
     'f_bias': 46.784,
     'c_gate_b': 3.023,
     'norm_cross': 8.0,
     'conv_b': 5.035,
     'ln1_w_2': 4.812,
     'cmp_pe_k_2': 116.183,
     'cmp_pe_v_2': 97.764,
     'gdn_norm_w_2': 22.223,
     'ln2_w_2': 13.176,
     'ln_f_w_2': 21.877,
     'norm_ffn': 3.702,
     'rel_table_2': 10.739,
     'cmp_w1_k_2': 2.686}
    for name, (base, spread) in spreads.items():
        noise = np.random.default_rng([zlib.crc32(name.encode()), seed]).standard_normal(out[name].shape)
        drawn = base * np.exp(spread * noise) if base else spread * noise
        out[name] = jnp.asarray(drawn.astype(out[name].dtype))
    for name, factor in factors.items():
        out[name] = (out[name] * factor).astype(out[name].dtype)
    return out
```

```python
import numpy as np
from contextlib import ExitStack

import concourse.bass as bass
from concourse import mybir

F32 = mybir.dt.float32
F32R = mybir.dt.float32r
ACT = mybir.ActivationFunctionType
ALU = mybir.AluOpType
AX = mybir.AxisListType

P = 128
S = 256
TT = S // P
D = 2048
KD = D // P
EPS = 1e-6
NEG = -1e30
FLOOR = 1e20
CH = 512
ITEM = 2048
RAW = 4
SPL = 2

A_W, A_H, A_D = 768, 12, 64
B_W, B_H = 512, 8
C_H, C_DK, C_DV = 4, 96, 192
C_KW, C_VW, C_R = 384, 768, 16
X_H, X_D = 4, 128
FF1 = 5504
KF1 = FF1 // P
P1_QA, P1_KA, P1_QB, P1_KB = 0, 768, 1536, 2048
P1_VA, P1_VB, P1_QC, P1_KC, P1_VC, P1_RC = 2560, 3328, 3840, 4224, 4608, 5376
P1_N = 6144
N_H, N_G, N_D = 8, 2, 128
N_CMP, CB, CSTR, CHID = 15, 32, 16, 256
G_H, G_D = 8, 128
FF2 = 8192
P2_Q, P2_KC, P2_VC, P2_KS, P2_KW, P2_VS, P2_VW = 0, 1024, 1280, 1536, 1792, 2048, 2304
P2_N = 2560
REL = 32
TOE = 384

CAUSAL = [(0, [0]), (1, [0, 1])]
FULL = [(0, [0, 1]), (1, [0, 1])]


def split_counts(total, items):
    return [total // items + (i < total % items) for i in range(items)]


def gemm_specs():
    four = [4] * 4
    return [
        ("ckv", 2, four, CH), ("win", 12, four, CH), ("wout", 4, four, CH), ("cq", 1, four, CH),
        ("co", 4, [4], CH),
        ("up_a", 11, four, CH), ("down_a", 4, split_counts(22, 8), CH),
        ("up_b", 10, four, CH), ("up_t", 1, four, CH // 2), ("down_b", 4, split_counts(21, 8), CH),
        ("win2", 5, four, CH), ("cmp_k", 1, split_counts(32, 8), CHID), ("cmp_v", 1, split_counts(32, 8), CHID),
        ("win2g", 6, four, CH), ("z", 2, four, CH),
        ("merge", 8, four, CH), ("pa", 4, [4] * 2, CH), ("pb", 4, [4] * 2, CH), ("wo", 4, four, CH),
        ("up2_a", 8, four, CH), ("down2_a", 4, [4] * 8, CH), ("up2_b", 8, four, CH), ("down2_b", 4, [4] * 8, CH),
    ]


def build(nc, t_in, out):
    ctx = ExitStack()
    with ctx:
        def sb(name, shape, dt=F32, c=ctx):
            return c.enter_context(nc.sbuf_tensor(name, shape, dt))

        def sem(name):
            return ctx.enter_context(nc.semaphore(name))

        pe_, act_, dve_ = nc.tensor, nc.scalar, nc.vector

        w_raw = sb("w_raw", [P, RAW, ITEM])
        w_hi = sb("w_hi", [P, SPL, ITEM], F32R)
        w_lo = sb("w_lo", [P, SPL, ITEM], F32R)
        x = sb("x", [P, TT, D])
        h_hi = sb("h_hi", [P, KD, S], F32R)
        h_lo = sb("h_lo", [P, KD, S], F32R)
        ident = sb("ident", [P, P])
        tri = sb("tri", [P, TT, S])
        gains = sb("gains", [P, 6, KD])
        st = sb("st", [P, 128])
        ones = sb("ones", [P, P])
        eps_c = sb("eps_c", [P, 1])
        acc = [ctx.enter_context(nc.psum_tensor(f"acc{i}", [P, 512], F32)) for i in range(2)]
        wk = [ctx.enter_context(nc.psum_tensor(f"wk{i}", [P, 512], F32)) for i in range(6)]
        toe1 = nc.dram_tensor("toe1_scratch", (A_H, P, TOE), F32, kind="Internal").ap()
        toe2 = nc.dram_tensor("toe2_scratch", (N_H, P, TOE), F32, kind="Internal").ap()

        raw_ready = [sem(f"raw_ready{i}") for i in range(RAW)]
        hi_ready = sem("hi_ready")
        lo_ready = sem("lo_ready")
        item_done = sem("item_done")
        tile0_done = sem("tile0_done")
        evac = [sem("evac0"), sem("evac1")]
        at_end = {k: sem(f"{k}_stage") for k in ("pe", "act", "dve")}
        landed = {}

        stages = []

        class Gemm:

            base_item = 0
            base_chunk = 0
            every = []

            def __init__(self, name, lhs, kt0=0, evac_act=None, evac_dve=None, epi=None):
                spec = {s[0]: s for s in gemm_specs()}[name]
                _, self.n, self.kts, self.width = spec
                self.name, self.lhs, self.kt0 = name, lhs, kt0
                self.w = t_in["w_" + name]
                self.ipc = len(self.kts)
                self.b, self.c = Gemm.base_item, Gemm.base_chunk
                Gemm.base_item += self.n * self.ipc
                Gemm.base_chunk += self.n
                assert self.b % RAW == 0 and (self.n * self.ipc) % RAW == 0
                self.loop = self.n > 1 and self.ipc % RAW == 0
                self.ea, self.ed, self.epi = evac_act, evac_dve, epi
                self.tiles = range(TT)
                Gemm.every.append(self)

            def chunks(self, e, body):
                body(0, True)
                if self.loop:
                    with e.Fori(1, self.n) as n:
                        body(n, False)
                else:
                    for n in range(1, self.n):
                        body(n, False)

            def cols(self, j):
                return self.kts[j] * self.width

            def load(self, e):
                def body(n, first):
                    for j in range(self.ipc):
                        i = self.b + n * self.ipc + j
                        if not (first and self.b + j < RAW):
                            e.wait_ge(lo_ready, i - RAW + 1)
                        e.dma_start(w_raw[:, (self.slot(n, j)) % RAW, 0:self.cols(j)],
                                    self.w[bass.ds(n * self.ipc + j, 1), :, 0:self.cols(j)].rearrange(
                                        "a p f -> p (a f)")).then_inc(raw_ready[self.slot(n, j) % RAW], 16)
                self.chunks(e, body)

            def slot(self, n, j):
                return j if self.loop else n * self.ipc + j

            def count(self, n, j):
                if self.loop or isinstance(n, int):
                    return (self.b + (n * self.ipc if isinstance(n, int) else 0) + j) // RAW + 1 + (
                        0 if isinstance(n, int) else n * (self.ipc // RAW))

            def make_hi(self, e, n, j):
                i, s, k = self.b + n * self.ipc + j, self.slot(n, j), self.cols(j)
                e.wait_ge(raw_ready[s % RAW], self.count(n, j) * 16)
                if not (isinstance(n, int) and i < SPL):
                    e.wait_ge(item_done, i - SPL + 1)
                act_.activation(w_hi[:, s % SPL, 0:k], w_raw[:, s % RAW, 0:k], ACT.Copy).then_inc(hi_ready, 1)

            def make_lo(self, e, n, j):
                i, s, k = self.b + n * self.ipc + j, self.slot(n, j), self.cols(j)
                e.wait_ge(hi_ready, i + 1)
                dve_.tensor_tensor(w_lo[:, s % SPL, 0:k], w_raw[:, s % RAW, 0:k],
                                   w_hi[:, s % SPL, 0:k].bitcast(F32), ALU.subtract).then_inc(lo_ready, 1)

            def ahead(self):
                return 0 if self is Gemm.every[0] else SPL

            def flat(self):
                return [(n, j) for n in range(self.n) for j in range(self.ipc)]

            def split(self, e, make, evacuate, epilogue):
                at = Gemm.every.index(self)

                def body(n, first):
                    for j in range(self.ipc):
                        if at == 0 or not (isinstance(n, int) and n * self.ipc + j < SPL):
                            make(self, e, n, j)
                        if j == 0 and not first:
                            evacuate(e, n - 1)
                        if self.epi and j >= 2 and not first:
                            epilogue(e, n - 1, j - 2)
                self.chunks(e, body)
                evacuate(e, self.n - 1)
                if self is not Gemm.every[-1]:
                    nxt = Gemm.every[at + 1]
                    for i in range(SPL):
                        make(nxt, e, i // nxt.ipc, i % nxt.ipc)
                if self.epi:
                    epilogue(e, self.n - 1, 0)
                    epilogue(e, self.n - 1, 1)

            def act(self, e):
                def evacuate(e, n):
                    if self.ea:
                        e.wait_ge(tile0_done, self.c + n + 1)
                        self.ea(e, n)
                self.split(e, Gemm.make_hi, evacuate, lambda e, n, part: self.epi.act(e, n, part))

            def dve(self, e):
                def evacuate(e, n):
                    if not self.ea:
                        e.wait_ge(tile0_done, self.c + n + 1)
                        self.ed(e, n, 0)
                    e.wait_ge(item_done, self.b + (n + 1) * self.ipc)
                    self.ed(e, n, 1)
                self.split(e, Gemm.make_lo, evacuate, lambda e, n, part: self.epi.dve(e, n, part))

            def pe(self, e):
                hi, lo = self.lhs
                last = self.ipc - 1
                kt_of = [sum(self.kts[:j]) for j in range(self.ipc)]
                K = sum(self.kts)
                w = self.width

                def body(n, first):
                    for j in range(self.ipc):
                        s = self.slot(n, j) % SPL
                        e.wait_ge(lo_ready, self.b + n * self.ipc + j + 1)
                        for t in self.tiles:
                            if j == 0 and not (first and self.c == 0):
                                e.wait_ge(evac[t], self.c + n)
                            for k in range(self.kts[j]):
                                kt = kt_of[j] + k
                                wh = w_hi[:, s, k * w:(k + 1) * w]
                                wl = w_lo[:, s, k * w:(k + 1) * w]
                                xh, xl = self.tile(hi, kt, t), self.tile(lo, kt, t)
                                o = acc[t][:, 0:w]
                                pe_.matmul(o, xh, wh, start=kt == 0, stop=False)
                                pe_.matmul(o, xh, wl, start=False, stop=False)
                                mm = pe_.matmul(o, xl, wh, start=False, stop=kt == K - 1)
                            if t == TT - 1:
                                mm.then_inc(item_done, 1)
                            elif j == last:
                                mm.then_inc(tile0_done, 1)
                        if j == last and len(self.tiles) == 1:
                            e.sem_inc(tile0_done, 1)
                        if self.epi and j == min(1, last) and not first:
                            self.epi.pe(e, n - 1)
                self.chunks(e, body)
                if self.epi:
                    self.epi.pe(e, self.n - 1)

            def tile(self, a, kt, t):
                return a[:, self.kt0 + kt, t * P:(t + 1) * P]

            def run(self, k, e):
                {"pe": self.pe, "act": self.act, "dve": self.dve}[k](e)

        def rows_to(dst, width=CH, f=ACT.Copy):
            def ea(e, n):
                act_.activation(dst[:, 0, bass.ds(n * width, width)], acc[0][:, 0:width], f).then_inc(evac[0], 1)

            def ed(e, n, t):
                dve_.tensor_copy(dst[:, t, bass.ds(n * width, width)], acc[t][:, 0:width]).then_inc(evac[t], 1)
            return ea, ed

        def add_to_x():
            def ed(e, n, t):
                xs = x[:, t, bass.ds(n * CH, CH)]
                dve_.tensor_tensor(xs, acc[t][:], xs, ALU.add).then_inc(evac[t], 1)
            return None, ed

        class Steps:

            def __init__(self, name, pe=None, act=None, dve=None, pool=None):
                self.name = name
                self.f = {"pe": pe, "act": act, "dve": dve}
                self.pool = pool

            def run(self, k, e):
                if self.f[k]:
                    self.f[k](e)

        turned = sem("turned")
        turned_hi = sem("turned_hi")
        turned_lo = sem("turned_lo")
        turns = [0]

        def to_lhs(src, n, hi, lo, kt0=0, gain=None, src_ready=None):
            base = turns[0]
            turns[0] += n
            hs, banks = S, (wk[0], wk[1], wk[2], wk[3])

            def pe(e):
                for i in range(n):
                    b = banks[i % 4]
                    if i >= 4:
                        e.wait_ge(turned_lo, base + i - 3)
                    for t in range(TT):
                        mm = pe_.matmul(b[:, t * P:(t + 1) * P], src(t, i), ident[:], start=True, stop=True,
                                        is_transpose=True)
                    mm.then_inc(turned, 1)

            def act(e):
                for i in range(n):
                    e.wait_ge(turned, base + i + 1)
                    act_.activation(hi[:, kt0 + i, :], banks[i % 4][:, 0:hs], ACT.Copy,
                                    scale=gain[:, i:i + 1] if gain is not None else 1.0).then_inc(turned_hi, 1)

            def dve(e):
                for i in range(n):
                    e.wait_ge(turned_hi, base + i + 1)
                    b, h = banks[i % 4][:, 0:hs], hi[:, kt0 + i, :].bitcast(F32)
                    if gain is not None:
                        ins = dve_.scalar_tensor_tensor(out=lo[:, kt0 + i, :], in0=b, scalar=gain[:, i:i + 1],
                                                        in1=h, op0=ALU.mult, op1=ALU.subtract)
                    else:
                        ins = dve_.tensor_tensor(lo[:, kt0 + i, :], b, h, ALU.subtract)
                    ins.then_inc(turned_lo, 1)
            return pe, act, dve

        tr_done = sem("tr_done")
        tr_out = sem("tr_out")
        tr_groups = [0]

        def to_tiles(pairs, scale=None):
            base = tr_groups[0]
            tr_groups[0] += len(pairs)
            banks = (wk[0], wk[1], wk[2], wk[3])

            def pe(e):
                for i, (src, dst) in enumerate(pairs):
                    if i >= 4:
                        e.wait_ge(tr_out, base + i - 3)
                    for t in range(TT):
                        a = src(t)
                        mm = pe_.matmul(banks[i % 4][0:a.shape[1], t * P:(t + 1) * P], a, ident[:],
                                        start=True, stop=True, is_transpose=True)
                    mm.then_inc(tr_done, 1)

            def act(e):
                for i, (src, dst) in enumerate(pairs):
                    e.wait_ge(tr_done, base + i + 1)
                    bank = banks[i % 4][0:dst.shape[0], 0:S]
                    if len(dst.shape) == 3:
                        bank = bank.rearrange("p (t c) -> p t c", t=TT)
                    act_.activation(dst, bank, ACT.Copy,
                                    scale=1.0 if scale is None else scale[i]).then_inc(tr_out, 1)
            return pe, act, None

        squared = sem("squared")
        scaled = sem("scaled")
        norms = [0]

        def norm_rows(src, rows):
            base = norms[0]
            norms[0] += TT

            def act(e):
                for t in range(TT):
                    act_.activation(rows[:, t, :], src[:, t, :], ACT.Square, accum_out=st[:, t:t + 1])
                    e.drain()
                    act_.activation(st[:, 2 + t:3 + t], st[:, t:t + 1], ACT.Sqrt, scale=1.0 / D,
                                    bias=eps_c[:]).then_inc(squared, 1)

            def dve(e):
                for t in range(TT):
                    e.wait_ge(squared, base + t + 1)
                    dve_.reciprocal(st[:, 4 + t:5 + t], st[:, 2 + t:3 + t])
                    e.drain()
                    dve_.tensor_scalar(rows[:, t, :], src[:, t, :], st[:, 4 + t:5 + t], None,
                                       ALU.mult).then_inc(scaled, 1)
            return act, dve, base

        def norm_to_lhs(name, src, rows, hi, lo, gain, need=None):
            na, nd, base = norm_rows(src, rows)
            tp, ta, td = to_lhs(lambda t, i: rows[:, t, i * P:(i + 1) * P], KD, hi, lo, gain=gain)

            def pe(e):
                e.wait_ge(scaled, base + TT)
                tp(e)

            def act(e):
                if need:
                    need(e)
                na(e)
                ta(e)

            def dve(e):
                nd(e)
                td(e)
            return Steps(name, pe, act, dve)

        s_done = sem("s_done")
        s_max = sem("s_max")
        s_exp = sem("s_exp")
        s_norm = sem("s_norm")
        p_turned = sem("p_turned")
        p_copied = sem("p_copied")
        o_done = sem("o_done")
        o_hi = sem("o_hi")
        o_lo = sem("o_lo")
        units_so_far, outs_so_far = [0], [0]

        class Unit:

            def __init__(self, q, k, v, blocks, scale, bias=None, kw=P, extra=None, gate=None, first=True,
                         last=True, part=(0, P), hi=None, lo=None):
                self.q, self.k, self.v, self.scale, self.bias, self.kw = q, k, v, scale, bias, kw
                self.extra, self.gate, self.first, self.last, self.part = extra, gate, first, last, part
                self.hi, self.lo = hi, lo
                self.cols = sum(len(k_) for _, k_ in blocks) * kw
                self.seg = []
                at = 0
                for qt, kts in blocks:
                    self.seg.append((qt, kts, at))
                    at += len(kts) * kw

        def attention(name, units, L, PT, need=None):
            ub, ob = units_so_far[0], outs_so_far[0]
            units_so_far[0] += len(units)
            outs = []
            for i, u in enumerate(units):
                u.out = len(outs)
                if u.last:
                    outs.append(i)
            outs_so_far[0] += len(outs)
            sc, tb, ov = (wk[0], wk[1]), wk[2], (wk[3], wk[4])
            N = len(units)

            def scores(e, i):
                u = units[i]
                if i >= 2:
                    e.wait_ge(s_max, ub + i - 1)
                for qt, kts, at in u.seg:
                    o = sc[i % 2][:, at:at + len(kts) * u.kw]
                    more = u.extra(qt, kts) if u.extra else []
                    mm = pe_.matmul(o, u.q[:, qt * P:(qt + 1) * P], u.k[:, 0:len(kts) * u.kw],
                                    start=True, stop=not more)
                    for n, (a, b) in enumerate(more):
                        mm = pe_.matmul(o, a, b, start=False, stop=n == len(more) - 1)
                mm.then_inc(s_done, 1)

            def turn(e, i):
                u = units[i]
                e.wait_ge(s_norm, ub + i + 1)
                if i >= 1:
                    e.wait_ge(p_copied, ub + i)
                c = 0
                for qt, kts, at in u.seg:
                    for n in range(len(kts)):
                        mm = pe_.matmul(tb[0:u.kw, c * P:(c + 1) * P],
                                        L[:, i % 2, at + n * u.kw:at + (n + 1) * u.kw], ident[:],
                                        start=True, stop=True, is_transpose=True)
                        c += 1
                mm.then_inc(p_turned, 1)

            def values(e, i):
                u = units[i]
                e.wait_ge(p_copied, ub + i + 1)
                if u.first and u.out >= 2:
                    e.wait_ge(o_lo, ob + u.out - 1)
                c = 0
                p0, p1 = u.part
                for qt, kts, at in u.seg:
                    for n, kt in enumerate(kts):
                        mm = pe_.matmul(ov[u.out % 2][p0:p1, qt * P:(qt + 1) * P], u.v(kt),
                                        PT[0:u.kw, i % 2, c * P:(c + 1) * P],
                                        start=u.first and n == 0 and qt == 0, stop=u.last and n == len(kts) - 1,
                                        skip_group_check=True)
                        c += 1
                mm.then_inc(o_done, 1)

            def pe(e):
                for i in range(N + 2):
                    if i < N:
                        scores(e, i)
                    if 1 <= i <= N:
                        turn(e, i - 1)
                    if i >= 2:
                        values(e, i - 2)

            def act(e):
                for i in range(N + 3):
                    if i < N:
                        u = units[i]
                        e.wait_ge(s_max, ub + i + 1)
                        for n, (qt, kts, at) in enumerate(u.seg):
                            a = L[:, i % 2, at:at + len(kts) * u.kw]
                            ins = act_.activation(a, a, ACT.Exp, bias=st[:, 16 + 8 * (i % 2) + n:17 + 8 * (i % 2) + n],
                                                  accum_out=st[:, 18 + 8 * (i % 2) + n:19 + 8 * (i % 2) + n])
                        ins.then_inc(s_exp, 1)
                    if 1 <= i <= N:
                        u = units[i - 1]
                        e.wait_ge(p_turned, ub + i)
                        if i >= 3:
                            e.wait_ge(o_done, ub + i - 2)
                        c = sum(len(k_) for _, k_, _ in u.seg) * P
                        act_.activation(PT[0:u.kw, (i - 1) % 2, 0:c], tb[0:u.kw, 0:c], ACT.Copy).then_inc(p_copied, 1)
                    if i >= 3 and units[i - 3].last:
                        u = units[i - 3]
                        e.wait_ge(o_done, ub + i - 2)
                        act_.activation(u.hi, ov[u.out % 2][u.part[0]:u.part[1], 0:S], ACT.Copy).then_inc(o_hi, 1)

            def dve(e):
                if need:
                    need(e)
                for i in range(N + 3):
                    if i < N:
                        u = units[i]
                        b = 16 + 8 * (i % 2)
                        e.wait_ge(s_done, ub + i + 1)
                        if i >= 2:
                            e.wait_ge(p_turned, ub + i - 1)
                        l = L[:, i % 2, 0:u.cols]
                        if u.bias is not None:
                            dve_.scalar_tensor_tensor(out=l, in0=sc[i % 2][:, 0:u.cols], scalar=u.scale, in1=u.bias,
                                                      op0=ALU.mult, op1=ALU.add)
                        else:
                            dve_.tensor_scalar(l, sc[i % 2][:, 0:u.cols], u.scale, None, ALU.mult)
                        e.drain()
                        for n, (qt, kts, at) in enumerate(u.seg):
                            dve_.tensor_reduce(st[:, b + n:b + n + 1], L[:, i % 2, at:at + len(kts) * u.kw],
                                               AX.X, ALU.max)
                        e.drain()
                        dve_.tensor_scalar(st[:, b:b + 2], st[:, b:b + 2], -1.0, FLOOR, ALU.mult,
                                           ALU.min).then_inc(s_max, 1)
                    if 1 <= i <= N:
                        u = units[i - 1]
                        b = 16 + 8 * ((i - 1) % 2)
                        e.wait_ge(s_exp, ub + i)
                        dve_.tensor_scalar(st[:, b + 2:b + 4], st[:, b + 2:b + 4], 1e-30, None, ALU.max)
                        e.drain()
                        dve_.reciprocal(st[:, b + 4:b + 6], st[:, b + 2:b + 4])
                        e.drain()
                        for n, (qt, kts, at) in enumerate(u.seg):
                            a = L[:, (i - 1) % 2, at:at + len(kts) * u.kw]
                            if u.gate:
                                ins = dve_.tensor_scalar(a, a, st[:, b + 4 + n:b + 5 + n], u.gate(qt), ALU.mult, ALU.mult)
                            else:
                                ins = dve_.tensor_scalar(a, a, st[:, b + 4 + n:b + 5 + n], None, ALU.mult)
                        ins.then_inc(s_norm, 1)
                    if i >= 3 and units[i - 3].last:
                        u = units[i - 3]
                        e.wait_ge(o_hi, ob + u.out + 1)
                        dve_.tensor_tensor(u.lo, ov[u.out % 2][u.part[0]:u.part[1], 0:S], u.hi.bitcast(F32),
                                           ALU.subtract).then_inc(o_lo, 1)
            return Steps(name, pe, act, dve)

        def stage_end(e, k, i):
            e.drain().then_inc(at_end[k], 1)
            for other in at_end:
                if other != k:
                    e.wait_ge(at_end[other], i + 1)

        def bc(ap, n):
            return ap.unsqueeze(1).to_broadcast([ap.shape[0], n, ap.shape[1]])

        def load(e, name, dst, src, after=None):
            landed[name] = landed.get(name) or sem("in_" + name)
            if after is not None:
                for k in at_end:
                    e.wait_ge(at_end[k], after)
            e.dma_start(dst, src).then_inc(landed[name], 16)

        def got(e, name):
            if name not in landed:
                landed[name] = sem("in_" + name)
            e.wait_ge(landed[name], 16)

        pool_steps = []
        def at(label):
            return [s.name for s in stages].index(label)

        ar1 = ExitStack()
        p1 = sb("p1", [P, TT, P1_N], F32, ar1)
        tt1 = sb("tt1", [P, 20, S], F32, ar1)
        c8 = sb("c8", [8, 2, S], F32, ar1)
        b_t = sb("b_t", [C_DK, C_H, S], F32, ar1)
        cmask = sb("cmask", [P, 384], F32, ar1)
        l1 = sb("l1", [P, 2, 384], F32, ar1)
        pt1 = sb("pt1", [P, 2, 384], F32, ar1)

        rows0 = p1[:, :, 0:D]
        toe_mm, toe_row, toe_out, toe_dma = sem("toe_mm"), sem("toe_row"), sem("toe_out"), sem("toe_dma")
        tt1f = tt1[:].rearrange("p a b -> p (a b)")

        def toe_place(rows, slot, w):
            return [tt1f[0:r, (4 * i + slot) * 400:(4 * i + slot) * 400 + c] for i, (r, c) in enumerate(zip(rows, w))]
        tw = toe_place((REL, REL), 0, (TOE, TOE))
        trel = toe_place((REL, REL), 1, (A_H, N_H))
        tadd = toe_place((A_H, N_H), 2, (TOE, TOE))
        tsum = toe_place((A_H, N_H), 3, (TOE, TOE))

        def toe_pool(e):
            load(e, "ident", ident[:], t_in["ident"])
            load(e, "x", x[:], t_in["x"])
            load(e, "gains", gains[:], t_in["gains"])
            load(e, "tri", tri[:], t_in["tri"])
            load(e, "cmask", cmask[:], t_in["cmask"])
            for i in range(2):
                load(e, f"tw{i}", tw[i], t_in[f"onehot{i}"])
                load(e, f"trel{i}", trel[i], t_in[f"rel{i}"])
                load(e, f"tadd{i}", tadd[i], t_in[f"toe_add{i}"])
            e.wait_ge(toe_out, 2)
            for table, row, heads in ((toe1, tsum[0], A_H), (toe2, tsum[1], N_H)):
                e.dma_start(table, row.unsqueeze(1).to_broadcast([heads, P, TOE])).then_inc(toe_dma, 16)
            e.wait_ge(toe_dma, 32)
        pool_steps.append(toe_pool)

        def toe_pe(e):
            for i in range(2):
                got(e, f"tw{i}")
                got(e, f"trel{i}")
                pe_.matmul(wk[4 + i][0:(A_H, N_H)[i], 0:TOE], trel[i], tw[i], start=True, stop=True).then_inc(toe_mm, 1)
            got(e, "ident")

        def toe_dve(e):
            dve_.memset(ones[:], 1.0)
            dve_.memset(eps_c[:], EPS)
            for i in range(2):
                got(e, f"tadd{i}")
                e.wait_ge(toe_mm, i + 1)
                dve_.tensor_tensor(tsum[i], wk[4 + i][0:(A_H, N_H)[i], 0:TOE], tadd[i], ALU.add).then_inc(toe_out, 1)
            got(e, "x")
            got(e, "gains")

        def toe_act(e):
            got(e, "x")
            got(e, "gains")
        stages.append(Steps("tables", toe_pe, toe_act, toe_dve))
        stages.append(norm_to_lhs("norm_mix", x, rows0, h_hi, h_lo, gains[:, 0, :]))
        stages[-1].pool_wait = True
        lhs = (h_hi, h_lo)
        stages.append(Gemm("win", lhs, 0, *rows_to(p1)))

        w_s1 = tt1[:, 0:2, :].rearrange("p a b -> p (a b)")[:, 0:KD * 24]
        srow = tt1[:, 2, 0:48]
        glt = tt1[0:C_R, 3, :]
        w_g2 = tt1[0:C_R, 4:6, :].rearrange("p a b -> p (a b)")[:, 0:C_KW]
        gb = tt1[0:1, 6:8, :].rearrange("p a b -> p (a b)")[:, 0:C_KW]
        fb = tt1[:, 8, 0:B_H]
        LAW = 16 + 2 * C_KW
        la = tt1[:, 9:13, :].rearrange("p a b -> p (a b)")[:, 0:LAW]
        la_t = tt1[:, 13:17, :].rearrange("p a b -> p (a b)")[:, 0:LAW]
        s1_mm, s1_row, s1_tr, s1_gl, s1_la, s1_abs, s1_ln, s1_log, s1_cum = [
            sem(n) for n in ("small_prod", "small_rows", "gl_turned", "gl_copied", "gate_logits", "gate_abs",
                             "gate_ln", "log_gates", "gates_summed")]

        def small1_pool(e):
            load(e, "w_s1", w_s1, t_in["w_small1"], after=0)
            load(e, "w_g2", w_g2, t_in["c_gate_w2"])
            load(e, "gb", gb, t_in["c_gate_b"])
            load(e, "fb", fb, t_in["f_bias"].to_broadcast([P, B_H]))
        pool_steps.append(small1_pool)

        def small1_pe(e):
            got(e, "w_s1")
            for t in range(TT):
                for kt in range(KD):
                    for a in lhs:
                        mm = pe_.matmul(wk[0][:, t * 24:(t + 1) * 24], a[:, kt, t * P:(t + 1) * P].bitcast(F32),
                                        w_s1[:, kt * 24:(kt + 1) * 24], start=kt == 0 and a is h_hi,
                                        stop=kt == KD - 1 and a is h_lo)
            mm.then_inc(s1_mm, 1)
            e.wait_ge(s1_row, 1)
            for t in range(TT):
                mm = pe_.matmul(wk[1][0:C_R, t * P:(t + 1) * P], srow[:, t * 24 + 8:t * 24 + 24], ident[:],
                                start=True, stop=True, is_transpose=True)
            mm.then_inc(s1_tr, 1)
            e.wait_ge(s1_gl, 1)
            got(e, "w_g2")
            got(e, "gb")
            for t in range(TT):
                pe_.matmul(wk[2 + t][:, 0:C_KW], glt[:, t * P:(t + 1) * P], w_g2, start=True, stop=False)
                mm = pe_.matmul(wk[2 + t][:, 0:C_KW], ones[0:1, :], gb, start=False, stop=True)
            mm.then_inc(s1_la, 1)
            e.wait_ge(s1_log, 1)
            got(e, "tri")
            for t in range(TT):
                pe_.matmul(wk[0][0:8, 0:S], la[:, t * 8:t * 8 + 8], tri[:, t, :], start=t == 0, stop=t == 1)
            for h in range(C_H):
                for t in range(TT):
                    c = 16 + t * C_KW + h * C_DK
                    mm = pe_.matmul(wk[4 + h // 2][0:C_DK, (h % 2) * S:(h % 2 + 1) * S], la[:, c:c + C_DK],
                                    tri[:, t, :], start=t == 0, stop=t == 1)
            mm.then_inc(s1_cum, 1)

        def small1_act(e):
            e.wait_ge(s1_mm, 1)
            act_.activation(srow, wk[0][:, 0:48], ACT.Copy).then_inc(s1_row, 1)
            e.wait_ge(s1_tr, 1)
            act_.activation(glt, wk[1][0:C_R, 0:S], ACT.Copy).then_inc(s1_gl, 1)
            e.wait_ge(s1_abs, 1)
            act_.activation(la_t, la_t, ACT.Exp)
            e.drain()
            act_.activation(la_t, la_t, ACT.Ln, bias=ones[:, 0:1]).then_inc(s1_ln, 1)
            e.wait_ge(s1_cum, 1)
            act_.activation(c8[:, 0, :], wk[0][0:8, 0:S], ACT.Copy, scale=8.0)
            act_.activation(c8[:, 1, :], wk[0][0:8, 0:S], ACT.Copy, scale=-8.0)
            for h in range(0, C_H, 2):
                act_.activation(b_t[:, h:h + 2, :].rearrange("p a b -> p (a b)"), wk[4 + h // 2][0:C_DK, :],
                                ACT.Copy, scale=1.0 / 16)

        def small1_dve(e):
            e.wait_ge(s1_row, 1)
            got(e, "fb")
            for t in range(TT):
                dve_.tensor_tensor(la[:, t * 8:t * 8 + 8], srow[:, t * 24:t * 24 + 8], fb, ALU.add)
            e.wait_ge(s1_la, 1)
            for t in range(TT):
                dve_.tensor_copy(la[:, 16 + t * C_KW:16 + (t + 1) * C_KW], wk[2 + t][:, 0:C_KW])
            e.drain()
            dve_.scalar_tensor_tensor(out=la_t, in0=la, scalar=-1.0, in1=la, op0=ALU.mult,
                                      op1=ALU.min).then_inc(s1_abs, 1)
            e.drain()
            dve_.tensor_scalar(la, la, 0.0, None, ALU.min)
            e.drain()
            e.wait_ge(s1_ln, 1)
            dve_.tensor_tensor(la, la, la_t, ALU.subtract).then_inc(s1_log, 1)
        stages.append(Steps("small1", small1_pe, small1_act, small1_dve))

        stages.append(Steps("turn1", *to_tiles([
            ((lambda t, i=i: p1[:, t, i * P:(i + 1) * P]), tt1[:, i, :]) for i in range(20)])))

        def toeplitz(e, name, dst, table, heads, at_stage):
            landed[name] = sem("in_" + name)
            for k in at_end:
                e.wait_ge(at_end[k], at_stage)
            for h in range(heads):
                for c0, w, off in ((0, P, 255), (P, S, 127)):
                    src = bass.AP(tensor=table.tensor, offset=h * P * TOE + off, ap=[[TOE - 1, P], [1, w]])
                    e.dma_start(dst(h)[:, c0:c0 + w], src).then_inc(landed[name], 16)

        def bias1(h):
            return p1[:, h // 6, (h % 6) * TOE:(h % 6 + 1) * TOE]
        after_turn1 = len(stages)
        pool_steps.append(lambda e: toeplitz(e, "bias1", bias1, toe1, A_H, after_turn1))

        def half(h):
            return (h % 2) * 64, (h % 2) * 64 + 64

        def a_unit(h):
            p0, p1_ = half(h)
            return Unit(tt1[p0:p1_, h // 2, :], tt1[p0:p1_, 6 + h // 2, :],
                        lambda kt: p1[:, kt, P1_VA + h * 64:P1_VA + (h + 1) * 64], CAUSAL, A_D ** -0.5, bias1(h),
                        part=(p0, p1_), hi=h_hi[p0:p1_, h // 2, :], lo=h_lo[p0:p1_, h // 2, :])

        def b_unit(h):
            p0, p1_ = half(h)

            def extra(qt, kts):
                one = ident[0:8, h:h + 1]
                n = len(kts) * P
                return [(c8[:, 0, qt * P:(qt + 1) * P], one.to_broadcast([8, n])),
                        (one.to_broadcast([8, P]), c8[:, 1, 0:n])]
            return Unit(tt1[p0:p1_, 12 + h // 2, :], tt1[p0:p1_, 16 + h // 2, :],
                        lambda kt: p1[:, kt, P1_VB + h * 64:P1_VB + (h + 1) * 64], CAUSAL, A_D ** -0.5, cmask[:],
                        extra=extra, part=(p0, p1_), hi=h_hi[p0:p1_, 6 + h // 2, :], lo=h_lo[p0:p1_, 6 + h // 2, :])

        def bias1_there(e):
            e.wait_ge(landed["bias1"], 16 * 2 * A_H)
            got(e, "cmask")
        stages.append(attention("attention_ab", [a_unit(h) for h in range(A_H)] + [b_unit(h) for h in range(B_H)],
                                l1, pt1, bias1_there))

        qk_c = tt1[0:C_DK, 0:8, :]
        q_c, k_c = qk_c[:, 0:4, :], qk_c[:, 4:8, :]
        stages.append(Steps("turn_c", *to_tiles(
            [((lambda t, c=c: p1[:, t, c:c + C_DK]), qk_c[:, i, :])
             for i, c in enumerate([P1_QC + h * C_DK for h in range(4)] + [P1_KC + h * C_DK for h in range(4)])],
            [C_DK ** -0.5] * 4 + [1.0] * 4)))
        dif = tt1[0:C_DK, 8:12, :]
        xqk = tt1[0:C_DK, 12:16, :]
        a_t = tt1[:, 16:20, :].rearrange("p a b -> p (a b)").rearrange("p (t h i) -> p t h i", t=2, h=4)
        a_off = l1[:].rearrange("p a b -> p (a b)")[:, 0:512].rearrange("p (h i) -> p h i", h=4)
        tmp_c = pt1[:].rearrange("p a b -> p (a b)")[:, 0:512].rearrange("p (h i) -> p h i", h=4)
        lmask = p1[:, 0, 1024:2048].rearrange("p (l i) -> p l i", l=8)
        cn = p1[:, 1, 1024:1024 + C_DV]
        o_c = p1[:, :, 0:C_VW]
        after_ab = len(stages) - 1

        def gla_pool(e):
            load(e, "lmask", lmask, t_in["lmask"], after=after_ab)
            load(e, "cn", cn, t_in["c_norm"].to_broadcast([P, C_DV]))
        pool_steps.append(gla_pool)
        g_dif, g_exp, g_x, g_mm, g_acc, g_o, g_ss, g_silu = [sem(n) for n in (
            "gla_exponent", "gla_decay", "gla_scaled", "gla_scores", "gla_summed", "gla_out", "gla_squares", "gla_gate")]
        LEV = 8

        def halves(a, s):
            return a.rearrange("p h (n two s) -> p (h n) two s", two=2, s=s)

        def gla_dve(e):
            def exponent(l):
                s = 1 << l
                b, d = halves(b_t[:], s), halves(dif, s)
                e.drain()
                ref = b[:, :, 0, s - 1:s].to_broadcast([C_DK, 4 * S // (2 * s), s])
                dve_.tensor_tensor(d[:, :, 1, :], b[:, :, 1, :], ref, ALU.subtract)
                dve_.tensor_tensor(d[:, :, 0, :], ref, b[:, :, 0, :], ALU.subtract).then_inc(g_dif, 1)

            def scaled_(l):
                s = 1 << l
                e.wait_ge(g_exp, l + 1)
                if l:
                    e.wait_ge(g_mm, l)
                d, xx = halves(dif, s), halves(xqk, s)
                dve_.tensor_tensor(xx[:, :, 1, :], halves(q_c, s)[:, :, 1, :], d[:, :, 1, :], ALU.mult)
                dve_.tensor_tensor(xx[:, :, 0, :], halves(k_c, s)[:, :, 0, :], d[:, :, 0, :],
                                   ALU.mult).then_inc(g_x, 1)

            def add_level(l):
                e.wait_ge(g_mm, l + 1)
                bank = [wk[2 * (l % 2) + t][:].rearrange("p (h i) -> p h i", h=4) for t in range(2)]
                if l == LEV - 1:
                    dve_.tensor_copy(a_off, bank[0]).then_inc(g_acc, 1)
                    return
                mask = bc(ident[:] if l == LEV else lmask[:, l, :], 4)
                for t in range(2):
                    if l == 0:
                        ins = dve_.tensor_tensor(a_t[:, t], bank[t], mask, ALU.mult)
                    else:
                        dve_.tensor_tensor(tmp_c, bank[t], mask, ALU.mult)
                        e.drain()
                        ins = dve_.tensor_tensor(a_t[:, t], a_t[:, t], tmp_c, ALU.add)
                        e.drain()
                ins.then_inc(g_acc, 1)
            got(e, "lmask")
            for l in range(LEV):
                exponent(l)
                if l:
                    add_level(l - 1)
                scaled_(l)
            add_level(LEV - 1)
            add_level(LEV)
            got(e, "cn")
            e.wait_ge(g_ss, 1)
            dve_.reciprocal(st[:, 48:56], st[:, 40:48])
            e.drain()
            for t in range(TT):
                for h in range(C_H):
                    dve_.scalar_tensor_tensor(out=o_c[:, t, h * C_DV:(h + 1) * C_DV],
                                              in0=wk[2 * t + h // 2][:, (h % 2) * C_DV:(h % 2 + 1) * C_DV],
                                              scalar=st[:, 48 + t * 4 + h:49 + t * 4 + h], in1=cn,
                                              op0=ALU.mult, op1=ALU.mult)
            e.drain()
            e.wait_ge(g_silu, 1)
            dve_.tensor_tensor(o_c, o_c, p1[:, :, P1_RC:P1_RC + C_VW], ALU.mult)

        def gla_act(e):
            for l in range(LEV):
                e.wait_ge(g_dif, l + 1)
                act_.activation(dif, dif, ACT.Exp).then_inc(g_exp, 1)
            act_.activation(p1[:, :, P1_RC:P1_RC + C_VW], p1[:, :, P1_RC:P1_RC + C_VW], ACT.Silu).then_inc(g_silu, 1)
            e.wait_ge(g_o, 1)
            for t in range(TT):
                for h in range(C_H):
                    ins = act_.activation(tmp_c.rearrange("p h i -> p (h i)")[:, 0:C_DV],
                                          wk[2 * t + h // 2][:, (h % 2) * C_DV:(h % 2 + 1) * C_DV],
                                          ACT.Square, accum_out=st[:, 32 + t * 4 + h:33 + t * 4 + h])
                    e.drain()
            act_.activation(st[:, 40:48], st[:, 32:40], ACT.Sqrt, scale=1.0 / C_DV, bias=eps_c[:]).then_inc(g_ss, 1)

        def gla_pe(e):
            for l in range(LEV + 1):
                if l < LEV:
                    e.wait_ge(g_x, l + 1)
                if l >= 2:
                    e.wait_ge(g_acc, l - 1)
                a, b = (xqk, xqk) if l < LEV else (k_c, q_c)
                for t in range(TT if l != LEV - 1 else 1):
                    t1 = t if l != LEV - 1 else 1
                    for h in range(C_H):
                        mm = pe_.matmul(wk[2 * (l % 2) + t][:, h * P:(h + 1) * P], a[:, h, t * P:(t + 1) * P],
                                        b[:, h, t1 * P:(t1 + 1) * P], start=True, stop=True)
                mm.then_inc(g_mm, 1)
            e.wait_ge(g_acc, LEV + 1)
            for t in range(TT):
                for h in range(C_H):
                    v = [p1[:, k, P1_VC + h * C_DV:P1_VC + (h + 1) * C_DV] for k in range(2)]
                    o = wk[2 * t + h // 2][:, (h % 2) * C_DV:(h % 2 + 1) * C_DV]
                    if t:
                        pe_.matmul(o, a_off[:, h, :], v[0], start=True, stop=False)
                    mm = pe_.matmul(o, a_t[:, t, h, :], v[t], start=t == 0, stop=True)
            mm.then_inc(g_o, 1)
        stages.append(Steps("gla", gla_pe, gla_act, gla_dve))
        stages.append(Steps("turn_oc", *to_lhs(lambda t, i: o_c[:, t, i * P:(i + 1) * P], 6, h_hi, h_lo, kt0=10)))
        stages.append(Gemm("wout", lhs, 0, *add_to_x()))

        mem = p1[:, :, 0:D]
        memr = p1[:, :, D:2 * D]
        kvr = p1[:, :, 2 * D:2 * D + 1024]
        qr = p1[:, :, 2 * D + 1024:2 * D + 1536]
        before_mem = len(stages) - 1
        pool_steps.append(lambda e: load(e, "mem", mem, t_in["mem"], after=before_mem))
        stages.append(norm_to_lhs("norm_mem", mem, memr, h_hi, h_lo, gains[:, 1, :], need=lambda e: got(e, "mem")))
        stages.append(Gemm("ckv", lhs, 0, *rows_to(kvr)))
        stages.append(norm_to_lhs("norm_cross", x, memr, h_hi, h_lo, gains[:, 2, :]))
        stages.append(Gemm("cq", lhs, 0, *rows_to(qr)))
        stages.append(Steps("turn_x", *to_tiles(
            [((lambda t, h=h: qr[:, t, h * P:(h + 1) * P]), tt1[:, h, :]) for h in range(4)] +
            [((lambda t, h=h: kvr[:, t, h * P:(h + 1) * P]), tt1[:, 4 + h, :]) for h in range(4)])))
        lx = tt1[:, 8:12, :].rearrange("p a b -> p (a b)").rearrange("p (a b) -> p a b", a=2)
        px = tt1[:, 12:16, :].rearrange("p a b -> p (a b)").rearrange("p (a b) -> p a b", a=2)
        stages.append(attention("attention_x", [
            Unit(tt1[:, h, :], tt1[:, 4 + h, :], (lambda kt, h=h: kvr[:, kt, 512 + h * P:512 + (h + 1) * P]), FULL,
                 X_D ** -0.5, hi=h_hi[:, h, :], lo=h_lo[:, h, :]) for h in range(4)], lx, px))
        stages.append(Gemm("co", lhs, 0, *add_to_x()))
        stages.append(norm_to_lhs("norm_ffn", x, memr, h_hi, h_lo, gains[:, 3, :]))
        ar1.close()

        ar = ExitStack()
        f_hi = sb("f_hi", [P, 32, S], F32R, ar)
        f_lo = sb("f_lo", [P, 32, S], F32R, ar)
        stg = sb("stg", [P, TT, CH], F32, ar)
        gp = sb("gp", [P, 2, S + 2], F32, ar)
        cv = sb("cv", [P, 2, S], F32, ar)
        sq = sb("sq", [P, 4, S], F32, ar)
        cw = sb("cw", [P, KF1, 4], F32, ar)
        flhs = (f_hi, f_lo)
        rows_f = f_hi[:, 0:16, :]
        stg_turned, ep_gate, ep_conv, ep_silu, ep_mul, ep_hi, ep_lo = [sem(n) for n in (
            "chunk_turned", "gate_copied", "conv_done", "silu_done", "hidden_done", "hidden_hi", "hidden_lo")]
        ep_n = [0]

        def stage_rows(f, width, stg):
            def ea(e, n):
                act_.activation(stg[:, 0, 0:width], acc[0][:, 0:width], f).then_inc(evac[0], 1)

            def ed(e, n, t):
                if f is ACT.Relu:
                    dve_.tensor_scalar(stg[:, t, 0:width], acc[t][:, 0:width], 0.0, None, ALU.max).then_inc(evac[t], 1)
                else:
                    dve_.tensor_copy(stg[:, t, 0:width], acc[t][:, 0:width]).then_inc(evac[t], 1)
            return ea, ed

        class Hidden:

            def __init__(self, kind, n, kt0, ct0, tiles, chunk0, bufs):
                self.f_hi, self.f_lo, self.stg, self.sq = bufs
                self.kind, self.kt0, self.ct0, self.tiles, self.chunk0 = kind, kt0, ct0, tiles, chunk0
                self.base = ep_n[0]
                ep_n[0] += n

            def pe(self, e, n):
                i = self.base + n
                for t in range(TT):
                    e.wait_ge(evac[t], self.chunk0 + n + 1)
                if self.base or not isinstance(n, int) or n:
                    e.wait_ge(ep_lo, i)
                nt = self.tiles * (2 if self.kind == "conv" else 1)
                for c in range(nt):
                    for t in range(TT):
                        per = self.tiles if self.kind == "conv" else 2
                        mm = pe_.matmul(wk[c // per][:, (c % per) * S + t * P:(c % per) * S + (t + 1) * P],
                                        self.stg[:, t, c * P:(c + 1) * P], ident[:], start=True, stop=True,
                                        is_transpose=True)
                mm.then_inc(stg_turned, 1)

            def out(self, a, n):
                return a[:, bass.ds(self.kt0 + n * self.tiles, self.tiles), :]

            def act(self, e, n, part):
                i, k = self.base + n, self.tiles
                if self.kind == "conv":
                    if part == 0:
                        e.wait_ge(stg_turned, i + 1)
                        act_.activation(gp[:, 0:k, 2:S + 2], wk[1][:, 0:k * S].rearrange("p (c s) -> p c s", c=k),
                                        ACT.Copy).then_inc(ep_gate, 1)
                    else:
                        e.wait_ge(ep_conv, i + 1)
                        act_.activation(cv[:, 0:k, :], cv[:, 0:k, :], ACT.Silu).then_inc(ep_silu, 1)
                        e.wait_ge(ep_mul, i + 1)
                        act_.activation(self.out(self.f_hi, n), self.sq[:, 0:k, :], ACT.Copy).then_inc(ep_hi, 1)
                elif part == 0:
                    e.wait_ge(stg_turned, i + 1)
                    for b in range(2):
                        act_.activation(self.sq[:, 2 * b:2 * b + 2, :], wk[b][:].rearrange("p (c s) -> p c s", c=2),
                                        ACT.Square)
                    e.drain()
                else:
                    act_.activation(self.out(self.f_hi, n), self.sq[:], ACT.Copy).then_inc(ep_hi, 1)

            def dve(self, e, n, part):
                i, k = self.base + n, self.tiles
                if self.kind == "conv":
                    if part == 0:
                        e.wait_ge(ep_gate, i + 1)
                        for tap in range(3):
                            for c in range(k):
                                w = cw[:, bass.ds(self.ct0 + n * k + c, 1), :].rearrange("p a b -> p (a b)")
                                g = gp[:, c, tap:tap + S]
                                if tap == 0:
                                    ins = dve_.tensor_scalar(cv[:, c, :], g, w[:, 0:1], w[:, 3:4], ALU.mult, ALU.add)
                                else:
                                    ins = dve_.scalar_tensor_tensor(out=cv[:, c, :], in0=g, scalar=w[:, tap:tap + 1],
                                                                    in1=cv[:, c, :], op0=ALU.mult, op1=ALU.add)
                            if tap < 2:
                                e.drain()
                        ins.then_inc(ep_conv, 1)
                    else:
                        e.wait_ge(ep_silu, i + 1)
                        dve_.tensor_tensor(self.sq[:, 0:k, :], cv[:, 0:k, :],
                                           wk[0][:, 0:k * S].rearrange("p (c s) -> p c s", c=k),
                                           ALU.mult).then_inc(ep_mul, 1)
                if part == 1:
                    e.wait_ge(ep_hi, i + 1)
                    kk = k if self.kind == "conv" else 4
                    dve_.tensor_tensor(self.out(self.f_lo, n), self.sq[:, 0:kk, :], self.out(self.f_hi, n).bitcast(F32),
                                       ALU.subtract).then_inc(ep_lo, 1)

        before_up = len(stages)
        pool_steps.append(lambda e: load(e, "cw", cw[:], t_in["conv1"], after=before_up))

        def pads(e):
            dve_.memset(gp[:, :, 0:2], 0.0)
            got(e, "cw")
        stages.append(Steps("pads", None, None, pads))

        def up(name, kind, kt0, ct0, tiles, f, width=CH):
            g = Gemm(name, lhs, 0, *stage_rows(f, width, stg))
            g.epi = Hidden(kind, g.n, kt0, ct0, tiles, g.c, (f_hi, f_lo, stg, sq))
            stages.append(g)
        up("up_a", "conv", 0, 0, 2, ACT.Copy)
        stages.append(Gemm("down_a", flhs, 0, *add_to_x()))
        up("up_b", "conv", 0, 22, 2, ACT.Copy)
        up("up_t", "conv", 20, 42, 1, ACT.Copy, CH // 2)
        stages.append(Gemm("down_b", flhs, 0, *add_to_x()))
        ar.close()


        def norm_times(name, row, gain_bc):
            base = norms[0]
            norms[0] += TT

            def act(e):
                for t in range(TT):
                    act_.activation(row, x[:, t, :], ACT.Square, accum_out=st[:, t:t + 1])
                    e.drain()
                    act_.activation(st[:, 2 + t:3 + t], st[:, t:t + 1], ACT.Sqrt, scale=1.0 / D,
                                    bias=eps_c[:]).then_inc(squared, 1)

            def dve(e):
                got(e, name)
                for t in range(TT):
                    e.wait_ge(squared, base + t + 1)
                    dve_.reciprocal(st[:, 4 + t:5 + t], st[:, 2 + t:3 + t])
                    e.drain()
                    dve_.scalar_tensor_tensor(out=x[:, t, :], in0=x[:, t, :], scalar=st[:, 4 + t:5 + t], in1=gain_bc,
                                              op0=ALU.mult, op1=ALU.mult).then_inc(scaled, 1)
            return Steps(name, None, act, dve)

        ar2 = ExitStack()
        oa_hi = sb("oa_hi", [P, 8, S], F32R, ar2)
        oa_lo = sb("oa_lo", [P, 8, S], F32R, ar2)
        sm = sb("sm", [P, 368], F32, ar2)
        gtt = sb("gtt", [8, 2, S], F32, ar2)
        arn = ExitStack()
        p2 = sb("p2", [P, TT, P2_N], F32, arn)
        tt2 = sb("tt2", [P, 16, S], F32, arn)
        lp2 = sb("lp2", [P, 4 * TOE], F32, arn)
        misc = sb("misc", [P, 1024], F32, arn)
        l2 = lp2[:, 0:2 * TOE].rearrange("p (a b) -> p a b", a=2)
        pt2 = lp2[:, 2 * TOE:].rearrange("p (a b) -> p a b", a=2)
        tt2f = tt2[:].rearrange("p a b -> p (a b)")

        before_nf = len(stages)
        pool_steps.append(lambda e: load(e, "norm_final", tt2f[:, 0:D], t_in["norm_final"].to_broadcast([P, D]),
                                         after=before_nf))
        p2f = p2[:].rearrange("p a b -> p (a b)")
        stages.append(norm_times("norm_final", p2f[:, 0:D], tt2f[:, 0:D]))
        stages.append(norm_to_lhs("norm_ln1", x, p2f[:, 0:2 * D].rearrange("p (t c) -> p t c", t=TT), h_hi, h_lo,
                                  gains[:, 4, :]))
        stages.append(Gemm("win2", lhs, 0, *rows_to(p2)))

        w_s2 = lp2[:, 0:KD * 40]
        rel_c = lp2[0:REL, 640:648]
        mask_c = lp2[:, 648:678]
        ohc = tt2f[0:REL, 0:N_CMP * S]
        alog = lp2[:, 680:688]
        dtb = lp2[:, 688:696]
        bias_c = misc[:, 0:240]
        srow2, gate3, beta = sm[:, 0:80], sm[:, 80:128], sm[:, 128:144]
        grow, gend, expg, kdec_s, yv, ya = [sm[:, 144 + 16 * k:160 + 16 * k] for k in range(6)]
        s2_mm, s2_row, s2_abs, s2_ln, s2_g, s2_cum, s2_cp = [sem(n) for n in (
            "small2_prod", "small2_rows", "rate_abs", "rate_ln", "log_decays", "decays_summed", "decays_copied")]
        before_s2 = len(stages)

        def small2_pool(e):
            load(e, "w_s2", w_s2, t_in["w_small2"], after=before_s2)
            load(e, "rel_c", rel_c, t_in["rel1"])
            load(e, "mask_c", mask_c, t_in["mask_c"])
            load(e, "ohc", ohc, t_in["onehot_c"])
            load(e, "alog", alog, t_in["a_log"].to_broadcast([P, 8]))
            load(e, "dtb", dtb, t_in["dt_bias"].to_broadcast([P, 8]))
        pool_steps.append(small2_pool)

        def small2_pe(e):
            got(e, "w_s2")
            for t in range(TT):
                for kt in range(KD):
                    for a in lhs:
                        mm = pe_.matmul(wk[0][:, t * 40:(t + 1) * 40], a[:, kt, t * P:(t + 1) * P].bitcast(F32),
                                        w_s2[:, kt * 40:(kt + 1) * 40], start=kt == 0 and a is h_hi,
                                        stop=kt == KD - 1 and a is h_lo)
            mm.then_inc(s2_mm, 1)
            got(e, "rel_c")
            got(e, "ohc")
            for t in range(TT):
                for n in range(N_CMP):
                    c = t * 120 + n * 8
                    mm = pe_.matmul(wk[1][:, c:c + 8], ohc[:, n * S + t * P:n * S + (t + 1) * P], rel_c,
                                    start=True, stop=True)
            mm.then_inc(s2_mm, 1)
            e.wait_ge(s2_g, 1)
            for t in range(TT):
                g = yv[:, t * 8:t * 8 + 8]
                pe_.matmul(wk[2][0:8, t * P:(t + 1) * P], g, tri[:, 0, 0:P], start=True, stop=True)
                pe_.matmul(wk[3][:, t * 8:t * 8 + 8], tri[:, 0, 0:P], g, start=True, stop=True)
                mm = pe_.matmul(wk[3][:, 16 + t * 8:24 + t * 8], ones[:], g, start=True, stop=True)
            mm.then_inc(s2_cum, 1)

        def small2_act(e):
            e.wait_ge(s2_mm, 1)
            act_.activation(srow2, wk[0][:, 0:80], ACT.Copy)
            e.drain()
            r = srow2.rearrange("p (t c) -> p t c", t=TT)
            act_.activation(gate3.rearrange("p (t c) -> p t c", t=TT), r[:, :, 0:24], ACT.Sigmoid)
            act_.activation(beta.rearrange("p (t c) -> p t c", t=TT), r[:, :, 32:40], ACT.Sigmoid).then_inc(s2_row, 1)
            got(e, "alog")
            act_.activation(alog, alog, ACT.Exp)
            e.wait_ge(s2_abs, 1)
            act_.activation(ya, ya, ACT.Exp)
            e.drain()
            act_.activation(ya, ya, ACT.Ln, bias=ones[:, 0:1]).then_inc(s2_ln, 1)
            e.wait_ge(s2_cum, 1)
            act_.activation(gtt[:, 0, :], wk[2][0:8, 0:S], ACT.Copy)
            act_.activation(gtt[:, 1, :], wk[2][0:8, 0:S], ACT.Copy, scale=-1.0)
            act_.activation(sm[:, 144:176], wk[3][:, 0:32], ACT.Copy)
            e.drain()
            act_.activation(expg, grow, ACT.Exp).then_inc(s2_cp, 1)
            e.wait_ge(s2_cp, 2)
            act_.activation(kdec_s, kdec_s, ACT.Exp)

        def small2_dve(e):
            e.wait_ge(s2_row, 1)
            got(e, "dtb")
            for t in range(TT):
                dve_.tensor_tensor(yv[:, t * 8:t * 8 + 8], srow2[:, t * 40 + 24:t * 40 + 32], dtb, ALU.add)
            e.drain()
            dve_.scalar_tensor_tensor(out=ya, in0=yv, scalar=-1.0, in1=yv, op0=ALU.mult, op1=ALU.min).then_inc(s2_abs, 1)
            e.drain()
            dve_.tensor_scalar(yv, yv, 0.0, None, ALU.max)
            e.drain()
            e.wait_ge(s2_ln, 1)
            dve_.tensor_tensor(yv, yv, ya, ALU.add)
            e.drain()
            for t in range(TT):
                ins = dve_.scalar_tensor_tensor(out=yv[:, t * 8:t * 8 + 8], in0=yv[:, t * 8:t * 8 + 8], scalar=-1.0,
                                                in1=alog, op0=ALU.mult, op1=ALU.mult)
            ins.then_inc(s2_g, 1)
            got(e, "mask_c")
            e.wait_ge(s2_mm, 2)
            for h in range(N_H):
                b = bias_c[:, h * 30:(h + 1) * 30].rearrange("p (t n) -> p t n", t=TT)
                ps = wk[1][:, 0:240].rearrange("p (t n h) -> p t n h", t=TT, h=8)[:, :, :, h]
                dve_.tensor_tensor(b, ps, mask_c.rearrange("p (t n) -> p t n", t=TT), ALU.add)
            e.wait_ge(s2_cp, 1)
            dve_.tensor_tensor(kdec_s, gend, grow, ALU.subtract).then_inc(s2_cp, 1)
        stages.append(Steps("small2", small2_pe, small2_act, small2_dve))

        stages.append(Steps("turn2", *to_tiles([
            ((lambda t, i=i: p2[:, t, i * P:(i + 1) * P]), tt2[:, i, :]) for i in range(16)])))
        after_turn2 = len(stages)

        def bias2(h):
            return p2[:, h // 4, (h % 4) * TOE:(h % 4 + 1) * TOE]
        pe_t = misc[:, 240:304].rearrange("p (k r) -> p k r", k=2)
        w2c = p2[:, 0, 4 * TOE:2048].rearrange("p (k a c) -> p k a c", k=2, a=2)
        hc = p2[0:30, 1, 4 * TOE:2048].rearrange("p (k c) -> p k c", k=2)
        h_t = misc[:, 304:424].rearrange("p (k a c) -> p k a c", k=2, a=2)
        kc_t = misc[:, 424:454]
        vc_r = misc[0:N_CMP, 512:768].rearrange("p (g c) -> p g c", g=2)

        def nsa_pool(e):
            load(e, "pe_t", pe_t, t_in["pe_t"], after=after_turn2)
            load(e, "w2c", w2c, t_in["w2c"])
            toeplitz(e, "bias2", bias2, toe2, N_H, after_turn2)
        pool_steps.append(nsa_pool)

        flat_hi = oa_hi[:].rearrange("p a b -> p (a b)")
        flat_lo = oa_lo[:].rearrange("p a b -> p (a b)")
        FW = 960
        f_sum, f_hi_s = sem("flat_sum"), sem("flat_hi")

        def flat_dve(e):
            got(e, "pe_t")
            dve_.memset(lp2[:, 0:4 * TOE], 0.0)
            e.drain()
            for k in range(2):
                if k:
                    e.wait_ge(f_hi_s, 2 * k)
                f = lp2[:, 0:FW].rearrange("p (r g n) -> p r g n", r=32, g=2)
                a = tt2[:, 8 + 2 * k:10 + 2 * k, :].rearrange("p g (n r) -> p r g n", r=CSTR)
                for hf in range(2):
                    pe4 = pe_t[:, k, hf * 16:(hf + 1) * 16].unsqueeze(2).unsqueeze(3).to_broadcast([P, 16, 2, N_CMP])
                    for g in range(2):
                        ins = dve_.tensor_tensor(f[:, hf * 16:(hf + 1) * 16, g, :], a[:, :, g, hf:hf + N_CMP],
                                                 pe4[:, :, g, :], ALU.add)
                ins.then_inc(f_sum, 1)
                e.wait_ge(f_hi_s, 2 * k + 1)
                dve_.tensor_tensor(flat_lo[:, k * FW:(k + 1) * FW], lp2[:, 0:FW],
                                   flat_hi[:, k * FW:(k + 1) * FW].bitcast(F32), ALU.subtract)
                e.drain()
                e.sem_inc(f_hi_s, 1)
            dve_.tensor_copy(flat_lo[:, 2 * FW:2048], lp2[:, 1100:1100 + 2048 - 2 * FW])

        def flat_act(e):
            for k in range(2):
                e.wait_ge(f_sum, k + 1)
                act_.activation(flat_hi[:, k * FW:(k + 1) * FW], lp2[:, 0:FW], ACT.Copy).then_inc(f_hi_s, 1)
            act_.activation(flat_hi[:, 2 * FW:2048], lp2[:, 1100:1100 + 2048 - 2 * FW], ACT.Copy)
        stages.append(Steps("flat", None, flat_act, flat_dve))

        class Compress(Gemm):

            def tile(self, a, kt, t):
                c = self.kt0 + kt * 30
                return a[:, c:c + P]

        for k, name in enumerate(("cmp_k", "cmp_v")):
            def ed(e, n, t, k=k):
                if t == 0:
                    e.sem_inc(evac[0], 1)
                else:
                    dve_.tensor_copy(hc[:, k, :], acc[1][0:30, 0:CHID]).then_inc(evac[1], 1)
            g = Compress(name, (flat_hi, flat_lo), k * FW, None, ed)
            g.tiles = range(1, 2)
            stages.append(g)
        c_act, c_tr, c_ht, c_mm = [sem(n) for n in ("cmp_gelu", "cmp_turned", "cmp_hidden", "cmp_out")]

        def cmp_act(e):
            act_.activation(hc, hc, ACT.Gelu_apprx_tanh).then_inc(c_act, 1)
            e.wait_ge(c_tr, 1)
            act_.activation(h_t.rearrange("p k a c -> p (k a c)"), wk[0][:, 0:120], ACT.Copy).then_inc(c_ht, 1)
            e.wait_ge(c_mm, 1)
            act_.activation(kc_t, wk[1][:, 0:30], ACT.Copy)
            act_.activation(vc_r, wk[2][0:N_CMP, 0:256].rearrange("p (g c) -> p g c", g=2), ACT.Copy)

        def cmp_pe(e):
            e.wait_ge(c_act, 1)
            for k in range(2):
                for a in range(2):
                    c = (2 * k + a) * 30
                    mm = pe_.matmul(wk[0][:, c:c + 30], hc[:, k, a * P:(a + 1) * P], ident[0:30, 0:30],
                                    start=True, stop=True, is_transpose=True)
            mm.then_inc(c_tr, 1)
            e.wait_ge(c_ht, 1)
            got(e, "w2c")
            for a in range(2):
                pe_.matmul(wk[1][:, 0:30], w2c[:, 0, a, :], h_t[:, 0, a, :], start=a == 0, stop=a == 1)
            for g in range(2):
                for a in range(2):
                    mm = pe_.matmul(wk[2][0:N_CMP, g * P:(g + 1) * P], h_t[:, 1, a, g * N_CMP:(g + 1) * N_CMP],
                                    w2c[:, 1, a, :], start=a == 0, stop=a == 1)
            mm.then_inc(c_mm, 1)
        stages.append(Steps("compress", cmp_pe, cmp_act, None))

        def branch(h, i):
            g = h // 4
            q = tt2[:, h, :]

            def gate(qt):
                return gate3[:, qt * 24 + h * 3 + i:qt * 24 + h * 3 + i + 1]
            kw = dict(gate=gate, first=i == 0, last=i == 2, hi=oa_hi[:, h, :], lo=oa_lo[:, h, :])
            if i == 0:
                return Unit(q, kc_t[:, g * N_CMP:(g + 1) * N_CMP], lambda kt: vc_r[:, g, :], [(0, [0]), (1, [0])],
                            N_D ** -0.5, bias_c[:, h * 30:(h + 1) * 30], kw=N_CMP, **kw)
            v = (P2_VS, P2_VW)[i - 1] + g * P
            return Unit(q, tt2[:, (12, 14)[i - 1] + g, :], lambda kt: p2[:, kt, v:v + P], CAUSAL, N_D ** -0.5,
                        bias2(h), **kw)

        def bias2_there(e):
            e.wait_ge(landed["bias2"], 16 * 2 * N_H)
        stages.append(attention("attention_nsa", [branch(h, i) for h in range(N_H) for i in range(3)], l2, pt2,
                                bias2_there))
        arn.close()

        arg = ExitStack()
        pg = sb("pg", [P, TT, 3072], F32, arg)
        argt = ExitStack()
        tg = sb("tg", [P, 24, S], F32, argt)
        wg = sb("wg", [P, 11, 512], F32, argt)
        cw2 = sb("cw2", [P, 24, 4], F32, argt)
        cmt = sb("cmt", [P, 2, P], F32, argt)
        wgf = wg[:].rearrange("p a b -> p (a b)")
        lmask2 = tg[:, 16:20, :].rearrange("p a b -> p (a b)").rearrange("p (l i) -> p l i", l=8)
        stages.append(Gemm("win2g", lhs, 0, *rows_to(pg)))
        before_conv = len(stages) - 1

        def conv_pool(e):
            load(e, "cw2", cw2[:], t_in["conv2"], after=before_conv)
            load(e, "cmt", cmt[:], t_in["cmt"])
        pool_steps.append(conv_pool)
        v_tr, v_first, v_done = sem("qkv_turned"), sem("conv_first"), sem("conv_all")

        def conv_pe(e):
            for i in range(24):
                if i >= 4:
                    e.wait_ge(v_done, i - 3)
                for t in range(TT):
                    mm = pe_.matmul(wk[i % 4][:, t * P:(t + 1) * P], pg[:, t, i * P:(i + 1) * P], ident[:],
                                    start=True, stop=True, is_transpose=True)
                mm.then_inc(v_tr, 1)

        def conv_act(e):
            got(e, "cw2")
            for i in range(24):
                e.wait_ge(v_tr, i + 1)
                act_.activation(tg[:, i, :], wk[i % 4][:, 0:S], ACT.Copy, scale=cw2[:, i, 3:4]).then_inc(v_first, 1)
            for k in range(4):
                e.wait_ge(v_done, 6 * k + 6)
                act_.activation(tg[:, 6 * k:6 * k + 6, :], tg[:, 6 * k:6 * k + 6, :], ACT.Silu)

        def conv_dve(e):
            got(e, "cw2")
            for i in range(0, 24, 2):
                for k in range(2):
                    e.wait_ge(v_first, i + k + 1)
                for d in range(1, 4):
                    for k in range(2):
                        a = tg[:, i + k, d:S]
                        ins = dve_.scalar_tensor_tensor(out=a, in0=wk[(i + k) % 4][:, 0:S - d],
                                                        scalar=cw2[:, i + k, 3 - d:4 - d], in1=a, op0=ALU.mult,
                                                        op1=ALU.add)
                        if d == 3:
                            ins.then_inc(v_done, 1)
                    if d < 3:
                        e.drain()
        stages.append(Steps("conv2", conv_pe, conv_act, conv_dve))
        stages.append(Steps("rows2", *to_tiles([
            ((lambda t, i=i: tg[:, i, t * P:(t + 1) * P]), pg[:, :, i * P:(i + 1) * P]) for i in range(24)])))

        n_sq, n_rt, n_qk = sem("qk_squared"), sem("qk_root"), sem("qk_unit")
        ssn, rtn = sm[:, 256:288], sm[:, 288:320]

        def heads_of(a, t, c0, n):
            return a[:, t, c0:c0 + n * P].rearrange("p (h c) -> p h c", c=P)

        def per_head(v, n):
            return v.unsqueeze(2).to_broadcast([P, n, P])

        def unit_act(e):
            for t in range(TT):
                act_.activation(wgf[:, t * 2048:(t + 1) * 2048], pg[:, t, 0:2048], ACT.Square).then_inc(n_sq, 1)
            e.wait_ge(n_rt, 1)
            act_.activation(ssn, ssn, ACT.Sqrt, bias=eps_c[:]).then_inc(n_rt, 1)

        def unit_dve(e):
            for t in range(TT):
                e.wait_ge(n_sq, t + 1)
                ins = dve_.tensor_reduce(ssn[:, t * 16:(t + 1) * 16],
                                         wgf[:, t * 2048:(t + 1) * 2048].rearrange("p (h c) -> p h c", c=P), AX.X,
                                         ALU.add)
            ins.then_inc(n_rt, 1)
            e.wait_ge(n_rt, 2)
            dve_.reciprocal(rtn, ssn)
            e.drain()
            for t in range(TT):
                dve_.tensor_scalar(rtn[:, t * 16:t * 16 + 8], rtn[:, t * 16:t * 16 + 8], G_D ** -0.5, None, ALU.mult)
            e.drain()
            for t in range(TT):
                a = heads_of(pg, t, 0, 16)
                dve_.tensor_tensor(a, a, per_head(rtn[:, t * 16:(t + 1) * 16], 16), ALU.mult)
                b = heads_of(pg, t, 2048, 8)
                dve_.tensor_tensor(b, b, per_head(beta[:, t * 8:t * 8 + 8], 8), ALU.mult)
        stages.append(Steps("unit2", None, unit_act, unit_dve))
        stages.append(Steps("turn_qk", *to_tiles([
            ((lambda t, i=i: pg[:, t, i * P:(i + 1) * P]), tg[:, i, :]) for i in range(16)])))
        before_rates = len(stages) - 1
        pool_steps.append(lambda e: load(e, "lmask2", lmask2, t_in["lmask"], after=before_rates))

        def rates_dve(e):
            be = sm[:, 320:336]
            dve_.tensor_tensor(be, beta, expg, ALU.mult)
            e.drain()
            for t in range(TT):
                dve_.tensor_tensor(heads_of(pg, t, 0, 8), heads_of(pg, t, 1024, 8),
                                   per_head(be[:, t * 8:t * 8 + 8], 8), ALU.mult)
            e.drain()
            k0 = heads_of(pg, 0, 1024, 8)
            dve_.tensor_tensor(k0, k0, per_head(kdec_s[:, 0:8], 8), ALU.mult)
            got(e, "lmask2")
            got(e, "cmt")
        stages.append(Steps("rates", None, None, rates_dve))

        NL = 7
        d_e, d_m, d_x, d_l, d_lt, d_ltc, d_qk, d_c, d_M, d_Mc, d_T, d_Tc, d_at = [sem("delta_" + n) for n in (
            "exponents", "masked", "decays", "gram_scaled", "l_turned", "l_copied", "scores", "level", "m",
            "m_copied", "t", "t_copied", "scores_done")]

        def w4(i):
            return wg[:, i, :].rearrange("p (h c) -> p h c", h=4)
        LT, TM, TR, MM, CT = [[w4(2 * i), w4(2 * i + 1)] for i in range(5)]
        DD = w4(10)
        at_f = tg[:, 20:24, :].rearrange("p a b -> p (a b)")
        AT = [at_f[:, t * 512:(t + 1) * 512].rearrange("p (h c) -> p h c", h=4) for t in range(2)]
        bank4 = [b[:].rearrange("p (h c) -> p h c", h=4) for b in wk]

        def q_t(h, t):
            return tg[:, h, t * P:(t + 1) * P]

        def k_t(h, t):
            return tg[:, 8 + h, t * P:(t + 1) * P]

        def delta(b):
            hs = range(4 * b, 4 * b + 4)
            z4, z2, zl = 4 * b, 2 * b, 2 * NL * b

            def pe(e):
                for t in range(TT):
                    for o in range(2):
                        for j, h in enumerate(hs):
                            one = ident[0:8, h:h + 1].to_broadcast([8, P])
                            gc, gn = gtt[:, 0, t * P:(t + 1) * P], gtt[:, 1, t * P:(t + 1) * P]
                            bb = bank4[2 * t + o][:, j, :]
                            pe_.matmul(bb, *((one, gc) if o == 0 else (gc, one)), start=True, stop=False)
                            mm = pe_.matmul(bb, *((gn, one) if o == 0 else (one, gn)), start=False, stop=True)
                        mm.then_inc(d_e, 1)
                for t in range(TT):
                    for o in range(2):
                        if o == 0:
                            bk = bank4[4]
                            if t:
                                e.wait_ge(d_at, z2 + t)
                        else:
                            bk = bank4[5]
                            if t:
                                e.wait_ge(d_l, z2 + t)
                        for j, h in enumerate(hs):
                            mm = pe_.matmul(bk[:, j, :], k_t(h, t), (q_t, k_t)[o](h, t), start=True, stop=True)
                        mm.then_inc(d_qk, 1)
                for t in range(TT):
                    e.wait_ge(d_l, z2 + t + 1)
                    for j in range(4):
                        mm = pe_.matmul(bank4[2 * t][:, j, :], LT[t][:, j, :], ident[:], start=True, stop=True,
                                        is_transpose=True)
                    mm.then_inc(d_lt, 1)
                for l in range(NL):
                    for t in range(TT):
                        e.wait_ge(d_c, zl + 2 * l + t + 1)
                        if l:
                            e.wait_ge(d_Tc, zl + 2 * (l - 1) + t + 1)
                        for j in range(4):
                            mm = pe_.matmul(bank4[t][:, j, :], CT[t][:, j, :], TM[t][:, j, :], start=True, stop=True)
                        mm.then_inc(d_M, 1)
                    for t in range(TT):
                        e.wait_ge(d_Mc, zl + 2 * l + t + 1)
                        if l < NL - 1:
                            for j in range(4):
                                pe_.matmul(bank4[2 + t][:, j, :], TR[t][:, j, :], MM[t][:, j, :], start=True, stop=True)
                        for j in range(4):
                            mm = pe_.matmul(bank4[4 + t][:, j, :], MM[t][:, j, :], TR[t][:, j, :], start=True, stop=True)
                        mm.then_inc(d_T, 1)

            def act(e):
                for t in range(TT):
                    for o in range(2):
                        e.wait_ge(d_m, z4 + 2 * t + o + 1)
                        a = AT[t] if o == 0 else LT[t]
                        act_.activation(a, a, ACT.Exp).then_inc(d_x, 1)
                for t in range(TT):
                    e.wait_ge(d_lt, z2 + t + 1)
                    act_.activation(LT[t], bank4[2 * t], ACT.Copy).then_inc(d_ltc, 1)
                for l in range(NL):
                    for t in range(TT):
                        e.wait_ge(d_M, zl + 2 * l + t + 1)
                        act_.activation(MM[t], bank4[t], ACT.Copy).then_inc(d_Mc, 1)

            def dve(e):
                for t in range(TT):
                    for o in range(2):
                        e.wait_ge(d_e, z4 + 2 * t + o + 1)
                        dve_.tensor_tensor(AT[t] if o == 0 else LT[t], bank4[2 * t + o], bc(cmt[:, o, :], 4),
                                           ALU.add).then_inc(d_m, 1)
                for t in range(TT):
                    dve_.tensor_copy(TM[t], bc(ident[:], 4))
                    dve_.tensor_copy(TR[t], bc(ident[:], 4))
                for t in range(TT):
                    e.wait_ge(d_qk, z4 + 2 * t + 2)
                    e.wait_ge(d_x, z4 + 2 * t + 2)
                    dve_.tensor_tensor(AT[t], bank4[4], AT[t], ALU.mult).then_inc(d_at, 1)
                    for j, h in enumerate(hs):
                        ins = dve_.scalar_tensor_tensor(out=LT[t][:, j, :], in0=bank4[5][:, j, :],
                                                        scalar=beta[:, t * 8 + h:t * 8 + h + 1], in1=LT[t][:, j, :],
                                                        op0=ALU.mult, op1=ALU.mult)
                    ins.then_inc(d_l, 1)

                def level(l, t):
                    if l:
                        e.wait_ge(d_M, zl + 2 * (l - 1) + t + 1)
                    dve_.tensor_tensor(CT[t], LT[t], bc(lmask2[:, l, :], 4), ALU.mult).then_inc(d_c, 1)
                for t in range(TT):
                    e.wait_ge(d_ltc, z2 + t + 1)
                    level(0, t)
                for l in range(NL):
                    for t in range(TT):
                        if l < NL - 1:
                            level(l + 1, t)
                    for t in range(TT):
                        e.wait_ge(d_T, zl + 2 * l + t + 1)
                        if l < NL - 1:
                            dve_.tensor_tensor(TM[t], TM[t], bank4[2 + t], ALU.subtract)
                        dve_.tensor_tensor(TR[t], TR[t], bank4[4 + t], ALU.subtract).then_inc(d_Tc, 1)
            return Steps(f"delta{b}", pe, act, dve)

        y_u0, y_u0c, y_s1, y_s1c, y_w, y_wc, y_v1, y_v1c, y_o = [sem("state_" + n) for n in (
            "u", "u_copied", "sum", "sum_copied", "w", "w_copied", "v", "v_copied", "out")]

        def state(b):
            hs = list(enumerate(range(4 * b, 4 * b + 4)))
            V0, V1, S1, WT = MM[0], MM[1], LT[0], TM[0]

            def rows_(c0, h, t):
                return pg[:, t, c0 + h * P:c0 + (h + 1) * P]

            def pe(e):
                for j, h in hs:
                    mm = pe_.matmul(bank4[0][:, j, :], TR[0][:, j, :], rows_(2048, h, 0), start=True, stop=True)
                mm.then_inc(y_u0, 1)
                for j, h in hs:
                    mm = pe_.matmul(bank4[1][:, j, :], rows_(0, h, 1), TR[1][:, j, :], start=True, stop=True)
                mm.then_inc(y_w, 1)
                e.wait_ge(y_u0c, b + 1)
                for j, h in hs:
                    mm = pe_.matmul(bank4[2][:, j, :], rows_(1024, h, 0), V0[:, j, :], start=True, stop=True)
                mm.then_inc(y_s1, 1)
                for j, h in hs:
                    pe_.matmul(bank4[3][:, j, :], AT[0][:, j, :], V0[:, j, :], start=True, stop=True)
                e.wait_ge(y_wc, b + 1)
                e.wait_ge(y_s1c, b + 1)
                for j, h in hs:
                    pe_.matmul(bank4[4][:, j, :], TR[1][:, j, :], rows_(2048, h, 1), start=True, stop=False)
                    mm = pe_.matmul(bank4[4][:, j, :], WT[:, j, :], S1[:, j, :], start=False, stop=True)
                mm.then_inc(y_v1, 1)
                for j, h in hs:
                    pe_.matmul(bank4[5][:, j, :], q_t(h, 1), S1[:, j, :], start=True, stop=True)
                e.wait_ge(y_v1c, b + 1)
                for j, h in hs:
                    mm = pe_.matmul(bank4[0][:, j, :], AT[1][:, j, :], V1[:, j, :], start=True, stop=True)
                mm.then_inc(y_o, 1)

            def act(e):
                e.wait_ge(y_u0, b + 1)
                act_.activation(V0, bank4[0], ACT.Copy).then_inc(y_u0c, 1)
                e.wait_ge(y_s1, b + 1)
                act_.activation(S1, bank4[2], ACT.Copy).then_inc(y_s1c, 1)
                e.wait_ge(y_v1, b + 1)
                act_.activation(V1, bank4[4], ACT.Copy).then_inc(y_v1c, 1)
                e.wait_ge(y_o, 2 * b + 1)
                act_.activation(heads_of(pg, 0, 2048 + 512 * b, 4), bank4[3], ACT.Copy)
                act_.activation(heads_of(pg, 1, 2048 + 512 * b, 4), bank4[0], ACT.Copy).then_inc(y_o, 1)

            def dve(e):
                e.wait_ge(y_w, b + 1)
                dve_.tensor_scalar(WT, bank4[1], -1.0, None, ALU.mult).then_inc(y_wc, 1)
                e.wait_ge(y_o, 2 * b + 2)
                for j, h in hs:
                    o = pg[:, 1, 2048 + h * P:2048 + (h + 1) * P]
                    dve_.scalar_tensor_tensor(out=o, in0=bank4[5][:, j, :], scalar=expg[:, 8 + h:9 + h], in1=o,
                                              op0=ALU.mult, op1=ALU.add)
            return Steps(f"state{b}", pe, act, dve)
        for b in range(2):
            stages.append(delta(b))
            stages.append(state(b))
        argt.close()

        ob_hi = sb("ob_hi", [P, 8, S], F32R, arg)
        ob_lo = sb("ob_lo", [P, 8, S], F32R, arg)
        gm = sb("gm", [P, TT, 2 * D], F32, arg)
        stages.append(Gemm("z", lhs, 0, *rows_to(pg)))
        gn_bc = gm[:, 0, 2048:2048 + P]
        before_gn = len(stages) - 1
        pool_steps.append(lambda e: load(e, "gn", gn_bc, t_in["gdn_norm"].to_broadcast([P, P]), after=before_gn))
        o_sq, o_rt = sem("delta_squared"), sem("delta_root")
        sso, rto = sm[:, 336:352], sm[:, 352:368]

        def gnorm_act(e):
            for t in range(TT):
                act_.activation(gm[:, t, 0:1024], pg[:, t, 2048:3072], ACT.Square).then_inc(o_sq, 1)
            act_.activation(pg[:, :, 0:1024], pg[:, :, 0:1024], ACT.Silu)
            e.wait_ge(o_rt, 1)
            act_.activation(sso, sso, ACT.Sqrt, scale=1.0 / G_D, bias=eps_c[:]).then_inc(o_rt, 1)

        def gnorm_dve(e):
            got(e, "gn")
            for t in range(TT):
                e.wait_ge(o_sq, t + 1)
                ins = dve_.tensor_reduce(sso[:, t * 8:(t + 1) * 8], heads_of(gm, t, 0, 8), AX.X, ALU.add)
            ins.then_inc(o_rt, 1)
            e.wait_ge(o_rt, 2)
            dve_.reciprocal(rto, sso)
            for t in range(TT):
                z = heads_of(pg, t, 0, 8)
                dve_.tensor_tensor(z, z, bc(gn_bc, 8), ALU.mult)
            e.drain()
            for t in range(TT):
                o = heads_of(pg, t, 2048, 8)
                dve_.tensor_tensor(o, o, per_head(rto[:, t * 8:(t + 1) * 8], 8), ALU.mult)
            e.drain()
            for t in range(TT):
                o = heads_of(pg, t, 2048, 8)
                dve_.tensor_tensor(o, o, heads_of(pg, t, 0, 8), ALU.mult)
        stages.append(Steps("gnorm", None, gnorm_act, gnorm_dve))
        stages.append(Steps("turn_ob", *to_lhs(lambda t, i: pg[:, t, 2048 + i * P:2048 + (i + 1) * P], 8, ob_hi, ob_lo)))

        stages.append(Gemm("merge", lhs, 0, *rows_to(gm)))
        stages.append(Steps("merge_gates", None, lambda e: act_.activation(gm[:], gm[:], ACT.Sigmoid), None))

        def pa_ed(e, n, t):
            g = gm[:, t, n * CH:(n + 1) * CH]
            dve_.tensor_tensor(g, acc[t][:], g, ALU.mult).then_inc(evac[t], 1)

        def pb_ed(e, n, t):
            g, a = gm[:, t, D + n * CH:D + (n + 1) * CH], gm[:, t, n * CH:(n + 1) * CH]
            dve_.tensor_tensor(g, acc[t][:], g, ALU.mult).then_inc(evac[t], 1)
            e.drain()
            dve_.tensor_tensor(a, a, g, ALU.add)
        stages.append(Gemm("pa", (oa_hi, oa_lo), 0, None, pa_ed))
        stages.append(Gemm("pb", (ob_hi, ob_lo), 0, None, pb_ed))
        stages.append(Steps("turn_m", *to_lhs(lambda t, i: gm[:, t, i * P:(i + 1) * P], KD, h_hi, h_lo)))
        stages.append(Gemm("wo", lhs, 0, *add_to_x()))
        stages.append(norm_to_lhs("norm_ln2", x, gm[:, :, 0:D], h_hi, h_lo, gains[:, 5, :]))
        arg.close()
        ar2.close()

        before_f2 = len(stages)
        arf = ExitStack()
        f_hi = sb("f2_hi", [P, 32, S], F32R, arf)
        f_lo = sb("f2_lo", [P, 32, S], F32R, arf)
        stg = sb("stg2", [P, TT, CH], F32, arf)
        sq = sb("sq2", [P, 4, S], F32, arf)
        flhs = (f_hi, f_lo)
        for half_ in ("a", "b"):
            up("up2_" + half_, "square", 0, 0, 4, ACT.Relu)
            stages.append(Gemm("down2_" + half_, flhs, 0, *add_to_x()))
        fin = ExitStack()
        row_f = sb("row_f", [P, D], F32, fin)
        gain_f = sb("gain_f", [P, D], F32, fin)
        pool_steps.append(lambda e: load(e, "norm_out", gain_f[:], t_in["ln_f"].to_broadcast([P, D]),
                                         after=before_f2))
        stages.append(norm_times("norm_out", row_f[:], gain_f[:]))
        OUT = x[:]
        fin.close()
        arf.close()

        out_done = sem("out_done")
        block = ctx.enter_context(nc.Block())

        @block.sync
        def _(e):
            for g in Gemm.every:
                g.load(e)

        @block.gpsimd
        def _(e):
            for f in pool_steps:
                f(e)
            for k in at_end:
                e.wait_ge(at_end[k], len(stages))
            e.dma_start(out, OUT).then_inc(out_done, 16)
            e.wait_ge(out_done, 16)

        def program(e, k):
            for i, s in enumerate(stages):
                s.run(k, e)
                stage_end(e, k, i)

        @block.tensor
        def _(e):
            program(e, "pe")

        @block.scalar
        def _(e):
            program(e, "act")

        @block.vector
        def _(e):
            program(e, "dve")


def layout(i):
    f = np.float32
    a = {}

    def cols(w, order):
        return np.concatenate([w[:, s:s + n] for s, n in order], axis=1)

    def weights(name, w):
        _, n, kts, width = {s[0]: s for s in gemm_specs()}[name]
        K = sum(kts)
        assert w.shape == (K * P, n * width), (name, w.shape)
        t = w.reshape(K, P, n, width).transpose(2, 1, 0, 3)
        o = np.zeros((n, len(kts), P, ITEM), f)
        k0 = 0
        for j, k in enumerate(kts):
            o[:, j, :, 0:k * width] = t[:, :, k0:k0 + k].reshape(n, P, k * width)
            k0 += k
        a["w_" + name] = o.reshape(n * len(kts), P, ITEM)

    def rows(m):
        return np.ascontiguousarray(m.reshape(TT, P, -1).transpose(1, 0, 2))

    def lanes(v):
        return np.ascontiguousarray(v.reshape(-1, P).T)

    w = i["w_in"][0]
    o = np.cumsum([0, 768, 768, 768, 512, 512, 512, 8, 384, 384, 768, 768, 16])
    qa, ka, va, qb, kb, vb, fl, qc, kc, vc, rc, gl = o[:12].tolist()
    weights("win", cols(w, [(qa, 768), (ka, 768), (qb, 512), (kb, 512), (va, 768), (vb, 512), (qc, 384), (kc, 384),
                            (vc, 768), (rc, 768)]))
    a["w_small1"] = cols(w, [(fl, 8), (gl, 16)]).reshape(KD, P, 24).transpose(1, 0, 2).reshape(P, KD * 24).copy()
    weights("wout", i["w_out"][0])
    weights("ckv", i["w_ckv"][0])
    weights("cq", i["w_cq"][0])
    weights("co", i["w_co"][0])
    up, dn = i["w_up"][0], i["w_down"][0]

    def pairs(c0, n, tiles):
        return cols(up, [s for c in range(n) for s in ((P * (c0 + c * tiles), P * tiles),
                                                       (FF1 + P * (c0 + c * tiles), P * tiles))])
    weights("up_a", pairs(0, 11, 2))
    weights("up_b", pairs(22, 10, 2))
    weights("up_t", pairs(42, 1, 1))
    weights("down_a", dn[0:22 * P])
    weights("down_b", dn[22 * P:])
    a["x"] = rows(i["x"][0])
    a["mem"] = rows(i["mem"][0])
    a["gains"] = np.stack([lanes(i["norm_mix"][0]), lanes(i["mem_norm"]), lanes(i["norm_cross"][0]),
                           lanes(i["norm_ffn"][0]), lanes(i["ln1_w_2"][0]),
                           lanes(i["ln2_w_2"][0])], axis=1).copy()
    a["c_gate_w2"] = i["c_gate_w2"][0]
    a["c_gate_b"] = i["c_gate_b"]
    a["f_bias"] = i["f_bias"]
    a["c_norm"] = i["c_norm"]
    a["conv1"] = np.stack([lanes(i["conv_w"][0][0]), lanes(i["conv_w"][0][1]), lanes(i["conv_w"][0][2]),
                           lanes(i["conv_b"][0])], axis=2).copy()
    a["rel0"] = i["rel_table"]
    a["rel1"] = i["rel_table_2"]
    a["ident"] = np.eye(P, dtype=f)
    tok = np.arange(S)
    a["tri"] = rows((tok[:, None] <= tok[None, :]).astype(f))
    d = 255 - np.arange(TOE)

    def bucket(dist, far):
        n = np.maximum(dist, 1).astype(f)
        large = 16 + (np.log(n / 16) / np.float32(np.log(far / 16)) * 16).astype(np.int32)
        return np.where(dist < 16, np.maximum(dist, 0), np.minimum(large, 31))
    count = (d <= 128) * 1 + (d % 4 == 0) * 1 + (d % 16 == 0) * 1
    ok = (d >= 0) & (count > 0)
    hot = ((np.arange(REL)[:, None] == bucket(d, 2048.0)[None]) & ok[None]).astype(f)
    a["onehot0"] = hot
    a["toe_add0"] = np.broadcast_to(np.where(ok, np.log(np.maximum(count, 1)), NEG).astype(f), (A_H, TOE)).copy()
    a["onehot1"] = ((np.arange(REL)[:, None] == bucket(d, 128.0)[None]) & (d >= 0)[None]).astype(f)
    a["toe_add1"] = np.broadcast_to(np.where(d >= 0, 0.0, NEG).astype(f), (N_H, TOE)).copy()
    p = np.arange(P)
    a["cmask"] = np.concatenate([np.where(p[None, :] <= p[:, None], 0.0, NEG),
                                 np.where(tok[None, :] <= (P + p)[:, None], 0.0, NEG)], axis=1).astype(f)
    lm = np.zeros((P, 8, P), f)
    for l in range(7):
        s = 1 << l
        same = p[:, None] // (2 * s) == p[None, :] // (2 * s)
        lm[:, l, :] = same & (p[:, None] // s % 2 == 0) & (p[None, :] // s % 2 == 1)
    a["lmask"] = lm

    w = i["w_in_2"][0]
    o = np.cumsum([0, 1024, 256, 256, 256, 256, 256, 256, 24, 3072, 1024, 8, 8]).tolist()
    q, kc, vc, ks, vs, kw, vw, ng, qkv, z, ga, gb = o[:12]
    mg = o[12]
    weights("win2", cols(w, [(q, 1024), (kc, 256), (vc, 256), (ks, 256), (kw, 256), (vs, 256), (vw, 256)]))
    weights("win2g", cols(w, [(qkv, 3072)]))
    weights("z", cols(w, [(z, 1024)]))
    weights("merge", cols(w, [(mg, 2 * D)]))
    a["w_small2"] = cols(w, [(ng, 24), (ga, 8), (gb, 8)]).reshape(KD, P, 40).transpose(1, 0, 2).reshape(P, KD * 40).copy()
    weights("cmp_k", i["cmp_w1_k_2"][0])
    weights("cmp_v", i["cmp_w1_v_2"][0])
    weights("pa", i["w_pa_2"][0])
    weights("pb", i["w_pb_2"][0])
    weights("wo", i["w_o_2"][0])
    weights("up2_a", i["w_up_2"][0][:, 0:FF2 // 2])
    weights("up2_b", i["w_up_2"][0][:, FF2 // 2:])
    weights("down2_a", i["w_down_2"][0][0:FF2 // 2])
    weights("down2_b", i["w_down_2"][0][FF2 // 2:])
    a["pe_t"] = np.stack([i["cmp_pe_k_2"][0].T, i["cmp_pe_v_2"][0].T], axis=1).copy()
    a["w2c"] = np.stack([i[n][0].reshape(2, P, P).transpose(1, 0, 2) for n in ("cmp_w2_k_2", "cmp_w2_v_2")], axis=1).copy()
    a["conv2"] = np.stack([lanes(i["conv_w_2"][0][k]) for k in range(4)], axis=2).copy()
    a["a_log"] = i["a_log_2"]
    a["dt_bias"] = i["dt_bias_2"]
    a["gdn_norm"] = i["gdn_norm_w_2"]
    a["norm_final"] = i["norm_final"][None]
    a["ln_f"] = i["ln_f_w_2"][None]
    end = np.arange(N_CMP) * CSTR + CB - 1
    dc = tok[None, :] - end[:, None]
    a["onehot_c"] = ((np.arange(REL)[:, None, None] == bucket(dc, 128.0)[None]) & (dc >= 0)[None]).astype(f).reshape(
        REL, N_CMP * S)
    a["mask_c"] = rows(np.where(dc.T >= 0, 0.0, NEG).astype(f)).reshape(P, TT * N_CMP)
    a["cmt"] = np.stack([np.where(p[None, :] >= p[:, None], 0.0, NEG), np.where(p[None, :] < p[:, None], 0.0, NEG)],
                        axis=1).astype(f)
    return a


def kernel(**inputs):
    import concourse.bacc as bacc
    from concourse.bass_utils import run_bass_kernel_spmd

    arrays = {k: np.ascontiguousarray(v) for k, v in layout({k: np.asarray(v) for k, v in inputs.items()}).items()}
    nc = bacc.Bacc("TRN2", target_bir_lowering=False, num_devices=1)
    t_in = {k: nc.dram_tensor("in_" + k, v.shape, F32, kind="ExternalInput").ap() for k, v in arrays.items()}
    out = nc.dram_tensor("result", (P, TT, D), F32, kind="ExternalOutput").ap()
    build(nc, t_in, out)
    r = run_bass_kernel_spmd(nc, [{"in_" + k: v for k, v in arrays.items()}], core_ids=[0])
    return r.results[0]["result"].transpose(1, 0, 2).reshape(1, S, D)
```

```python
import numpy as np
from contextlib import ExitStack

import concourse.bass as bass
from concourse import mybir

F32 = mybir.dt.float32
F32R = mybir.dt.float32r
ACT = mybir.ActivationFunctionType
ALU = mybir.AluOpType
AX = mybir.AxisListType

P = 128
S = 256
TT = S // P
D = 2048
KD = D // P
EPS = 1e-6
NEG = -1e30
FLOOR = 1e20
CH = 512
ITEM = 2048
RAW = 4
SPL = 2

A_W, A_H, A_D = 768, 12, 64
B_W, B_H = 512, 8
C_H, C_DK, C_DV = 4, 96, 192
C_KW, C_VW, C_R = 384, 768, 16
X_H, X_D = 4, 128
FF1 = 5504
KF1 = FF1 // P
P1_QA, P1_KA, P1_QB, P1_KB = 0, 768, 1536, 2048
P1_VA, P1_VB, P1_QC, P1_KC, P1_VC, P1_RC = 2560, 3328, 3840, 4224, 4608, 5376
P1_N = 6144
N_H, N_G, N_D = 8, 2, 128
N_CMP, CB, CSTR, CHID = 15, 32, 16, 256
G_H, G_D = 8, 128
FF2 = 8192
P2_Q, P2_KC, P2_VC, P2_KS, P2_KW, P2_VS, P2_VW = 0, 1024, 1280, 1536, 1792, 2048, 2304
P2_N = 2560
REL = 32
TOE = 384

CAUSAL = [(0, [0]), (1, [0, 1])]
FULL = [(0, [0, 1]), (1, [0, 1])]


def split_counts(total, items):
    return [total // items + (i < total % items) for i in range(items)]


def gemm_specs():
    four = [4] * 4
    return [
        ("ckv", 2, four, CH), ("win", 8, four, CH), ("winc", 4, four, CH), ("wout", 4, four, CH), ("cq", 1, four, CH),
        ("co", 4, [4], CH),
        ("up_a", 11, four, CH), ("down_a", 4, split_counts(22, 8), CH),
        ("up_b", 10, four, CH), ("up_t", 1, four, CH // 2), ("down_b", 4, split_counts(21, 8), CH),
        ("win2", 5, four, CH), ("cmp_k", 1, split_counts(32, 8), CHID), ("cmp_v", 1, split_counts(32, 8), CHID),
        ("win2g", 6, four, CH), ("z", 2, four, CH),
        ("merge", 8, four, CH), ("pa", 4, [4] * 2, CH), ("pb", 4, [4] * 2, CH), ("wo", 4, four, CH),
        ("up2_a", 8, four, CH), ("down2_a", 4, [4] * 8, CH), ("up2_b", 8, four, CH), ("down2_b", 4, [4] * 8, CH),
    ]


def build(nc, t_in, out):
    ctx = ExitStack()
    with ctx:
        def sb(name, shape, dt=F32, c=ctx):
            return c.enter_context(nc.sbuf_tensor(name, shape, dt))

        def sem(name):
            return ctx.enter_context(nc.semaphore(name))

        pe_, act_, dve_ = nc.tensor, nc.scalar, nc.vector

        w_raw = sb("w_raw", [P, RAW, ITEM])
        w_hi = sb("w_hi", [P, SPL, ITEM], F32R)
        w_lo = sb("w_lo", [P, SPL, ITEM], F32R)
        x = sb("x", [P, TT, D])
        h_hi = sb("h_hi", [P, KD, S], F32R)
        h_lo = sb("h_lo", [P, KD, S], F32R)
        ident = sb("ident", [P, P])
        tri = sb("tri", [P, TT, S])
        gains = sb("gains", [P, 6, KD])
        st = sb("st", [P, 128])
        ones = sb("ones", [P, P])
        eps_c = sb("eps_c", [P, 1])
        acc = [ctx.enter_context(nc.psum_tensor(f"acc{i}", [P, 512], F32)) for i in range(2)]
        wk = [ctx.enter_context(nc.psum_tensor(f"wk{i}", [P, 512], F32)) for i in range(6)]
        toe1 = nc.dram_tensor("toe1_scratch", (A_H, P, TOE), F32, kind="Internal").ap()
        toe2 = nc.dram_tensor("toe2_scratch", (N_H, P, TOE), F32, kind="Internal").ap()

        raw_ready = [sem(f"raw_ready{i}") for i in range(RAW)]
        hi_ready = sem("hi_ready")
        lo_ready = sem("lo_ready")
        item_done = sem("item_done")
        tile0_done = sem("tile0_done")
        evac = [sem("evac0"), sem("evac1")]
        at_end = {k: sem(f"{k}_stage") for k in ("pe", "act", "dve")}
        landed = {}

        stages = []

        class Gemm:

            base_item = 0
            base_chunk = 0
            every = []
            unmet = False

            def __init__(self, name, lhs, kt0=0, evac_act=None, evac_dve=None, epi=None):
                spec = {s[0]: s for s in gemm_specs()}[name]
                _, self.n, self.kts, self.width = spec
                self.name, self.lhs, self.kt0 = name, lhs, kt0
                self.w = t_in["w_" + name]
                self.ipc = len(self.kts)
                self.b, self.c = Gemm.base_item, Gemm.base_chunk
                Gemm.base_item += self.n * self.ipc
                Gemm.base_chunk += self.n
                assert self.b % RAW == 0 and (self.n * self.ipc) % RAW == 0
                self.loop = self.n > 1 and self.ipc % RAW == 0
                self.ea, self.ed, self.epi = evac_act, evac_dve, epi
                self.tiles = range(TT)
                self.after_first = {}
                self.hidden_from = None
                self.needs = None
                self.lhs_from = None
                Gemm.every.append(self)

            def chunks(self, e, body):
                body(0, True)
                if self.loop:
                    with e.Fori(1, self.n) as n:
                        body(n, False)
                else:
                    for n in range(1, self.n):
                        body(n, False)

            def cols(self, j):
                return self.kts[j] * self.width

            def load(self, e):
                def body(n, first):
                    for j in range(self.ipc):
                        i = self.b + n * self.ipc + j
                        if not (first and self.b + j < RAW):
                            e.wait_ge(lo_ready, i - RAW + 1)
                        e.dma_start(w_raw[:, (self.slot(n, j)) % RAW, 0:self.cols(j)],
                                    self.w[bass.ds(n * self.ipc + j, 1), :, 0:self.cols(j)].rearrange(
                                        "a p f -> p (a f)")).then_inc(raw_ready[self.slot(n, j) % RAW], 16)
                self.chunks(e, body)

            def slot(self, n, j):
                return j if self.loop else n * self.ipc + j

            def count(self, n, j):
                if self.loop or isinstance(n, int):
                    return (self.b + (n * self.ipc if isinstance(n, int) else 0) + j) // RAW + 1 + (
                        0 if isinstance(n, int) else n * (self.ipc // RAW))

            def make_hi(self, e, n, j):
                i, s, k = self.b + n * self.ipc + j, self.slot(n, j), self.cols(j)
                e.wait_ge(raw_ready[s % RAW], self.count(n, j) * 16)
                if not (isinstance(n, int) and i < SPL):
                    e.wait_ge(item_done, i - SPL + 1)
                act_.activation(w_hi[:, s % SPL, 0:k], w_raw[:, s % RAW, 0:k], ACT.Copy).then_inc(hi_ready, 1)

            def make_lo(self, e, n, j):
                i, s, k = self.b + n * self.ipc + j, self.slot(n, j), self.cols(j)
                e.wait_ge(hi_ready, i + 1)
                dve_.tensor_tensor(w_lo[:, s % SPL, 0:k], w_raw[:, s % RAW, 0:k],
                                   w_hi[:, s % SPL, 0:k].bitcast(F32), ALU.subtract).then_inc(lo_ready, 1)

            def split(self, e, make, evacuate, epilogue):
                at = Gemm.every.index(self)

                def body(n, first):
                    for j in range(self.ipc):
                        if not (first and j == 0):
                            make(self, e, n, j)
                        if j == 0 and not first:
                            evacuate(e, n - 1)
                        if first and j == 2 and self.needs:
                            got(e, self.needs)
                            if make is Gemm.make_hi:
                                act_.activation(st[:, 8:9], st[:, 2:3], ACT.Silu)
                        if self.epi and j >= 2 and not first:
                            epilogue(e, n - 1, j - 2)
                    if first and make is Gemm.make_lo and "dve" in self.after_first:
                        self.after_first["dve"](e)
                self.chunks(e, body)
                if self is not Gemm.every[-1]:
                    make(Gemm.every[at + 1], e, 0, 0)
                evacuate(e, self.n - 1)
                if self.epi:
                    epilogue(e, self.n - 1, 0)
                    epilogue(e, self.n - 1, 1)

            both_act = False

            def out_act(self, e, n):
                if self.both_act:
                    e.wait_ge(tile0_done, self.c + n + 1)
                    self.ea(e, n, 0)
                    e.wait_ge(item_done, self.b + (n + 1) * self.ipc)
                    self.ea(e, n, 1)
                elif self.ea:
                    e.wait_ge(tile0_done, self.c + n + 1)
                    self.ea(e, n)

            def out_dve(self, e, n):
                if self.both_act:
                    return
                if not self.ea:
                    e.wait_ge(tile0_done, self.c + n + 1)
                    self.ed(e, n, 0)
                e.wait_ge(item_done, self.b + (n + 1) * self.ipc)
                self.ed(e, n, 1)

            def act(self, e):
                self.split(e, Gemm.make_hi, self.out_act, lambda e, n, part: self.epi.act(e, n, part))

            def dve(self, e):
                self.split(e, Gemm.make_lo, self.out_dve, lambda e, n, part: self.epi.dve(e, n, part))

            def pe_item(self, e, n, j, first):
                hi, lo = self.lhs
                last = self.ipc - 1
                K = sum(self.kts)
                w = self.width
                s = self.slot(n, j) % SPL
                e.wait_ge(lo_ready, self.b + n * self.ipc + j + 1)
                if first and self.lhs_from is not None:
                    base, kt0 = self.lhs_from
                    pairs = (sum(self.kts[:j + 1]) - kt0 + 1) // 2
                    if pairs > 0:
                        e.wait_ge(turned_lo, base + pairs)
                if first and self.hidden_from is not None:
                    base, tiles = self.hidden_from
                    e.wait_ge(ep_lo, base - (-sum(self.kts[:j + 1]) // tiles))
                for t in self.tiles:
                    if j == 0 and not (first and self.c == 0):
                        e.wait_ge(evac[t], self.c + n)
                    for k in range(self.kts[j]):
                        kt = sum(self.kts[:j]) + k
                        wh = w_hi[:, s, k * w:(k + 1) * w]
                        wl = w_lo[:, s, k * w:(k + 1) * w]
                        xh, xl = self.tile(hi, kt, t), self.tile(lo, kt, t)
                        o = acc[t][:, 0:w]
                        pe_.matmul(o, xh, wh, start=kt == 0, stop=False)
                        pe_.matmul(o, xh, wl, start=False, stop=False)
                        mm = pe_.matmul(o, xl, wh, start=False, stop=kt == K - 1)
                    if t == TT - 1:
                        mm.then_inc(item_done, 1)
                    elif j == last:
                        mm.then_inc(tile0_done, 1)
                if j == last and len(self.tiles) == 1:
                    e.sem_inc(tile0_done, 1)

            def pe(self, e):
                def body(n, first):
                    for j in range(self.ipc):
                        self.pe_item(e, n, j, first)
                        if self.epi and j == 0 and not first:
                            self.epi.pe(e, n - 1)
                    if first and "pe" in self.after_first:
                        self.after_first["pe"](e)
                self.chunks(e, body)
                if self.epi:
                    self.epi.pe(e, self.n - 1)

            def tile(self, a, kt, t):
                return a[:, self.kt0 + kt, t * P:(t + 1) * P]

            def run(self, k, e):
                {"pe": self.pe, "act": self.act, "dve": self.dve}[k](e)

        def rows_to(dst, width=CH, f=ACT.Copy, norm=None):
            def ea(e, n):
                if norm:
                    e.wait_ge(scaled, norm.ready)
                act_.activation(dst[:, 0, bass.ds(n * width, width)], acc[0][:, 0:width], f,
                                scale=norm.inv(0) if norm else 1.0).then_inc(evac[0], 1)

            def ed(e, n, t):
                o = dst[:, t, bass.ds(n * width, width)]
                if norm:
                    dve_.tensor_scalar(o, acc[t][:, 0:width], norm.inv(t), None, ALU.mult).then_inc(evac[t], 1)
                else:
                    dve_.tensor_copy(o, acc[t][:, 0:width]).then_inc(evac[t], 1)
            return ea, ed

        def add_to_x():
            def ed(e, n, t):
                xs = x[:, t, bass.ds(n * CH, CH)]
                dve_.tensor_tensor(xs, acc[t][:], xs, ALU.add).then_inc(evac[t], 1)
            return None, ed

        class Steps:

            unmet = False

            def __init__(self, name, pe=None, act=None, dve=None, parts=1):
                self.name = name
                self.f = {"pe": pe, "act": act, "dve": dve}
                self.parts = parts

            def walk(self, k, e):
                if self.parts > 1 and self.f[k]:
                    yield from self.f[k](e)
                elif self.parts > 1:
                    for _ in range(self.parts):
                        yield
                elif self.f[k]:
                    self.f[k](e)
                    yield
                else:
                    yield

            def run(self, k, e):
                for _ in self.walk(k, e):
                    pass

        fenced = {k: sem(f"{k}_fence") for k in ("pe", "act", "dve")}
        fences = [0]

        class Together:

            def __init__(self, name, gemms, work, lead=0):
                self.name, self.gemms, self.work = name, gemms, work
                self.unmet = False
                self.parts = sum(w.parts for w in work)
                self.lead = lead
                self.base = fences[0]
                fences[0] += len(work)

            def pieces(self, k, e):
                for i, w in enumerate(self.work):
                    yield from w.walk(k, e)
                    e.drain().then_inc(fenced[k], 1)
                    for other in fenced:
                        if other != k:
                            e.wait_ge(fenced[other], self.base + i + 1)

            def run(self, k, e):
                items = [(g, n, j) for g in self.gemms for n in range(g.n) for j in range(g.ipc)]
                at = Gemm.every.index(self.gemms[-1])
                nxt = Gemm.every[at + 1]
                ahead = items + [(nxt, 0, 0)]
                make = Gemm.make_hi if k == "act" else Gemm.make_lo
                work, done, Q = self.pieces(k, e), 0, len(items)
                for q, (g, n, j) in enumerate(items):
                    if k == "pe":
                        g.pe_item(e, n, j, False)
                    else:
                        if j == 0 and q:
                            (g0, n0, _) = items[q - 1]
                            (g0.out_act if k == "act" else g0.out_dve)(e, n0)
                        make(ahead[q + 1][0], e, ahead[q + 1][1], ahead[q + 1][2])
                    while done < (q + 1) * self.parts // Q:
                        next(work)
                        done += 1
                if k != "pe":
                    g, n, _ = items[-1]
                    (g.out_act if k == "act" else g.out_dve)(e, n)
                for _ in work:
                    pass

        turned = sem("turned")
        turned_hi = sem("turned_hi")
        turned_lo = sem("turned_lo")
        turns = [0]

        def to_lhs(src, n, hi, lo, kt0=0, gain=None):
            base = turns[0]
            turns[0] += n // 2
            W = len(wk)

            def pe(e):
                for p in range(n // 2):
                    if p >= W:
                        e.wait_ge(turned_lo, base + p - W + 1)
                    for i in (2 * p, 2 * p + 1):
                        for t in range(TT):
                            c = (i % 2) * S + t * P
                            mm = pe_.matmul(wk[p % W][:, c:c + P], src(t, i), ident[:], start=True, stop=True,
                                            is_transpose=True)
                    mm.then_inc(turned, 1)

            def act(e):
                for p in range(n // 2):
                    e.wait_ge(turned, base + p + 1)
                    b = wk[p % W]
                    if gain is None:
                        ins = act_.activation(hi[:, kt0 + 2 * p:kt0 + 2 * p + 2, :],
                                              b[:].rearrange("p (c s) -> p c s", c=2), ACT.Copy)
                    else:
                        for i in (2 * p, 2 * p + 1):
                            ins = act_.activation(hi[:, kt0 + i, :], b[:, (i % 2) * S:(i % 2 + 1) * S], ACT.Copy,
                                                  scale=gain[:, i:i + 1])
                    ins.then_inc(turned_hi, 1)

            def dve(e):
                for p in range(n // 2):
                    e.wait_ge(turned_hi, base + p + 1)
                    b = wk[p % W]
                    if gain is None:
                        k = slice(kt0 + 2 * p, kt0 + 2 * p + 2)
                        ins = dve_.tensor_tensor(lo[:, k, :], b[:].rearrange("p (c s) -> p c s", c=2),
                                                 hi[:, k, :].bitcast(F32), ALU.subtract)
                    else:
                        for i in (2 * p, 2 * p + 1):
                            ins = dve_.scalar_tensor_tensor(out=lo[:, kt0 + i, :], in0=b[:, (i % 2) * S:(i % 2 + 1) * S],
                                                            scalar=gain[:, i:i + 1], in1=hi[:, kt0 + i, :].bitcast(F32),
                                                            op0=ALU.mult, op1=ALU.subtract)
                    ins.then_inc(turned_lo, 1)
            return pe, act, dve

        def turn(name, src, n, hi, lo, kt0=0):
            s = Steps(name, *to_lhs(src, n, hi, lo, kt0))
            s.unmet = True
            s.lhs_from = (turns[0] - n // 2, kt0)
            return s

        tr_done = sem("tr_done")
        tr_out = sem("tr_out")
        tr_groups = [0]

        def to_tiles(pairs, scale=None):
            base = tr_groups[0]
            tr_groups[0] += len(pairs)
            banks = (wk[0], wk[1], wk[2], wk[3])

            def pe(e):
                for i, (src, dst) in enumerate(pairs):
                    if i >= 4:
                        e.wait_ge(tr_out, base + i - 3)
                    for t in range(TT):
                        a = src(t)
                        mm = pe_.matmul(banks[i % 4][0:a.shape[1], t * P:(t + 1) * P], a, ident[:],
                                        start=True, stop=True, is_transpose=True)
                    mm.then_inc(tr_done, 1)
                    if i % 4 == 3 or i == len(pairs) - 1:
                        yield

            def act(e):
                for i, (src, dst) in enumerate(pairs):
                    e.wait_ge(tr_done, base + i + 1)
                    bank = banks[i % 4][0:dst.shape[0], 0:S]
                    if len(dst.shape) == 3:
                        bank = bank.rearrange("p (t c) -> p t c", t=TT)
                    act_.activation(dst, bank, ACT.Copy,
                                    scale=1.0 if scale is None else scale[i]).then_inc(tr_out, 1)
                    if i % 4 == 3 or i == len(pairs) - 1:
                        yield
            return pe, act, None, -(-len(pairs) // 4)

        squared = sem("squared")
        scaled = sem("scaled")
        norms = [0]

        class Norm:

            def __init__(self):
                self.base = norms[0]
                norms[0] += TT
                self.ready = self.base + TT

            def inv(self, t):
                c = 64 + self.base + t
                return st[:, c:c + 1]

            def roots(self, e, src, row):
                for t in range(TT):
                    act_.activation(row(t), src[:, t, :], ACT.Square, accum_out=st[:, t:t + 1])
                    e.drain()
                    act_.activation(st[:, 2 + t:3 + t], st[:, t:t + 1], ACT.Sqrt, scale=1.0 / D,
                                    bias=eps_c[:]).then_inc(squared, 1)

            def inverse(self, e, t):
                e.wait_ge(squared, self.base + t + 1)
                return dve_.reciprocal(self.inv(t), st[:, 2 + t:3 + t])

        def norm_to_lhs(name, src, rows, hi, lo, gain, need=None):
            norm = Norm()
            base = turns[0]
            tp, ta, td = to_lhs(lambda t, i: src[:, t, i * P:(i + 1) * P], KD, hi, lo, gain=gain)

            def pe(e):
                if need:
                    need(e)
                tp(e)

            def act(e):
                if need:
                    need(e)
                ta(e)
                norm.roots(e, src, lambda t: rows[:, t, :])

            def dve(e):
                td(e)
                for t in range(TT):
                    norm.inverse(e, t).then_inc(scaled, 1)
            s = Steps(name, pe, act, dve)
            s.unmet = True
            s.norm, s.lhs_from = norm, (base, 0)
            return s

        s_done = sem("s_done")
        s_max = sem("s_max")
        s_exp = sem("s_exp")
        s_norm = sem("s_norm")
        p_turned = sem("p_turned")
        p_copied = sem("p_copied")
        o_done = sem("o_done")
        o_hi = sem("o_hi")
        o_lo = sem("o_lo")
        units_so_far, outs_so_far, lows_so_far = [0], [0], [0]

        class Unit:

            def __init__(self, q, k, v, blocks, scale, bias=None, kw=P, extra=None, gate=None, first=True,
                         last=True, part=(0, P), hi=None, lo=None):
                self.q, self.k, self.v, self.scale, self.bias, self.kw = q, k, v, scale, bias, kw
                self.extra, self.gate, self.first, self.last, self.part = extra, gate, first, last, part
                self.hi, self.lo = hi, lo
                self.cols = sum(len(k_) for _, k_ in blocks) * kw
                self.seg = []
                at = 0
                for qt, kts in blocks:
                    self.seg.append((qt, kts, at))
                    at += len(kts) * kw

        def attention(name, units, L, PT, need=None, needs={}):
            ub, ob = units_so_far[0], outs_so_far[0]
            units_so_far[0] += len(units)
            outs = []
            for i, u in enumerate(units):
                u.out = len(outs)
                if u.last:
                    outs.append(i)
            outs_so_far[0] += len(outs)
            lb = lows_so_far[0]
            if units[0].lo is not None:
                lows_so_far[0] += len(outs)
            sc, tb, ov = (wk[0], wk[1]), wk[2], (wk[3], wk[4])
            N = len(units)

            def scores(e, i):
                u = units[i]
                if i >= 2:
                    e.wait_ge(s_max, ub + i - 1)
                for qt, kts, at in u.seg:
                    o = sc[i % 2][:, at:at + len(kts) * u.kw]
                    more = u.extra(qt, kts) if u.extra else []
                    mm = pe_.matmul(o, u.q[:, qt * P:(qt + 1) * P], u.k[:, 0:len(kts) * u.kw],
                                    start=True, stop=not more)
                    for n, (a, b) in enumerate(more):
                        mm = pe_.matmul(o, a, b, start=False, stop=n == len(more) - 1)
                mm.then_inc(s_done, 1)

            def turn(e, i):
                u = units[i]
                e.wait_ge(s_norm, ub + i + 1)
                if i >= 1:
                    e.wait_ge(p_copied, ub + i)
                c = 0
                for qt, kts, at in u.seg:
                    for n in range(len(kts)):
                        mm = pe_.matmul(tb[0:u.kw, c * P:(c + 1) * P],
                                        L[:, i % 2, at + n * u.kw:at + (n + 1) * u.kw], ident[:],
                                        start=True, stop=True, is_transpose=True)
                        c += 1
                mm.then_inc(p_turned, 1)

            def values(e, i):
                u = units[i]
                e.wait_ge(p_copied, ub + i + 1)
                if u.first and u.out >= 2:
                    e.wait_ge(o_hi, ob + u.out - 1)
                    if u.lo is not None:
                        e.wait_ge(o_lo, lb + u.out - 1)
                c = 0
                p0, p1 = u.part
                for qt, kts, at in u.seg:
                    for n, kt in enumerate(kts):
                        mm = pe_.matmul(ov[u.out % 2][p0:p1, qt * P:(qt + 1) * P], u.v(kt),
                                        PT[0:u.kw, i % 2, c * P:(c + 1) * P],
                                        start=u.first and n == 0 and qt == 0, stop=u.last and n == len(kts) - 1,
                                        skip_group_check=True)
                        c += 1
                mm.then_inc(o_done, 1)

            def pe(e):
                for i in range(N + 4):
                    if 2 <= i < N + 2:
                        turn(e, i - 2)
                    if 3 <= i < N + 3:
                        values(e, i - 3)
                    if i < N:
                        scores(e, i)
                    yield

            def act(e):
                for i in range(N + 4):
                    if 2 <= i < N + 2:
                        u = units[i - 2]
                        e.wait_ge(p_turned, ub + i - 1)
                        if i >= 4:
                            e.wait_ge(o_done, ub + i - 3)
                        c = sum(len(k_) for _, k_, _ in u.seg) * P
                        act_.activation(PT[0:u.kw, i % 2, 0:c], tb[0:u.kw, 0:c], ACT.Copy).then_inc(p_copied, 1)
                    if i < N:
                        u = units[i]
                        e.wait_ge(s_max, ub + i + 1)
                        for n, (qt, kts, at) in enumerate(u.seg):
                            a = L[:, i % 2, at:at + len(kts) * u.kw]
                            ins = act_.activation(a, a, ACT.Exp, bias=st[:, 16 + 8 * (i % 2) + n:17 + 8 * (i % 2) + n],
                                                  accum_out=st[:, 18 + 8 * (i % 2) + n:19 + 8 * (i % 2) + n])
                        ins.then_inc(s_exp, 1)
                    if i >= 4 and units[i - 4].last:
                        u = units[i - 4]
                        e.wait_ge(o_done, ub + i - 3)
                        act_.activation(u.hi, ov[u.out % 2][u.part[0]:u.part[1], 0:S], ACT.Copy).then_inc(o_hi, 1)
                    yield

            def dve(e):
                if need:
                    need(e)
                for i in range(N + 4):
                    if i in needs:
                        needs[i](e)
                    if i < N:
                        u = units[i]
                        b = 16 + 8 * (i % 2)
                        e.wait_ge(s_done, ub + i + 1)
                        if i >= 2:
                            e.wait_ge(p_turned, ub + i - 1)
                        l = L[:, i % 2, 0:u.cols]
                        if u.bias is not None:
                            dve_.scalar_tensor_tensor(out=l, in0=sc[i % 2][:, 0:u.cols], scalar=u.scale, in1=u.bias,
                                                      op0=ALU.mult, op1=ALU.add)
                        else:
                            dve_.tensor_scalar(l, sc[i % 2][:, 0:u.cols], u.scale, None, ALU.mult)
                        e.drain()
                        for n, (qt, kts, at) in enumerate(u.seg):
                            dve_.tensor_reduce(st[:, b + n:b + n + 1], L[:, i % 2, at:at + len(kts) * u.kw],
                                               AX.X, ALU.max)
                        e.drain()
                        dve_.tensor_scalar(st[:, b:b + 2], st[:, b:b + 2], -1.0, FLOOR, ALU.mult,
                                           ALU.min).then_inc(s_max, 1)
                    if 1 <= i <= N:
                        u = units[i - 1]
                        b = 16 + 8 * ((i - 1) % 2)
                        e.wait_ge(s_exp, ub + i)
                        dve_.tensor_scalar(st[:, b + 2:b + 4], st[:, b + 2:b + 4], 1e-30, None, ALU.max)
                        e.drain()
                        dve_.reciprocal(st[:, b + 4:b + 6], st[:, b + 2:b + 4])
                        e.drain()
                        for n, (qt, kts, at) in enumerate(u.seg):
                            a = L[:, (i - 1) % 2, at:at + len(kts) * u.kw]
                            if u.gate:
                                ins = dve_.tensor_scalar(a, a, st[:, b + 4 + n:b + 5 + n], u.gate(qt), ALU.mult, ALU.mult)
                            else:
                                ins = dve_.tensor_scalar(a, a, st[:, b + 4 + n:b + 5 + n], None, ALU.mult)
                        ins.then_inc(s_norm, 1)
                    if i >= 4 and units[i - 4].last and units[i - 4].lo is not None:
                        u = units[i - 4]
                        e.wait_ge(o_hi, ob + u.out + 1)
                        dve_.tensor_tensor(u.lo, ov[u.out % 2][u.part[0]:u.part[1], 0:S], u.hi.bitcast(F32),
                                           ALU.subtract).then_inc(o_lo, 1)
                    yield
            return Steps(name, pe, act, dve, parts=N + 4)

        def stage_end(e, k, i, s):
            e.drain().then_inc(at_end[k], 1)
            for other in at_end:
                if other != k and not s.unmet:
                    e.wait_ge(at_end[other], i + 1)

        def bc(ap, n):
            return ap.unsqueeze(1).to_broadcast([ap.shape[0], n, ap.shape[1]])

        def load(e, name, dst, src, after=None):
            if name not in landed:
                landed[name] = sem("in_" + name)
            if after is not None:
                for k in at_end:
                    e.wait_ge(at_end[k], after)
            e.dma_start(dst, src).then_inc(landed[name], 16)

        def got(e, name):
            if name not in landed:
                landed[name] = sem("in_" + name)
            e.wait_ge(landed[name], 16)

        pool_steps = []
        def at(label):
            return [s.name for s in stages].index(label)

        ar1 = ExitStack()
        p1 = sb("p1", [P, TT, P1_N], F32, ar1)
        tt1 = sb("tt1", [P, 20, S], F32, ar1)
        c8 = sb("c8", [8, 2, S], F32, ar1)
        b_t = sb("b_t", [C_DK, C_H, S], F32, ar1)
        cmask = sb("cmask", [P, 384], F32, ar1)
        ws1_hi = sb("ws1_hi", [P, KD * 24], F32R, ar1)
        ws1_lo = sb("ws1_lo", [P, KD * 24], F32R, ar1)
        l1 = sb("l1", [P, 2, 384], F32, ar1)
        pt1 = sb("pt1", [P, 2, 384], F32, ar1)

        rows0 = p1[:, :, 0:D]
        toe_mm, toe_row, toe_out, toe_dma = sem("toe_mm"), sem("toe_row"), sem("toe_out"), sem("toe_dma")
        tt1f = tt1[:].rearrange("p a b -> p (a b)")

        def toe_place(rows, slot, w):
            return [tt1f[0:r, (4 * i + slot) * 400:(4 * i + slot) * 400 + c] for i, (r, c) in enumerate(zip(rows, w))]
        tw = toe_place((REL, REL), 0, (TOE, TOE))
        trel = toe_place((REL, REL), 1, (A_H, N_H))
        tadd = toe_place((A_H, N_H), 2, (TOE, TOE))
        tsum = toe_place((A_H, N_H), 3, (TOE, TOE))

        def toe_pool(e):
            for i in range(2):
                load(e, f"tw{i}", tw[i], t_in[f"onehot{i}"])
                load(e, f"trel{i}", trel[i], t_in[f"rel{i}"])
                load(e, f"tadd{i}", tadd[i], t_in[f"toe_add{i}"])
            e.wait_ge(toe_out, 2)
            for table, row, heads in ((toe1, tsum[0], A_H), (toe2, tsum[1], N_H)):
                e.dma_start(table, row.unsqueeze(1).to_broadcast([heads, P, TOE])).then_inc(toe_dma, 16)
            e.wait_ge(toe_dma, 32)
            load(e, "tri", tri[:], t_in["tri"])
            load(e, "cmask", cmask[:], t_in["cmask"])
        pool_steps.append(toe_pool)

        def toe_pe(e):
            for i in range(2):
                got(e, f"tw{i}")
                got(e, f"trel{i}")
                pe_.matmul(wk[4 + i][0:(A_H, N_H)[i], 0:TOE], trel[i], tw[i], start=True, stop=True).then_inc(toe_mm, 1)

        def toe_dve(e):
            for i in range(2):
                got(e, f"tadd{i}")
                e.wait_ge(toe_mm, i + 1)
                dve_.tensor_tensor(tsum[i], wk[4 + i][0:(A_H, N_H)[i], 0:TOE], tadd[i], ALU.add).then_inc(toe_out, 1)

        def start_pe(e):
            got(e, "ident")
            got(e, "x")

        def start_dve(e):
            dve_.memset(ones[:], 1.0)
            dve_.memset(eps_c[:], EPS)
            Gemm.every[0].make_lo(e, 0, 0)
            got(e, "gains")

        def start_act(e):
            Gemm.every[0].make_hi(e, 0, 0)
            got(e, "gains")
            got(e, "x")
        stages.append(Steps("start", start_pe, start_act, start_dve))
        stages.append(norm_to_lhs("norm_mix", x, rows0, h_hi, h_lo, gains[:, 0, :]))
        mix = stages[-1]
        lhs = (h_hi, h_lo)
        stages.append(Gemm("win", lhs, 0, *rows_to(p1, norm=mix.norm)))
        stages[-1].lhs_from = mix.lhs_from
        stages[-1].after_first = {"pe": toe_pe, "dve": toe_dve}
        winc = Gemm("winc", lhs, 0, *rows_to(p1[:, :, 8 * CH:], norm=mix.norm))

        w_s1 = tt1[:, 0:2, :].rearrange("p a b -> p (a b)")[:, 0:KD * 24]
        srow = tt1[:, 2, 0:48]
        glt = tt1[0:C_R, 3, :]
        w_g2 = tt1[0:C_R, 4:6, :].rearrange("p a b -> p (a b)")[:, 0:C_KW]
        gb = tt1[0:1, 6:8, :].rearrange("p a b -> p (a b)")[:, 0:C_KW]
        fb = tt1[:, 8, 0:B_H]
        LAW = 16 + 2 * C_KW
        la = tt1[:, 9:13, :].rearrange("p a b -> p (a b)")[:, 0:LAW]
        la_t = tt1[:, 13:17, :].rearrange("p a b -> p (a b)")[:, 0:LAW]
        s1_mm, s1_row, s1_tr, s1_gl, s1_la, s1_abs, s1_ln, s1_log, s1_cum = [
            sem(n) for n in ("small_prod", "small_rows", "gl_turned", "gl_copied", "gate_logits", "gate_abs",
                             "gate_ln", "log_gates", "gates_summed")]

        s1_split, s2_split = sem("small1_split"), sem("small2_split")

        def small_product(bank, w_hi, w_lo, c):
            for t in range(TT):
                for kt in range(KD):
                    xh, xl = h_hi[:, kt, t * P:(t + 1) * P], h_lo[:, kt, t * P:(t + 1) * P]
                    wh, wl = w_hi[:, kt * c:(kt + 1) * c], w_lo[:, kt * c:(kt + 1) * c]
                    o = bank[:, t * c:(t + 1) * c]
                    pe_.matmul(o, xh, wh, start=kt == 0, stop=False)
                    pe_.matmul(o, xh, wl, start=False, stop=False)
                    mm = pe_.matmul(o, xl, wh, start=False, stop=kt == KD - 1)
            return mm

        def small1_pool(e):
            load(e, "w_s1", w_s1, t_in["w_small1"], after=0)
            load(e, "w_g2", w_g2, t_in["c_gate_w2"])
            load(e, "gb", gb, t_in["c_gate_b"])
            load(e, "fb", fb, t_in["f_bias"].to_broadcast([P, B_H]))
        pool_steps.append(small1_pool)

        def small1_pe(e):
            e.wait_ge(s1_split, 2)
            small_product(wk[0], ws1_hi[:], ws1_lo[:], 24).then_inc(s1_mm, 1)
            yield
            e.wait_ge(s1_row, 1)
            for t in range(TT):
                mm = pe_.matmul(wk[1][0:C_R, t * P:(t + 1) * P], srow[:, t * 24 + 8:t * 24 + 24], ident[:],
                                start=True, stop=True, is_transpose=True)
            mm.then_inc(s1_tr, 1)
            yield
            e.wait_ge(s1_gl, 1)
            got(e, "w_g2")
            got(e, "gb")
            for t in range(TT):
                pe_.matmul(wk[2 + t][:, 0:C_KW], glt[:, t * P:(t + 1) * P], w_g2, start=True, stop=False)
                mm = pe_.matmul(wk[2 + t][:, 0:C_KW], ones[0:1, :], gb, start=False, stop=True)
            mm.then_inc(s1_la, 1)
            yield
            e.wait_ge(s1_log, 1)
            got(e, "tri")
            for t in range(TT):
                pe_.matmul(wk[0][0:8, 0:S], la[:, t * 8:t * 8 + 8], tri[:, t, :], start=t == 0, stop=t == 1)
            for h in range(C_H):
                for t in range(TT):
                    c = 16 + t * C_KW + h * C_DK
                    mm = pe_.matmul(wk[4 + h // 2][0:C_DK, (h % 2) * S:(h % 2 + 1) * S], la[:, c:c + C_DK],
                                    tri[:, t, :], start=t == 0, stop=t == 1)
            mm.then_inc(s1_cum, 1)
            yield

        def small1_act(e):
            got(e, "w_s1")
            act_.activation(ws1_hi[:], w_s1, ACT.Copy).then_inc(s1_split, 1)
            e.wait_ge(s1_mm, 1)
            for t in range(TT):
                ins = act_.activation(srow[:, t * 24:(t + 1) * 24], wk[0][:, t * 24:(t + 1) * 24], ACT.Copy,
                                      scale=mix.norm.inv(t))
            ins.then_inc(s1_row, 1)
            yield
            e.wait_ge(s1_tr, 1)
            act_.activation(glt, wk[1][0:C_R, 0:S], ACT.Copy).then_inc(s1_gl, 1)
            yield
            e.wait_ge(s1_abs, 1)
            act_.activation(la_t, la_t, ACT.Exp)
            e.drain()
            act_.activation(la_t, la_t, ACT.Ln, bias=ones[:, 0:1]).then_inc(s1_ln, 1)
            yield
            e.wait_ge(s1_cum, 1)
            act_.activation(c8[:, 0, :], wk[0][0:8, 0:S], ACT.Copy, scale=8.0)
            act_.activation(c8[:, 1, :], wk[0][0:8, 0:S], ACT.Copy, scale=-8.0)
            for h in range(0, C_H, 2):
                act_.activation(b_t[:, h:h + 2, :].rearrange("p a b -> p (a b)"), wk[4 + h // 2][0:C_DK, :],
                                ACT.Copy, scale=1.0 / 16)
            yield

        def small1_dve(e):
            e.wait_ge(s1_split, 1)
            dve_.tensor_tensor(ws1_lo[:], w_s1, ws1_hi[:].bitcast(F32), ALU.subtract).then_inc(s1_split, 1)
            e.wait_ge(s1_row, 1)
            got(e, "fb")
            for t in range(TT):
                dve_.tensor_tensor(la[:, t * 8:t * 8 + 8], srow[:, t * 24:t * 24 + 8], fb, ALU.add)
            yield
            yield
            e.wait_ge(s1_la, 1)
            for t in range(TT):
                dve_.tensor_copy(la[:, 16 + t * C_KW:16 + (t + 1) * C_KW], wk[2 + t][:, 0:C_KW])
            e.drain()
            dve_.scalar_tensor_tensor(out=la_t, in0=la, scalar=-1.0, in1=la, op0=ALU.mult,
                                      op1=ALU.min).then_inc(s1_abs, 1)
            e.drain()
            dve_.tensor_scalar(la, la, 0.0, None, ALU.min)
            e.drain()
            e.wait_ge(s1_ln, 1)
            dve_.tensor_tensor(la, la, la_t, ALU.subtract).then_inc(s1_log, 1)
            yield
            yield
        small1 = Steps("small1", small1_pe, small1_act, small1_dve, 4)

        turn1 = Steps("turn1", *to_tiles([
            ((lambda t, i=i: p1[:, t, i * P:(i + 1) * P]), tt1[:, i, :]) for i in range(20)]))

        def toeplitz(e, name, dst, table, heads, at_stage):
            landed[name] = sem("in_" + name)
            for k, sems in (at_stage.items() if isinstance(at_stage, dict) else ((k, at_stage) for k in at_end)):
                if isinstance(at_stage, dict):
                    e.wait_ge(fenced[k], sems)
                else:
                    e.wait_ge(at_end[k], sems)
            for h in range(heads):
                for c0, w, off in ((0, P, 255), (P, S, 127)):
                    src = bass.AP(tensor=table.tensor, offset=h * P * TOE + off, ap=[[TOE - 1, P], [1, w]])
                    e.dma_start(dst(h)[:, c0:c0 + w], src).then_inc(landed[name], 16)

        ab_hi = sem("ab_hi")

        def split_ab_dve(e):
            e.wait_ge(ab_hi, 1)
            dve_.tensor_tensor(h_lo[:, 0:10, :], o_ab, h_hi[:, 0:10, :].bitcast(F32), ALU.subtract)

        def bias1(h):
            return p1[:, h // 6, (h % 6) * TOE:(h % 6 + 1) * TOE]
        after_turn1 = {k: fences[0] + 2 for k in fenced}
        pool_steps.append(lambda e: toeplitz(e, "bias1", bias1, toe1, A_H, after_turn1))
        o_ab = x[:].rearrange("p a b -> p (a b)")[:, 0:10 * S].rearrange("p (i s) -> p i s", i=10)

        def half(h):
            return (h % 2) * 64, (h % 2) * 64 + 64

        def a_unit(h):
            p0, p1_ = half(h)
            return Unit(tt1[p0:p1_, h // 2, :], tt1[p0:p1_, 6 + h // 2, :],
                        lambda kt: p1[:, kt, P1_VA + h * 64:P1_VA + (h + 1) * 64], CAUSAL, A_D ** -0.5, bias1(h),
                        part=(p0, p1_), hi=o_ab[p0:p1_, h // 2, :])

        def b_unit(h):
            p0, p1_ = half(h)

            def extra(qt, kts):
                one = ident[0:8, h:h + 1]
                n = len(kts) * P
                return [(c8[:, 0, qt * P:(qt + 1) * P], one.to_broadcast([8, n])),
                        (one.to_broadcast([8, P]), c8[:, 1, 0:n])]
            return Unit(tt1[p0:p1_, 12 + h // 2, :], tt1[p0:p1_, 16 + h // 2, :],
                        lambda kt: p1[:, kt, P1_VB + h * 64:P1_VB + (h + 1) * 64], CAUSAL, A_D ** -0.5, cmask[:],
                        extra=extra, part=(p0, p1_), hi=o_ab[p0:p1_, 6 + h // 2, :])

        def bias1_there(e):
            e.wait_ge(landed["bias1"], 16 * 2 * A_H)
        stages.append(Together("ab+winc", [winc], [small1, turn1, attention(
            "attention_ab", [b_unit(h) for h in range(B_H)] + [a_unit(h) for h in range(A_H)], l1, pt1,
            lambda e: got(e, "cmask"), {B_H: bias1_there})]))
        stages.append(Steps("split_ab", None,
                            lambda e: act_.activation(h_hi[:, 0:10, :], o_ab, ACT.Copy).then_inc(ab_hi, 1),
                            split_ab_dve))
        after_split = len(stages)
        pool_steps.append(lambda e: load(e, "x_again", x[:], t_in["x"], after=after_split))

        qk_c = tt1[0:C_DK, 0:8, :]
        q_c, k_c = qk_c[:, 0:4, :], qk_c[:, 4:8, :]
        stages.append(Steps("turn_c", *to_tiles(
            [((lambda t, c=c: p1[:, t, c:c + C_DK]), qk_c[:, i, :])
             for i, c in enumerate([P1_QC + h * C_DK for h in range(4)] + [P1_KC + h * C_DK for h in range(4)])],
            [C_DK ** -0.5] * 4 + [1.0] * 4)))
        dif = tt1[0:C_DK, 8:12, :]
        xqk = tt1[0:C_DK, 12:16, :]
        a_t = tt1[:, 16:20, :].rearrange("p a b -> p (a b)").rearrange("p (t h i) -> p t h i", t=2, h=4)
        a_off = l1[:].rearrange("p a b -> p (a b)")[:, 0:512].rearrange("p (h i) -> p h i", h=4)
        tmp_c = pt1[:].rearrange("p a b -> p (a b)")[:, 0:512].rearrange("p (h i) -> p h i", h=4)
        lmask = p1[:, 0, 1024:2048].rearrange("p (l i) -> p l i", l=8)
        cn = p1[:, 1, 1024:1024 + C_DV]
        o_c = p1[:, :, 0:C_VW]
        after_ab = len(stages) - 1

        def gla_pool(e):
            load(e, "lmask", lmask, t_in["lmask"], after=after_ab)
            load(e, "cn", cn, t_in["c_norm"].to_broadcast([P, C_DV]))
        pool_steps.append(gla_pool)
        g_dif, g_exp, g_x, g_mm, g_acc, g_o, g_ss, g_silu = [sem(n) for n in (
            "gla_exponent", "gla_decay", "gla_scaled", "gla_scores", "gla_summed", "gla_out", "gla_squares", "gla_gate")]
        LEV = 8

        def halves(a, s):
            return a.rearrange("p h (n two s) -> p (h n) two s", two=2, s=s)

        def gla_dve(e):
            def exponent(l):
                s = 1 << l
                b, d = halves(b_t[:], s), halves(dif, s)
                e.drain()
                ref = b[:, :, 0, s - 1:s].to_broadcast([C_DK, 4 * S // (2 * s), s])
                dve_.tensor_tensor(d[:, :, 1, :], b[:, :, 1, :], ref, ALU.subtract)
                dve_.tensor_tensor(d[:, :, 0, :], ref, b[:, :, 0, :], ALU.subtract).then_inc(g_dif, 1)

            def scaled_(l):
                s = 1 << l
                e.wait_ge(g_exp, l + 1)
                if l:
                    e.wait_ge(g_mm, l)
                d, xx = halves(dif, s), halves(xqk, s)
                dve_.tensor_tensor(xx[:, :, 1, :], halves(q_c, s)[:, :, 1, :], d[:, :, 1, :], ALU.mult)
                dve_.tensor_tensor(xx[:, :, 0, :], halves(k_c, s)[:, :, 0, :], d[:, :, 0, :],
                                   ALU.mult).then_inc(g_x, 1)

            def add_level(l):
                e.wait_ge(g_mm, l + 1)
                bank = [wk[2 * (l % 2) + t][:].rearrange("p (h i) -> p h i", h=4) for t in range(2)]
                if l == LEV - 1:
                    dve_.tensor_copy(a_off, bank[0]).then_inc(g_acc, 1)
                    return
                mask = bc(ident[:] if l == LEV else lmask[:, l, :], 4)
                for t in range(2):
                    if l == 0:
                        ins = dve_.tensor_tensor(a_t[:, t], bank[t], mask, ALU.mult)
                    else:
                        dve_.tensor_tensor(tmp_c, bank[t], mask, ALU.mult)
                        e.drain()
                        ins = dve_.tensor_tensor(a_t[:, t], a_t[:, t], tmp_c, ALU.add)
                        e.drain()
                ins.then_inc(g_acc, 1)
            got(e, "lmask")
            for l in range(LEV):
                exponent(l)
                if l:
                    add_level(l - 1)
                scaled_(l)
            add_level(LEV - 1)
            add_level(LEV)
            got(e, "cn")
            e.wait_ge(g_ss, 1)
            dve_.reciprocal(st[:, 48:56], st[:, 40:48])
            e.drain()
            for t in range(TT):
                for h in range(C_H):
                    dve_.scalar_tensor_tensor(out=o_c[:, t, h * C_DV:(h + 1) * C_DV],
                                              in0=wk[2 * t + h // 2][:, (h % 2) * C_DV:(h % 2 + 1) * C_DV],
                                              scalar=st[:, 48 + t * 4 + h:49 + t * 4 + h], in1=cn,
                                              op0=ALU.mult, op1=ALU.mult)
            e.drain()
            e.wait_ge(g_silu, 1)
            dve_.tensor_tensor(o_c, o_c, p1[:, :, P1_RC:P1_RC + C_VW], ALU.mult)

        def gla_act(e):
            for l in range(LEV):
                e.wait_ge(g_dif, l + 1)
                act_.activation(dif, dif, ACT.Exp).then_inc(g_exp, 1)
            act_.activation(p1[:, :, P1_RC:P1_RC + C_VW], p1[:, :, P1_RC:P1_RC + C_VW], ACT.Silu).then_inc(g_silu, 1)
            e.wait_ge(g_o, 1)
            for t in range(TT):
                for h in range(C_H):
                    ins = act_.activation(tmp_c.rearrange("p h i -> p (h i)")[:, 0:C_DV],
                                          wk[2 * t + h // 2][:, (h % 2) * C_DV:(h % 2 + 1) * C_DV],
                                          ACT.Square, accum_out=st[:, 32 + t * 4 + h:33 + t * 4 + h])
                    e.drain()
            act_.activation(st[:, 40:48], st[:, 32:40], ACT.Sqrt, scale=1.0 / C_DV, bias=eps_c[:]).then_inc(g_ss, 1)

        def gla_pe(e):
            for l in range(LEV + 1):
                if l < LEV:
                    e.wait_ge(g_x, l + 1)
                if l >= 2:
                    e.wait_ge(g_acc, l - 1)
                a, b = (xqk, xqk) if l < LEV else (k_c, q_c)
                for t in range(TT if l != LEV - 1 else 1):
                    t1 = t if l != LEV - 1 else 1
                    for h in range(C_H):
                        mm = pe_.matmul(wk[2 * (l % 2) + t][:, h * P:(h + 1) * P], a[:, h, t * P:(t + 1) * P],
                                        b[:, h, t1 * P:(t1 + 1) * P], start=True, stop=True)
                mm.then_inc(g_mm, 1)
            e.wait_ge(g_acc, LEV + 1)
            for t in range(TT):
                for h in range(C_H):
                    v = [p1[:, k, P1_VC + h * C_DV:P1_VC + (h + 1) * C_DV] for k in range(2)]
                    o = wk[2 * t + h // 2][:, (h % 2) * C_DV:(h % 2 + 1) * C_DV]
                    if t:
                        pe_.matmul(o, a_off[:, h, :], v[0], start=True, stop=False)
                    mm = pe_.matmul(o, a_t[:, t, h, :], v[t], start=t == 0, stop=True)
            mm.then_inc(g_o, 1)
        stages.append(Steps("gla", gla_pe, gla_act, gla_dve))
        stages.append(turn("turn_oc", lambda t, i: o_c[:, t, i * P:(i + 1) * P], 6, h_hi, h_lo, kt0=10))
        turn_oc = stages[-1]
        stages.append(Steps("x_back", None, None, lambda e: got(e, "x_again")))
        stages[-1].unmet = True
        stages.append(Gemm("wout", lhs, 0, *add_to_x()))
        stages[-1].lhs_from = turn_oc.lhs_from

        mem = p1[:, :, 0:D]
        memr = p1[:, :, D:2 * D]
        kvr = p1[:, :, 2 * D:2 * D + 1024]
        qr = p1[:, :, 2 * D + 1024:2 * D + 1536]
        before_mem = len(stages) - 1
        pool_steps.append(lambda e: load(e, "mem", mem, t_in["mem"], after=before_mem))
        stages.append(norm_to_lhs("norm_mem", mem, memr, h_hi, h_lo, gains[:, 1, :], need=lambda e: got(e, "mem")))
        mem_n = stages[-1]
        stages.append(Gemm("ckv", lhs, 0, *rows_to(kvr, norm=mem_n.norm)))
        stages[-1].lhs_from = mem_n.lhs_from
        stages.append(norm_to_lhs("norm_cross", x, memr, h_hi, h_lo, gains[:, 2, :]))
        cross_n = stages[-1]
        stages.append(Gemm("cq", lhs, 0, *rows_to(qr, norm=cross_n.norm)))
        stages[-1].lhs_from = cross_n.lhs_from
        stages.append(Steps("turn_x", *to_tiles(
            [((lambda t, h=h: qr[:, t, h * P:(h + 1) * P]), tt1[:, h, :]) for h in range(4)] +
            [((lambda t, h=h: kvr[:, t, h * P:(h + 1) * P]), tt1[:, 4 + h, :]) for h in range(4)])))
        lx = tt1[:, 8:12, :].rearrange("p a b -> p (a b)").rearrange("p (a b) -> p a b", a=2)
        px = tt1[:, 12:16, :].rearrange("p a b -> p (a b)").rearrange("p (a b) -> p a b", a=2)
        stages.append(attention("attention_x", [
            Unit(tt1[:, h, :], tt1[:, 4 + h, :], (lambda kt, h=h: kvr[:, kt, 512 + h * P:512 + (h + 1) * P]), FULL,
                 X_D ** -0.5, hi=h_hi[:, h, :], lo=h_lo[:, h, :]) for h in range(4)], lx, px))
        stages.append(Gemm("co", lhs, 0, *add_to_x()))
        stages.append(norm_to_lhs("norm_ffn", x, memr, h_hi, h_lo, gains[:, 3, :]))
        ar1.close()

        ar = ExitStack()
        f_hi = sb("f_hi", [P, 32, S], F32R, ar)
        f_lo = sb("f_lo", [P, 32, S], F32R, ar)
        stg = sb("stg", [P, TT, CH], F32, ar)
        cv = sb("cv", [P, 2, S], F32, ar)
        sq = sb("sq", [P, 4, S], F32, ar)
        cw = sb("cw", [P, KF1, 4], F32, ar)
        flhs = (f_hi, f_lo)
        rows_f = f_hi[:, 0:16, :]
        stg_turned, ep_tap, ep_conv, ep_silu, ep_mul, ep_hi, ep_lo = [sem(n) for n in (
            "chunk_turned", "last_tap", "conv_done", "silu_done", "hidden_done", "hidden_hi", "hidden_lo")]
        ep_n = [0]

        def stage_rows(f, width, stg, norm):
            def ea(e, n):
                e.wait_ge(scaled, norm.ready)
                act_.activation(stg[:, 0, 0:width], acc[0][:, 0:width], f, scale=norm.inv(0)).then_inc(evac[0], 1)

            def ed(e, n, t):
                if f is ACT.Relu:
                    dve_.tensor_scalar(stg[:, t, 0:width], acc[t][:, 0:width], norm.inv(t), 0.0, ALU.mult,
                                       ALU.max).then_inc(evac[t], 1)
                else:
                    dve_.tensor_scalar(stg[:, t, 0:width], acc[t][:, 0:width], norm.inv(t), None,
                                       ALU.mult).then_inc(evac[t], 1)
            return ea, ed

        class Hidden:

            def __init__(self, kind, n, kt0, ct0, tiles, chunk0, bufs):
                self.f_hi, self.f_lo, self.stg, self.sq = bufs
                self.kind, self.kt0, self.ct0, self.tiles, self.chunk0 = kind, kt0, ct0, tiles, chunk0
                self.base = ep_n[0]
                ep_n[0] += n

            def pe(self, e, n):
                i = self.base + n
                for t in range(TT):
                    e.wait_ge(evac[t], self.chunk0 + n + 1)
                if self.base or not isinstance(n, int) or n:
                    e.wait_ge(ep_lo, i)
                nt = self.tiles * (2 if self.kind == "conv" else 1)
                for c in range(nt):
                    for t in range(TT):
                        per = self.tiles if self.kind == "conv" else 2
                        mm = pe_.matmul(wk[c // per][:, (c % per) * S + t * P:(c % per) * S + (t + 1) * P],
                                        self.stg[:, t, c * P:(c + 1) * P], ident[:], start=True, stop=True,
                                        is_transpose=True)
                mm.then_inc(stg_turned, 1)

            def taps(self, n, c):
                return cw[:, bass.ds(self.ct0 + n * self.tiles + c, 1), :].rearrange("p a b -> p (a b)")

            def out(self, a, n):
                return a[:, bass.ds(self.kt0 + n * self.tiles, self.tiles), :]

            def act(self, e, n, part):
                i, k = self.base + n, self.tiles
                if self.kind == "conv":
                    if part == 0:
                        e.wait_ge(stg_turned, i + 1)
                        for c in range(k):
                            w = self.taps(n, c)
                            ins = act_.activation(cv[:, c, :], wk[1][:, c * S:(c + 1) * S], ACT.Identity,
                                                  scale=w[:, 2:3], bias=w[:, 3:4])
                        ins.then_inc(ep_tap, 1)
                    else:
                        e.wait_ge(ep_conv, i + 1)
                        act_.activation(cv[:, 0:k, :], cv[:, 0:k, :], ACT.Silu).then_inc(ep_silu, 1)
                        e.wait_ge(ep_mul, i + 1)
                        act_.activation(self.out(self.f_hi, n), self.sq[:, 0:k, :], ACT.Copy).then_inc(ep_hi, 1)
                elif part == 0:
                    e.wait_ge(stg_turned, i + 1)
                    for b in range(2):
                        act_.activation(self.sq[:, 2 * b:2 * b + 2, :], wk[b][:].rearrange("p (c s) -> p c s", c=2),
                                        ACT.Square)
                    e.drain()
                else:
                    act_.activation(self.out(self.f_hi, n), self.sq[:], ACT.Copy).then_inc(ep_hi, 1)

            def dve(self, e, n, part):
                i, k = self.base + n, self.tiles
                if self.kind == "conv":
                    if part == 0:
                        e.wait_ge(ep_tap, i + 1)
                        for back in (1, 2):
                            for c in range(k):
                                y = cv[:, c, back:S]
                                ins = dve_.scalar_tensor_tensor(
                                    out=y, in0=wk[1][:, c * S:c * S + S - back],
                                    scalar=self.taps(n, c)[:, 2 - back:3 - back], in1=y, op0=ALU.mult, op1=ALU.add)
                            if back == 1:
                                e.drain()
                        ins.then_inc(ep_conv, 1)
                    else:
                        e.wait_ge(ep_silu, i + 1)
                        dve_.tensor_tensor(self.sq[:, 0:k, :], cv[:, 0:k, :],
                                           wk[0][:, 0:k * S].rearrange("p (c s) -> p c s", c=k),
                                           ALU.mult).then_inc(ep_mul, 1)
                if part == 1:
                    e.wait_ge(ep_hi, i + 1)
                    kk = k if self.kind == "conv" else 4
                    dve_.tensor_tensor(self.out(self.f_lo, n), self.sq[:, 0:kk, :], self.out(self.f_hi, n).bitcast(F32),
                                       ALU.subtract).then_inc(ep_lo, 1)

        before_up = len(stages)
        pool_steps.append(lambda e: load(e, "cw", cw[:], t_in["conv1"], after=before_up))

        ffn = stages[-1]

        def up(name, kind, kt0, ct0, tiles, f, width=CH, norm=None, first=False):
            g = Gemm(name, lhs, 0, *stage_rows(f, width, stg, norm.norm))
            g.lhs_from = norm.lhs_from if first else None
            g.needs = "cw" if first and kind == "conv" else None
            g.epi = Hidden(kind, g.n, kt0, ct0, tiles, g.c, (f_hi, f_lo, stg, sq))
            g.unmet = True
            stages.append(g)
            return g

        def down(name, hidden, tiles):
            g = Gemm(name, flhs, 0, *add_to_x())
            g.hidden_from = (hidden.epi.base, tiles)
            stages.append(g)
        hidden = up("up_a", "conv", 0, 0, 2, ACT.Copy, norm=ffn, first=True)
        down("down_a", hidden, 2)
        hidden = up("up_b", "conv", 0, 22, 2, ACT.Copy, norm=ffn)
        up("up_t", "conv", 20, 42, 1, ACT.Copy, CH // 2, norm=ffn)
        down("down_b", hidden, 2)
        ar.close()


        def norm_times(name, row, gain_bc):
            norm = Norm()

            def act(e):
                norm.roots(e, x, lambda t: row)

            def dve(e):
                got(e, name)
                for t in range(TT):
                    norm.inverse(e, t)
                    e.drain()
                    dve_.scalar_tensor_tensor(out=x[:, t, :], in0=x[:, t, :], scalar=norm.inv(t), in1=gain_bc,
                                              op0=ALU.mult, op1=ALU.mult).then_inc(scaled, 1)
            return Steps(name, None, act, dve)

        ar2 = ExitStack()
        oa_hi = sb("oa_hi", [P, 8, S], F32R, ar2)
        oa_lo = sb("oa_lo", [P, 8, S], F32R, ar2)
        sm = sb("sm", [P, 368], F32, ar2)
        gtt = sb("gtt", [8, 2, S], F32, ar2)
        arg = ExitStack()
        pg = sb("pg", [P, TT, 3072], F32, arg)
        arn = ExitStack()
        p2 = sb("p2", [P, TT, P2_N], F32, arn)
        tt2 = sb("tt2", [P, 16, S], F32, arn)
        lp2 = sb("lp2", [P, 4 * TOE], F32, arn)
        misc = sb("misc", [P, 1024], F32, arn)
        l2 = lp2[:, 0:2 * TOE].rearrange("p (a b) -> p a b", a=2)
        pt2 = lp2[:, 2 * TOE:].rearrange("p (a b) -> p a b", a=2)
        tt2f = tt2[:].rearrange("p a b -> p (a b)")

        before_nf = len(stages)
        pool_steps.append(lambda e: load(e, "norm_final", tt2f[:, 0:D], t_in["norm_final"].to_broadcast([P, D]),
                                         after=before_nf))
        p2f = p2[:].rearrange("p a b -> p (a b)")
        stages.append(norm_times("norm_final", p2f[:, 0:D], tt2f[:, 0:D]))
        stages.append(norm_to_lhs("norm_ln1", x, p2f[:, 0:2 * D].rearrange("p (t c) -> p t c", t=TT), h_hi, h_lo,
                                  gains[:, 4, :]))
        x_out = sem("x_spilled")
        x_dram = nc.dram_tensor("x_scratch", (P, TT, D), F32, kind="Internal").ap()
        gate_dram = nc.dram_tensor("gate_scratch", (P, TT, 2 * D), F32, kind="Internal").ap()
        before_spill = len(stages)

        def spill_x(e):
            for k in at_end:
                e.wait_ge(at_end[k], before_spill)
            e.dma_start(x_dram, x[:]).then_inc(x_out, 16)
        pool_steps.append(spill_x)

        def x_gone(e):
            e.wait_ge(x_out, 16)
        spilled = Steps("spill_x", None, x_gone, x_gone)
        ln1 = stages[-1]
        stages.append(Gemm("win2", lhs, 0, *rows_to(p2, norm=ln1.norm)))
        stages[-1].lhs_from = ln1.lhs_from
        stages.append(spilled)

        w_s2 = lp2[:, 0:KD * 40]
        rel_c = lp2[0:REL, 640:648]
        mask_c = lp2[:, 648:678]
        ohc = tt2f[0:REL, 0:N_CMP * S]
        alog = lp2[:, 680:688]
        dtb = lp2[:, 688:696]
        bias_c = misc[:, 0:240]
        srow2, gate3, beta = sm[:, 0:80], sm[:, 80:128], sm[:, 128:144]
        grow, gend, expg, kdec_s, yv, ya = [sm[:, 144 + 16 * k:160 + 16 * k] for k in range(6)]
        s2_mm, s2_row, s2_abs, s2_ln, s2_g, s2_cum, s2_cp = [sem(n) for n in (
            "small2_prod", "small2_rows", "rate_abs", "rate_ln", "log_decays", "decays_summed", "decays_copied")]
        before_s2 = len(stages)

        def small2_pool(e):
            load(e, "w_s2", w_s2, t_in["w_small2"], after=before_s2)
            load(e, "pe_t", pe_t, t_in["pe_t"])
            load(e, "rel_c", rel_c, t_in["rel1"])
            load(e, "mask_c", mask_c, t_in["mask_c"])
            load(e, "ohc", ohc, t_in["onehot_c"])
            load(e, "alog", alog, t_in["a_log"].to_broadcast([P, 8]))
            load(e, "dtb", dtb, t_in["dt_bias"].to_broadcast([P, 8]))
        pool_steps.append(small2_pool)
        pe_t = misc[:, 240:304].rearrange("p (k r) -> p k r", k=2)

        def small2_pe(e):
            e.wait_ge(s2_split, 2)
            small_product(wk[0], ws2_hi, ws2_lo, 40).then_inc(s2_mm, 1)
            got(e, "rel_c")
            got(e, "ohc")
            for t in range(TT):
                for n in range(N_CMP):
                    c = t * 120 + n * 8
                    mm = pe_.matmul(wk[1][:, c:c + 8], ohc[:, n * S + t * P:n * S + (t + 1) * P], rel_c,
                                    start=True, stop=True)
            mm.then_inc(s2_mm, 1)
            yield
            yield
            e.wait_ge(s2_g, 1)
            for t in range(TT):
                g = yv[:, t * 8:t * 8 + 8]
                pe_.matmul(wk[2][0:8, t * P:(t + 1) * P], g, tri[:, 0, 0:P], start=True, stop=True)
                pe_.matmul(wk[3][:, t * 8:t * 8 + 8], tri[:, 0, 0:P], g, start=True, stop=True)
                mm = pe_.matmul(wk[3][:, 16 + t * 8:24 + t * 8], ones[:], g, start=True, stop=True)
            mm.then_inc(s2_cum, 1)
            yield

        ws2_hi = oa_hi[:].rearrange("p a b -> p (a b)")[:, 0:KD * 40]
        ws2_lo = oa_lo[:].rearrange("p a b -> p (a b)")[:, 0:KD * 40]

        def small2_act(e):
            got(e, "w_s2")
            act_.activation(ws2_hi, w_s2, ACT.Copy).then_inc(s2_split, 1)
            e.wait_ge(s2_mm, 1)
            for t in range(TT):
                act_.activation(srow2[:, t * 40:(t + 1) * 40], wk[0][:, t * 40:(t + 1) * 40], ACT.Copy,
                                scale=ln1.norm.inv(t))
            e.drain()
            r = srow2.rearrange("p (t c) -> p t c", t=TT)
            act_.activation(gate3.rearrange("p (t c) -> p t c", t=TT), r[:, :, 0:24], ACT.Sigmoid)
            act_.activation(beta.rearrange("p (t c) -> p t c", t=TT), r[:, :, 32:40], ACT.Sigmoid).then_inc(s2_row, 1)
            yield
            got(e, "alog")
            act_.activation(alog, alog, ACT.Exp)
            e.wait_ge(s2_abs, 1)
            act_.activation(ya, ya, ACT.Exp)
            e.drain()
            act_.activation(ya, ya, ACT.Ln, bias=ones[:, 0:1]).then_inc(s2_ln, 1)
            yield
            e.wait_ge(s2_cum, 1)
            act_.activation(gtt[:, 0, :], wk[2][0:8, 0:S], ACT.Copy)
            act_.activation(gtt[:, 1, :], wk[2][0:8, 0:S], ACT.Copy, scale=-1.0)
            act_.activation(sm[:, 144:176], wk[3][:, 0:32], ACT.Copy)
            e.drain()
            act_.activation(expg, grow, ACT.Exp).then_inc(s2_cp, 1)
            e.wait_ge(s2_cp, 2)
            act_.activation(kdec_s, kdec_s, ACT.Exp)
            yield

        def small2_dve(e):
            e.wait_ge(s2_split, 1)
            dve_.tensor_tensor(ws2_lo, w_s2, ws2_hi.bitcast(F32), ALU.subtract).then_inc(s2_split, 1)
            e.wait_ge(s2_row, 1)
            got(e, "dtb")
            yield
            for t in range(TT):
                dve_.tensor_tensor(yv[:, t * 8:t * 8 + 8], srow2[:, t * 40 + 24:t * 40 + 32], dtb, ALU.add)
            e.drain()
            dve_.scalar_tensor_tensor(out=ya, in0=yv, scalar=-1.0, in1=yv, op0=ALU.mult, op1=ALU.min).then_inc(s2_abs, 1)
            e.drain()
            dve_.tensor_scalar(yv, yv, 0.0, None, ALU.max)
            e.drain()
            e.wait_ge(s2_ln, 1)
            dve_.tensor_tensor(yv, yv, ya, ALU.add)
            e.drain()
            for t in range(TT):
                ins = dve_.scalar_tensor_tensor(out=yv[:, t * 8:t * 8 + 8], in0=yv[:, t * 8:t * 8 + 8], scalar=-1.0,
                                                in1=alog, op0=ALU.mult, op1=ALU.mult)
            ins.then_inc(s2_g, 1)
            yield
            got(e, "mask_c")
            e.wait_ge(s2_mm, 2)
            for h in range(N_H):
                b = bias_c[:, h * 30:(h + 1) * 30].rearrange("p (t n) -> p t n", t=TT)
                ps = wk[1][:, 0:240].rearrange("p (t n h) -> p t n h", t=TT, h=8)[:, :, :, h]
                dve_.tensor_tensor(b, ps, mask_c.rearrange("p (t n) -> p t n", t=TT), ALU.add)
            e.wait_ge(s2_cp, 1)
            dve_.tensor_tensor(kdec_s, gend, grow, ALU.subtract).then_inc(s2_cp, 1)
            yield
        small2 = Steps("small2", small2_pe, small2_act, small2_dve, 3)

        turn2 = Steps("turn2", *to_tiles([
            ((lambda t, i=i: p2[:, t, i * P:(i + 1) * P]), tt2[:, i, :]) for i in range(16)]))
        after_turn2 = len(stages) + 1

        def bias2(h):
            return p2[:, h // 4, (h % 4) * TOE:(h % 4 + 1) * TOE]
        pe_t = misc[:, 240:304].rearrange("p (k r) -> p k r", k=2)
        w2c = p2[:, 0, 4 * TOE:2048].rearrange("p (k a c) -> p k a c", k=2, a=2)
        hc = p2[0:30, 1, 4 * TOE:2048].rearrange("p (k c) -> p k c", k=2)
        h_t = misc[:, 304:424].rearrange("p (k a c) -> p k a c", k=2, a=2)
        kc_t = misc[:, 424:454]
        vc_r = misc[0:N_CMP, 512:768].rearrange("p (g c) -> p g c", g=2)

        def nsa_pool(e):
            load(e, "w2c", w2c, t_in["w2c"], after=after_turn2)
            toeplitz(e, "bias2", bias2, toe2, N_H, after_turn2)
        pool_steps.append(nsa_pool)

        flat_hi = oa_hi[:].rearrange("p a b -> p (a b)")
        flat_lo = oa_lo[:].rearrange("p a b -> p (a b)")
        FW = 960
        f_sum, f_hi_s = sem("flat_sum"), sem("flat_hi")

        def flat_dve(e):
            got(e, "pe_t")
            dve_.memset(lp2[:, 0:4 * TOE], 0.0)
            e.drain()
            for k in range(2):
                if k:
                    e.wait_ge(f_hi_s, 2 * k)
                f = lp2[:, 0:FW].rearrange("p (r g n) -> p r g n", r=32, g=2)
                a = tt2[:, 8 + 2 * k:10 + 2 * k, :].rearrange("p g (n r) -> p r g n", r=CSTR)
                for hf in range(2):
                    pe4 = pe_t[:, k, hf * 16:(hf + 1) * 16].unsqueeze(2).unsqueeze(3).to_broadcast([P, 16, 2, N_CMP])
                    for g in range(2):
                        ins = dve_.tensor_tensor(f[:, hf * 16:(hf + 1) * 16, g, :], a[:, :, g, hf:hf + N_CMP],
                                                 pe4[:, :, g, :], ALU.add)
                ins.then_inc(f_sum, 1)
                e.wait_ge(f_hi_s, 2 * k + 1)
                dve_.tensor_tensor(flat_lo[:, k * FW:(k + 1) * FW], lp2[:, 0:FW],
                                   flat_hi[:, k * FW:(k + 1) * FW].bitcast(F32), ALU.subtract)
                e.drain()
                e.sem_inc(f_hi_s, 1)
            dve_.tensor_copy(flat_lo[:, 2 * FW:2048], lp2[:, 1100:1100 + 2048 - 2 * FW])

        def flat_act(e):
            for k in range(2):
                e.wait_ge(f_sum, k + 1)
                act_.activation(flat_hi[:, k * FW:(k + 1) * FW], lp2[:, 0:FW], ACT.Copy).then_inc(f_hi_s, 1)
            act_.activation(flat_hi[:, 2 * FW:2048], lp2[:, 1100:1100 + 2048 - 2 * FW], ACT.Copy)
        z_rows = x[:, :, 0:1024]
        stages.append(Together("small2+z", [Gemm("z", lhs, 0, *rows_to(z_rows, norm=ln1.norm))], [
            small2, turn2, Steps("flat", None, flat_act, flat_dve)]))

        class Compress(Gemm):

            def tile(self, a, kt, t):
                c = self.kt0 + kt * 30
                return a[:, c:c + P]

        for k, name in enumerate(("cmp_k", "cmp_v")):
            def ed(e, n, t, k=k):
                if t == 0:
                    e.sem_inc(evac[0], 1)
                else:
                    dve_.tensor_copy(hc[:, k, :], acc[1][0:30, 0:CHID]).then_inc(evac[1], 1)
            g = Compress(name, (flat_hi, flat_lo), k * FW, None, ed)
            g.tiles = range(1, 2)
            stages.append(g)
        c_act, c_tr, c_ht, c_mm = [sem(n) for n in ("cmp_gelu", "cmp_turned", "cmp_hidden", "cmp_out")]

        def cmp_act(e):
            act_.activation(hc, hc, ACT.Gelu_apprx_tanh).then_inc(c_act, 1)
            e.wait_ge(c_tr, 1)
            act_.activation(h_t.rearrange("p k a c -> p (k a c)"), wk[0][:, 0:120], ACT.Copy).then_inc(c_ht, 1)
            e.wait_ge(c_mm, 1)
            act_.activation(kc_t, wk[1][:, 0:30], ACT.Copy)
            act_.activation(vc_r, wk[2][0:N_CMP, 0:256].rearrange("p (g c) -> p g c", g=2), ACT.Copy)

        def cmp_pe(e):
            e.wait_ge(c_act, 1)
            for k in range(2):
                for a in range(2):
                    c = (2 * k + a) * 30
                    mm = pe_.matmul(wk[0][:, c:c + 30], hc[:, k, a * P:(a + 1) * P], ident[0:30, 0:30],
                                    start=True, stop=True, is_transpose=True)
            mm.then_inc(c_tr, 1)
            e.wait_ge(c_ht, 1)
            got(e, "w2c")
            for a in range(2):
                pe_.matmul(wk[1][:, 0:30], w2c[:, 0, a, :], h_t[:, 0, a, :], start=a == 0, stop=a == 1)
            for g in range(2):
                for a in range(2):
                    mm = pe_.matmul(wk[2][0:N_CMP, g * P:(g + 1) * P], h_t[:, 1, a, g * N_CMP:(g + 1) * N_CMP],
                                    w2c[:, 1, a, :], start=a == 0, stop=a == 1)
            mm.then_inc(c_mm, 1)
        stages.append(Steps("compress", cmp_pe, cmp_act, None))

        def branch(h, i):
            g = h // 4
            q = tt2[:, h, :]

            def gate(qt):
                return gate3[:, qt * 24 + h * 3 + i:qt * 24 + h * 3 + i + 1]
            kw = dict(gate=gate, first=i == 0, last=i == 2, hi=oa_hi[:, h, :], lo=oa_lo[:, h, :])
            if i == 0:
                return Unit(q, kc_t[:, g * N_CMP:(g + 1) * N_CMP], lambda kt: vc_r[:, g, :], [(0, [0]), (1, [0])],
                            N_D ** -0.5, bias_c[:, h * 30:(h + 1) * 30], kw=N_CMP, **kw)
            v = (P2_VS, P2_VW)[i - 1] + g * P
            return Unit(q, tt2[:, (12, 14)[i - 1] + g, :], lambda kt: p2[:, kt, v:v + P], CAUSAL, N_D ** -0.5,
                        bias2(h), **kw)

        def bias2_there(e):
            e.wait_ge(landed["bias2"], 16 * 2 * N_H)
        stages.append(Together("nsa+win2g", [Gemm("win2g", lhs, 0, *rows_to(pg, norm=ln1.norm))], [
            attention("attention_nsa", [branch(h, i) for h in range(N_H) for i in range(3)], l2, pt2, bias2_there)]))
        arn.close()

        argt = ExitStack()
        tg = sb("tg", [P, 24, S], F32, argt)
        wg = sb("wg", [P, 11, 512], F32, argt)
        cw2 = sb("cw2", [P, 24, 4], F32, argt)
        cmt = sb("cmt", [P, 2, P], F32, argt)
        wgf = wg[:].rearrange("p a b -> p (a b)")
        lmask2 = tg[:, 16:20, :].rearrange("p a b -> p (a b)").rearrange("p (l i) -> p l i", l=8)
        before_conv = len(stages) - 1

        def conv_pool(e):
            load(e, "cw2", cw2[:], t_in["conv2"], after=before_conv)
            load(e, "cmt", cmt[:], t_in["cmt"])
        pool_steps.append(conv_pool)
        v_tr, v_first, v_done = sem("qkv_turned"), sem("conv_first"), sem("conv_all")

        def conv_pe(e):
            for i in range(24):
                if i >= 4:
                    e.wait_ge(v_done, i - 3)
                for t in range(TT):
                    mm = pe_.matmul(wk[i % 4][:, t * P:(t + 1) * P], pg[:, t, i * P:(i + 1) * P], ident[:],
                                    start=True, stop=True, is_transpose=True)
                mm.then_inc(v_tr, 1)
                if i % 2:
                    yield
            yield

        def conv_act(e):
            got(e, "cw2")
            for i in range(26):
                if i < 24:
                    e.wait_ge(v_tr, i + 1)
                    act_.activation(tg[:, i, :], wk[i % 4][:, 0:S], ACT.Copy, scale=cw2[:, i, 3:4]).then_inc(v_first, 1)
                if i % 6 == 1 and i > 6:
                    k = i // 6 - 1
                    e.wait_ge(v_done, 6 * k + 6)
                    act_.activation(tg[:, 6 * k:6 * k + 6, :], tg[:, 6 * k:6 * k + 6, :], ACT.Silu)
                if i % 2:
                    yield

        def conv_dve(e):
            got(e, "cw2")
            for i in range(0, 24, 2):
                for k in range(2):
                    e.wait_ge(v_first, i + k + 1)
                for d in range(1, 4):
                    for k in range(2):
                        a = tg[:, i + k, d:S]
                        ins = dve_.scalar_tensor_tensor(out=a, in0=wk[(i + k) % 4][:, 0:S - d],
                                                        scalar=cw2[:, i + k, 3 - d:4 - d], in1=a, op0=ALU.mult,
                                                        op1=ALU.add)
                        if d == 3:
                            ins.then_inc(v_done, 1)
                    if d < 3:
                        e.drain()
                yield
            yield
        gdn = [Steps("conv2", conv_pe, conv_act, conv_dve, 13)]
        gdn.append(Steps("rows2", *to_tiles([
            ((lambda t, i=i: tg[:, i, t * P:(t + 1) * P]), pg[:, :, i * P:(i + 1) * P]) for i in range(24)])))

        n_sq, n_rt, n_qk = sem("qk_squared"), sem("qk_root"), sem("qk_unit")
        ssn, rtn = sm[:, 256:288], sm[:, 288:320]

        def heads_of(a, t, c0, n):
            return a[:, t, c0:c0 + n * P].rearrange("p (h c) -> p h c", c=P)

        def per_head(v, n):
            return v.unsqueeze(2).to_broadcast([P, n, P])

        def unit_act(e):
            for t in range(TT):
                act_.activation(wgf[:, t * 2048:(t + 1) * 2048], pg[:, t, 0:2048], ACT.Square).then_inc(n_sq, 1)
            e.wait_ge(n_rt, 1)
            act_.activation(ssn, ssn, ACT.Sqrt, bias=eps_c[:]).then_inc(n_rt, 1)

        def unit_dve(e):
            for t in range(TT):
                e.wait_ge(n_sq, t + 1)
                ins = dve_.tensor_reduce(ssn[:, t * 16:(t + 1) * 16],
                                         wgf[:, t * 2048:(t + 1) * 2048].rearrange("p (h c) -> p h c", c=P), AX.X,
                                         ALU.add)
            ins.then_inc(n_rt, 1)
            e.wait_ge(n_rt, 2)
            dve_.reciprocal(rtn, ssn)
            e.drain()
            for t in range(TT):
                dve_.tensor_scalar(rtn[:, t * 16:t * 16 + 8], rtn[:, t * 16:t * 16 + 8], G_D ** -0.5, None, ALU.mult)
            e.drain()
            for t in range(TT):
                a = heads_of(pg, t, 0, 16)
                dve_.tensor_tensor(a, a, per_head(rtn[:, t * 16:(t + 1) * 16], 16), ALU.mult)
                b = heads_of(pg, t, 2048, 8)
                dve_.tensor_tensor(b, b, per_head(beta[:, t * 8:t * 8 + 8], 8), ALU.mult)
        gdn.append(Steps("unit2", None, unit_act, unit_dve))
        after_conv = {k: fences[0] + 2 for k in fenced}
        gdn.append(Steps("turn_qk", *to_tiles([
            ((lambda t, i=i: pg[:, t, i * P:(i + 1) * P]), tg[:, i, :]) for i in range(16)])))

        def lmask_pool(e):
            for k, n in after_conv.items():
                e.wait_ge(fenced[k], n)
            load(e, "lmask2", lmask2, t_in["lmask"])
        pool_steps.append(lmask_pool)

        def rates_dve(e):
            be = sm[:, 320:336]
            dve_.tensor_tensor(be, beta, expg, ALU.mult)
            e.drain()
            for t in range(TT):
                dve_.tensor_tensor(heads_of(pg, t, 0, 8), heads_of(pg, t, 1024, 8),
                                   per_head(be[:, t * 8:t * 8 + 8], 8), ALU.mult)
            e.drain()
            k0 = heads_of(pg, 0, 1024, 8)
            dve_.tensor_tensor(k0, k0, per_head(kdec_s[:, 0:8], 8), ALU.mult)
            got(e, "lmask2")
            got(e, "cmt")
        gdn.append(Steps("rates", None, None, rates_dve))

        NL = 7
        d_e, d_m, d_x, d_l, d_lt, d_ltc, d_qk, d_c, d_M, d_Mc, d_T, d_Tc, d_at = [sem("delta_" + n) for n in (
            "exponents", "masked", "decays", "gram_scaled", "l_turned", "l_copied", "scores", "level", "m",
            "m_copied", "t", "t_copied", "scores_done")]

        def w4(i):
            return wg[:, i, :].rearrange("p (h c) -> p h c", h=4)
        LT, TM, TR, MM, CT = [[w4(2 * i), w4(2 * i + 1)] for i in range(5)]
        DD = w4(10)
        at_f = tg[:, 20:24, :].rearrange("p a b -> p (a b)")
        AT = [at_f[:, t * 512:(t + 1) * 512].rearrange("p (h c) -> p h c", h=4) for t in range(2)]
        bank4 = [b[:].rearrange("p (h c) -> p h c", h=4) for b in wk]

        def q_t(h, t):
            return tg[:, h, t * P:(t + 1) * P]

        def k_t(h, t):
            return tg[:, 8 + h, t * P:(t + 1) * P]

        def delta(b):
            hs = range(4 * b, 4 * b + 4)
            z4, z2, zl = 4 * b, 2 * b, 2 * NL * b

            def pe(e):
                for t in range(TT):
                    for o in range(2):
                        for j, h in enumerate(hs):
                            one = ident[0:8, h:h + 1].to_broadcast([8, P])
                            gc, gn = gtt[:, 0, t * P:(t + 1) * P], gtt[:, 1, t * P:(t + 1) * P]
                            bb = bank4[2 * t + o][:, j, :]
                            pe_.matmul(bb, *((one, gc) if o == 0 else (gc, one)), start=True, stop=False)
                            mm = pe_.matmul(bb, *((gn, one) if o == 0 else (one, gn)), start=False, stop=True)
                        mm.then_inc(d_e, 1)
                yield
                for t in range(TT):
                    for o in range(2):
                        if o == 0:
                            bk = bank4[4]
                            if t:
                                e.wait_ge(d_at, z2 + t)
                        else:
                            bk = bank4[5]
                            if t:
                                e.wait_ge(d_l, z2 + t)
                        for j, h in enumerate(hs):
                            mm = pe_.matmul(bk[:, j, :], k_t(h, t), (q_t, k_t)[o](h, t), start=True, stop=True)
                        mm.then_inc(d_qk, 1)
                yield
                for t in range(TT):
                    e.wait_ge(d_l, z2 + t + 1)
                    for j in range(4):
                        mm = pe_.matmul(bank4[2 * t][:, j, :], LT[t][:, j, :], ident[:], start=True, stop=True,
                                        is_transpose=True)
                    mm.then_inc(d_lt, 1)
                yield
                for l in range(NL):
                    for t in range(TT):
                        e.wait_ge(d_c, zl + 2 * l + t + 1)
                        if l:
                            e.wait_ge(d_Tc, zl + 2 * (l - 1) + t + 1)
                        for j in range(4):
                            mm = pe_.matmul(bank4[t][:, j, :], CT[t][:, j, :], TM[t][:, j, :], start=True, stop=True)
                        mm.then_inc(d_M, 1)
                    yield
                    for t in range(TT):
                        e.wait_ge(d_Mc, zl + 2 * l + t + 1)
                        if l < NL - 1:
                            for j in range(4):
                                pe_.matmul(bank4[2 + t][:, j, :], TR[t][:, j, :], MM[t][:, j, :], start=True, stop=True)
                        for j in range(4):
                            mm = pe_.matmul(bank4[4 + t][:, j, :], MM[t][:, j, :], TR[t][:, j, :], start=True, stop=True)
                        mm.then_inc(d_T, 1)
                    yield

            def act(e):
                for t in range(TT):
                    for o in range(2):
                        e.wait_ge(d_m, z4 + 2 * t + o + 1)
                        a = AT[t] if o == 0 else LT[t]
                        act_.activation(a, a, ACT.Exp).then_inc(d_x, 1)
                yield
                yield
                for t in range(TT):
                    e.wait_ge(d_lt, z2 + t + 1)
                    act_.activation(LT[t], bank4[2 * t], ACT.Copy).then_inc(d_ltc, 1)
                yield
                for l in range(NL):
                    for t in range(TT):
                        e.wait_ge(d_M, zl + 2 * l + t + 1)
                        act_.activation(MM[t], bank4[t], ACT.Copy).then_inc(d_Mc, 1)
                    yield
                    yield

            def dve(e):
                for t in range(TT):
                    for o in range(2):
                        e.wait_ge(d_e, z4 + 2 * t + o + 1)
                        dve_.tensor_tensor(AT[t] if o == 0 else LT[t], bank4[2 * t + o], bc(cmt[:, o, :], 4),
                                           ALU.add).then_inc(d_m, 1)
                for t in range(TT):
                    dve_.tensor_copy(TM[t], bc(ident[:], 4))
                    dve_.tensor_copy(TR[t], bc(ident[:], 4))
                yield
                for t in range(TT):
                    e.wait_ge(d_qk, z4 + 2 * t + 2)
                    e.wait_ge(d_x, z4 + 2 * t + 2)
                    dve_.tensor_tensor(AT[t], bank4[4], AT[t], ALU.mult).then_inc(d_at, 1)
                    for j, h in enumerate(hs):
                        ins = dve_.scalar_tensor_tensor(out=LT[t][:, j, :], in0=bank4[5][:, j, :],
                                                        scalar=beta[:, t * 8 + h:t * 8 + h + 1], in1=LT[t][:, j, :],
                                                        op0=ALU.mult, op1=ALU.mult)
                    ins.then_inc(d_l, 1)
                yield

                def level(l, t):
                    if l:
                        e.wait_ge(d_M, zl + 2 * (l - 1) + t + 1)
                    dve_.tensor_tensor(CT[t], LT[t], bc(lmask2[:, l, :], 4), ALU.mult).then_inc(d_c, 1)
                for t in range(TT):
                    e.wait_ge(d_ltc, z2 + t + 1)
                    level(0, t)
                yield
                for l in range(NL):
                    for t in range(TT):
                        if l < NL - 1:
                            level(l + 1, t)
                    yield
                    for t in range(TT):
                        e.wait_ge(d_T, zl + 2 * l + t + 1)
                        if l < NL - 1:
                            dve_.tensor_tensor(TM[t], TM[t], bank4[2 + t], ALU.subtract)
                        dve_.tensor_tensor(TR[t], TR[t], bank4[4 + t], ALU.subtract).then_inc(d_Tc, 1)
                    yield
            return Steps(f"delta{b}", pe, act, dve, 3 + 2 * NL)

        y_u0, y_u0c, y_s1, y_s1c, y_w, y_wc, y_v1, y_v1c, y_o = [sem("state_" + n) for n in (
            "u", "u_copied", "sum", "sum_copied", "w", "w_copied", "v", "v_copied", "out")]

        def state(b):
            hs = list(enumerate(range(4 * b, 4 * b + 4)))
            V0, V1, S1, WT = MM[0], MM[1], LT[0], TM[0]

            def rows_(c0, h, t):
                return pg[:, t, c0 + h * P:c0 + (h + 1) * P]

            def pe(e):
                for j, h in hs:
                    mm = pe_.matmul(bank4[0][:, j, :], TR[0][:, j, :], rows_(2048, h, 0), start=True, stop=True)
                mm.then_inc(y_u0, 1)
                for j, h in hs:
                    mm = pe_.matmul(bank4[1][:, j, :], rows_(0, h, 1), TR[1][:, j, :], start=True, stop=True)
                mm.then_inc(y_w, 1)
                yield
                e.wait_ge(y_u0c, b + 1)
                for j, h in hs:
                    mm = pe_.matmul(bank4[2][:, j, :], rows_(1024, h, 0), V0[:, j, :], start=True, stop=True)
                mm.then_inc(y_s1, 1)
                for j, h in hs:
                    pe_.matmul(bank4[3][:, j, :], AT[0][:, j, :], V0[:, j, :], start=True, stop=True)
                yield
                e.wait_ge(y_wc, b + 1)
                e.wait_ge(y_s1c, b + 1)
                for j, h in hs:
                    pe_.matmul(bank4[4][:, j, :], TR[1][:, j, :], rows_(2048, h, 1), start=True, stop=False)
                    mm = pe_.matmul(bank4[4][:, j, :], WT[:, j, :], S1[:, j, :], start=False, stop=True)
                mm.then_inc(y_v1, 1)
                yield
                for j, h in hs:
                    pe_.matmul(bank4[5][:, j, :], q_t(h, 1), S1[:, j, :], start=True, stop=True)
                e.wait_ge(y_v1c, b + 1)
                for j, h in hs:
                    mm = pe_.matmul(bank4[0][:, j, :], AT[1][:, j, :], V1[:, j, :], start=True, stop=True)
                mm.then_inc(y_o, 1)
                yield

            def act(e):
                e.wait_ge(y_u0, b + 1)
                act_.activation(V0, bank4[0], ACT.Copy).then_inc(y_u0c, 1)
                yield
                e.wait_ge(y_s1, b + 1)
                act_.activation(S1, bank4[2], ACT.Copy).then_inc(y_s1c, 1)
                yield
                e.wait_ge(y_v1, b + 1)
                act_.activation(V1, bank4[4], ACT.Copy).then_inc(y_v1c, 1)
                yield
                e.wait_ge(y_o, 2 * b + 1)
                act_.activation(heads_of(pg, 0, 2048 + 512 * b, 4), bank4[3], ACT.Copy)
                act_.activation(heads_of(pg, 1, 2048 + 512 * b, 4), bank4[0], ACT.Copy).then_inc(y_o, 1)
                yield

            def dve(e):
                e.wait_ge(y_w, b + 1)
                dve_.tensor_scalar(WT, bank4[1], -1.0, None, ALU.mult).then_inc(y_wc, 1)
                yield
                yield
                yield
                e.wait_ge(y_o, 2 * b + 2)
                for j, h in hs:
                    o = pg[:, 1, 2048 + h * P:2048 + (h + 1) * P]
                    dve_.scalar_tensor_tensor(out=o, in0=bank4[5][:, j, :], scalar=expg[:, 8 + h:9 + h], in1=o,
                                              op0=ALU.mult, op1=ALU.add)
                yield
            return Steps(f"state{b}", pe, act, dve, 4)
        for b in range(2):
            gdn += [delta(b), state(b)]

        gates_out = [sem("gates_out0"), sem("gates_out1")]

        def gate_ea(e, n, t):
            if n >= 2 and t == 0:
                e.wait_ge(gates_out[n % 2], 16 * (n // 2))
            act_.activation(x[:, t, 1024 + (n % 2) * CH:1024 + (n % 2 + 1) * CH], acc[t][:],
                            ACT.Sigmoid, scale=ln1.norm.inv(t)).then_inc(evac[t], 1)
        merge = Gemm("merge", lhs, 0, gate_ea, None)
        merge.both_act = True
        stages.append(Together("gdn+merge", [merge], gdn))

        def gates_pool(e):
            for n in range(merge.n):
                for t in range(TT):
                    e.wait_ge(evac[t], merge.c + n + 1)
                e.dma_start(gate_dram[:, :, n * CH:(n + 1) * CH],
                            x[:, :, 1024 + (n % 2) * CH:1024 + (n % 2 + 1) * CH]).then_inc(gates_out[n % 2], 16)
        pool_steps.append(gates_pool)
        argt.close()

        ob_hi = sb("ob_hi", [P, 8, S], F32R, arg)
        ob_lo = sb("ob_lo", [P, 8, S], F32R, arg)
        gm = sb("gm", [P, TT, 2 * D], F32, arg)
        gn_bc = tri[:, 0, 0:P]
        after_gdn = len(stages)

        def gates_back(e):
            load(e, "gn", gn_bc, t_in["gdn_norm"].to_broadcast([P, P]), after=after_gdn)
            for p in gates_out:
                e.wait_ge(p, 16 * merge.n // 2)
            load(e, "gates", gm[:], gate_dram)
        pool_steps.append(gates_back)
        o_sq, o_rt = sem("delta_squared"), sem("delta_root")
        sso, rto = sm[:, 336:352], sm[:, 352:368]

        def gnorm_act(e):
            for t in range(TT):
                act_.activation(pg[:, t, 1024:2048], pg[:, t, 2048:3072], ACT.Square).then_inc(o_sq, 1)
            act_.activation(pg[:, :, 0:1024], z_rows, ACT.Silu)
            e.wait_ge(o_rt, 1)
            act_.activation(sso, sso, ACT.Sqrt, scale=1.0 / G_D, bias=eps_c[:]).then_inc(o_rt, 1)

        def gnorm_dve(e):
            got(e, "gn")
            for t in range(TT):
                e.wait_ge(o_sq, t + 1)
                ins = dve_.tensor_reduce(sso[:, t * 8:(t + 1) * 8], heads_of(pg, t, 1024, 8), AX.X, ALU.add)
            ins.then_inc(o_rt, 1)
            e.wait_ge(o_rt, 2)
            dve_.reciprocal(rto, sso)
            for t in range(TT):
                z = heads_of(pg, t, 0, 8)
                dve_.tensor_tensor(z, z, bc(gn_bc, 8), ALU.mult)
            e.drain()
            for t in range(TT):
                o = heads_of(pg, t, 2048, 8)
                dve_.tensor_tensor(o, o, per_head(rto[:, t * 8:(t + 1) * 8], 8), ALU.mult)
            e.drain()
            for t in range(TT):
                o = heads_of(pg, t, 2048, 8)
                dve_.tensor_tensor(o, o, heads_of(pg, t, 0, 8), ALU.mult)
        gnorm = Steps("gnorm", None, gnorm_act, gnorm_dve)
        turn_ob = Steps("turn_ob", *to_lhs(lambda t, i: pg[:, t, 2048 + i * P:2048 + (i + 1) * P], 8, ob_hi, ob_lo))

        def pa_ed(e, n, t):
            if n == 0 and t == 0:
                got(e, "gates")
            g = gm[:, t, n * CH:(n + 1) * CH]
            dve_.tensor_tensor(g, acc[t][:], g, ALU.mult).then_inc(evac[t], 1)

        def pb_ed(e, n, t):
            g, a = gm[:, t, D + n * CH:D + (n + 1) * CH], gm[:, t, n * CH:(n + 1) * CH]
            dve_.tensor_tensor(g, acc[t][:], g, ALU.mult).then_inc(evac[t], 1)
            e.drain()
            dve_.tensor_tensor(a, a, g, ALU.add)
        stages.append(Together("pa+gnorm", [Gemm("pa", (oa_hi, oa_lo), 0, None, pa_ed)], [gnorm, turn_ob]))
        after_pa = len(stages)
        pool_steps.append(lambda e: load(e, "x_back2", x[:], x_dram, after=after_pa))
        stages.append(Gemm("pb", (ob_hi, ob_lo), 0, None, pb_ed))
        turn_m = turn("turn_m", lambda t, i: gm[:, t, i * P:(i + 1) * P], KD, h_hi, h_lo)
        stages.append(turn_m)
        stages.append(Steps("x_back2", None, None, lambda e: got(e, "x_back2")))
        stages[-1].unmet = True
        stages.append(Gemm("wo", lhs, 0, *add_to_x()))
        stages[-1].lhs_from = turn_m.lhs_from
        stages.append(norm_to_lhs("norm_ln2", x, gm[:, :, 0:D], h_hi, h_lo, gains[:, 5, :]))
        ln2 = stages[-1]
        arg.close()
        ar2.close()

        before_f2 = len(stages)
        arf = ExitStack()
        f_hi = sb("f2_hi", [P, 32, S], F32R, arf)
        f_lo = sb("f2_lo", [P, 32, S], F32R, arf)
        stg = sb("stg2", [P, TT, CH], F32, arf)
        sq = sb("sq2", [P, 4, S], F32, arf)
        flhs = (f_hi, f_lo)
        for half_ in ("a", "b"):
            hidden = up("up2_" + half_, "square", 0, 0, 4, ACT.Relu, norm=ln2, first=half_ == "a")
            down("down2_" + half_, hidden, 4)
        fin = ExitStack()
        row_f = sb("row_f", [P, D], F32, fin)
        gain_f = sb("gain_f", [P, D], F32, fin)
        pool_steps.append(lambda e: load(e, "norm_out", gain_f[:], t_in["ln_f"].to_broadcast([P, D]),
                                         after=before_f2))
        stages.append(norm_times("norm_out", row_f[:], gain_f[:]))
        OUT = x[:]
        fin.close()
        arf.close()

        out_done = sem("out_done")
        block = ctx.enter_context(nc.Block())

        @block.sync
        def _(e):
            load(e, "x", x[:], t_in["x"])
            load(e, "gains", gains[:], t_in["gains"])
            load(e, "ident", ident[:], t_in["ident"])
            for g in Gemm.every:
                g.load(e)

        @block.gpsimd
        def _(e):
            for f in pool_steps:
                f(e)
            for k in at_end:
                e.wait_ge(at_end[k], len(stages))
            e.dma_start(out, OUT).then_inc(out_done, 16)
            e.wait_ge(out_done, 16)

        def program(e, k):
            for i, s in enumerate(stages):
                s.run(k, e)
                stage_end(e, k, i, s)

        @block.tensor
        def _(e):
            program(e, "pe")

        @block.scalar
        def _(e):
            program(e, "act")

        @block.vector
        def _(e):
            program(e, "dve")


def layout(i):
    f = np.float32
    a = {}

    def cols(w, order):
        return np.concatenate([w[:, s:s + n] for s, n in order], axis=1)

    def weights(name, w):
        _, n, kts, width = {s[0]: s for s in gemm_specs()}[name]
        K = sum(kts)
        assert w.shape == (K * P, n * width), (name, w.shape)
        t = w.reshape(K, P, n, width).transpose(2, 1, 0, 3)
        o = np.zeros((n, len(kts), P, ITEM), f)
        k0 = 0
        for j, k in enumerate(kts):
            o[:, j, :, 0:k * width] = t[:, :, k0:k0 + k].reshape(n, P, k * width)
            k0 += k
        a["w_" + name] = o.reshape(n * len(kts), P, ITEM)

    def rows(m):
        return np.ascontiguousarray(m.reshape(TT, P, -1).transpose(1, 0, 2))

    def lanes(v):
        return np.ascontiguousarray(v.reshape(-1, P).T)

    w = i["w_in"][0]
    o = np.cumsum([0, 768, 768, 768, 512, 512, 512, 8, 384, 384, 768, 768, 16])
    qa, ka, va, qb, kb, vb, fl, qc, kc, vc, rc, gl = o[:12].tolist()
    first = cols(w, [(qa, 768), (ka, 768), (qb, 512), (kb, 512), (va, 768), (vb, 512), (qc, 384), (kc, 384),
                     (vc, 768), (rc, 768)])
    weights("win", first[:, 0:8 * CH])
    weights("winc", first[:, 8 * CH:])
    a["w_small1"] = cols(w, [(fl, 8), (gl, 16)]).reshape(KD, P, 24).transpose(1, 0, 2).reshape(P, KD * 24).copy()
    weights("wout", i["w_out"][0])
    weights("ckv", i["w_ckv"][0])
    weights("cq", i["w_cq"][0])
    weights("co", i["w_co"][0])
    up, dn = i["w_up"][0], i["w_down"][0]

    def pairs(c0, n, tiles):
        return cols(up, [s for c in range(n) for s in ((P * (c0 + c * tiles), P * tiles),
                                                       (FF1 + P * (c0 + c * tiles), P * tiles))])
    weights("up_a", pairs(0, 11, 2))
    weights("up_b", pairs(22, 10, 2))
    weights("up_t", pairs(42, 1, 1))
    weights("down_a", dn[0:22 * P])
    weights("down_b", dn[22 * P:])
    a["x"] = rows(i["x"][0])
    a["mem"] = rows(i["mem"][0])
    a["gains"] = np.stack([lanes(i["norm_mix"][0]), lanes(i["mem_norm"]), lanes(i["norm_cross"][0]),
                           lanes(i["norm_ffn"][0]), lanes(i["ln1_w_2"][0]),
                           lanes(i["ln2_w_2"][0])], axis=1).copy()
    a["c_gate_w2"] = i["c_gate_w2"][0]
    a["c_gate_b"] = i["c_gate_b"]
    a["f_bias"] = i["f_bias"]
    a["c_norm"] = i["c_norm"]
    a["conv1"] = np.stack([lanes(i["conv_w"][0][0]), lanes(i["conv_w"][0][1]), lanes(i["conv_w"][0][2]),
                           lanes(i["conv_b"][0])], axis=2).copy()
    a["rel0"] = i["rel_table"]
    a["rel1"] = i["rel_table_2"]
    a["ident"] = np.eye(P, dtype=f)
    tok = np.arange(S)
    a["tri"] = rows((tok[:, None] <= tok[None, :]).astype(f))
    d = 255 - np.arange(TOE)

    def bucket(dist, far):
        n = np.maximum(dist, 1).astype(f)
        large = 16 + (np.log(n / 16) / np.float32(np.log(far / 16)) * 16).astype(np.int32)
        return np.where(dist < 16, np.maximum(dist, 0), np.minimum(large, 31))
    count = (d <= 128) * 1 + (d % 4 == 0) * 1 + (d % 16 == 0) * 1
    ok = (d >= 0) & (count > 0)
    hot = ((np.arange(REL)[:, None] == bucket(d, 2048.0)[None]) & ok[None]).astype(f)
    a["onehot0"] = hot
    a["toe_add0"] = np.broadcast_to(np.where(ok, np.log(np.maximum(count, 1)), NEG).astype(f), (A_H, TOE)).copy()
    a["onehot1"] = ((np.arange(REL)[:, None] == bucket(d, 128.0)[None]) & (d >= 0)[None]).astype(f)
    a["toe_add1"] = np.broadcast_to(np.where(d >= 0, 0.0, NEG).astype(f), (N_H, TOE)).copy()
    p = np.arange(P)
    a["cmask"] = np.concatenate([np.where(p[None, :] <= p[:, None], 0.0, NEG),
                                 np.where(tok[None, :] <= (P + p)[:, None], 0.0, NEG)], axis=1).astype(f)
    lm = np.zeros((P, 8, P), f)
    for l in range(7):
        s = 1 << l
        same = p[:, None] // (2 * s) == p[None, :] // (2 * s)
        lm[:, l, :] = same & (p[:, None] // s % 2 == 0) & (p[None, :] // s % 2 == 1)
    a["lmask"] = lm

    w = i["w_in_2"][0]
    o = np.cumsum([0, 1024, 256, 256, 256, 256, 256, 256, 24, 3072, 1024, 8, 8]).tolist()
    q, kc, vc, ks, vs, kw, vw, ng, qkv, z, ga, gb = o[:12]
    mg = o[12]
    weights("win2", cols(w, [(q, 1024), (kc, 256), (vc, 256), (ks, 256), (kw, 256), (vs, 256), (vw, 256)]))
    weights("win2g", cols(w, [(qkv, 3072)]))
    weights("z", cols(w, [(z, 1024)]))
    weights("merge", cols(w, [(mg, 2 * D)]))
    a["w_small2"] = cols(w, [(ng, 24), (ga, 8), (gb, 8)]).reshape(KD, P, 40).transpose(1, 0, 2).reshape(P, KD * 40).copy()
    weights("cmp_k", i["cmp_w1_k_2"][0])
    weights("cmp_v", i["cmp_w1_v_2"][0])
    weights("pa", i["w_pa_2"][0])
    weights("pb", i["w_pb_2"][0])
    weights("wo", i["w_o_2"][0])
    weights("up2_a", i["w_up_2"][0][:, 0:FF2 // 2])
    weights("up2_b", i["w_up_2"][0][:, FF2 // 2:])
    weights("down2_a", i["w_down_2"][0][0:FF2 // 2])
    weights("down2_b", i["w_down_2"][0][FF2 // 2:])
    a["pe_t"] = np.stack([i["cmp_pe_k_2"][0].T, i["cmp_pe_v_2"][0].T], axis=1).copy()
    a["w2c"] = np.stack([i[n][0].reshape(2, P, P).transpose(1, 0, 2) for n in ("cmp_w2_k_2", "cmp_w2_v_2")], axis=1).copy()
    a["conv2"] = np.stack([lanes(i["conv_w_2"][0][k]) for k in range(4)], axis=2).copy()
    a["a_log"] = i["a_log_2"]
    a["dt_bias"] = i["dt_bias_2"]
    a["gdn_norm"] = i["gdn_norm_w_2"]
    a["norm_final"] = i["norm_final"][None]
    a["ln_f"] = i["ln_f_w_2"][None]
    end = np.arange(N_CMP) * CSTR + CB - 1
    dc = tok[None, :] - end[:, None]
    a["onehot_c"] = ((np.arange(REL)[:, None, None] == bucket(dc, 128.0)[None]) & (dc >= 0)[None]).astype(f).reshape(
        REL, N_CMP * S)
    a["mask_c"] = rows(np.where(dc.T >= 0, 0.0, NEG).astype(f)).reshape(P, TT * N_CMP)
    a["cmt"] = np.stack([np.where(p[None, :] >= p[:, None], 0.0, NEG), np.where(p[None, :] < p[:, None], 0.0, NEG)],
                        axis=1).astype(f)
    return a


def kernel(**inputs):
    import concourse.bacc as bacc
    from concourse.bass_utils import run_bass_kernel_spmd

    arrays = {k: np.ascontiguousarray(v) for k, v in layout({k: np.asarray(v) for k, v in inputs.items()}).items()}
    nc = bacc.Bacc("TRN2", target_bir_lowering=False, num_devices=1)
    t_in = {k: nc.dram_tensor("in_" + k, v.shape, F32, kind="ExternalInput").ap() for k, v in arrays.items()}
    out = nc.dram_tensor("result", (P, TT, D), F32, kind="ExternalOutput").ap()
    build(nc, t_in, out)
    r = run_bass_kernel_spmd(nc, [{"in_" + k: v for k, v in arrays.items()}], core_ids=[0])
    return r.results[0]["result"].transpose(1, 0, 2).reshape(1, S, D)
```
